# Optimizing a Trainium2 kernel written in Bass

```python
import jax
import jax.numpy as jnp
from jax import lax
import numpy as np

D_MODEL = 1024
BATCH = 1
SEQ = 512
DEPTH = 2
DEC_BATCH = 1
DEC_SEQ = 64
PAST_LEN = 512

CHUNK = 64
HEAD_DIM = 64
N_MIXERS = 4
D_MIX = D_MODEL
W_GROUP = D_MIX // N_MIXERS
H_A = W_GROUP // HEAD_DIM
H_B = W_GROUP // HEAD_DIM
H_C = W_GROUP // HEAD_DIM
H_D = W_GROUP // HEAD_DIM
LRU_BLOCK = W_GROUP // H_D
A_BAND_CHUNKS = 8
A_REACH = A_BAND_CHUNKS * CHUNK
REL_CLIP = 128
CONV_W = 4
LRU_C = 8.0
N_MEM = 256
H_X = 4
D_X = H_X * HEAD_DIM
D_FF = ((8 * D_MODEL // 3 + 127) // 128) * 128
ALPHA = (2.0 * DEPTH) ** 0.25
BETA = (8.0 * DEPTH) ** -0.25
LN_EPS = 1e-5
IN_WIDTHS = (W_GROUP,) * 13 + (H_C, H_C)
IN_COLS = sum(IN_WIDTHS)
IN_SPLITS = tuple(int(s) for s in np.cumsum(IN_WIDTHS)[:-1])

kernel_name = 'hybrid_streaming_encoder_step'

F32 = jnp.float32

def layer_norm(x, g, b):
    xf = x.astype(F32)
    mu = jnp.mean(xf, -1, keepdims=True)
    var = jnp.mean(jnp.square(xf - mu), -1, keepdims=True)
    return ((xf - mu) * lax.rsqrt(var + LN_EPS) * g.astype(F32) + b.astype(F32)).astype(x.dtype)

def head_norm(h):
    mu = jnp.mean(h, -1, keepdims=True)
    var = jnp.mean(jnp.square(h - mu), -1, keepdims=True)
    return (h - mu) * lax.rsqrt(var + LN_EPS)

def swiglu(x, w_gate, w_up, w_down):
    return (jax.nn.silu(x @ w_gate) * (x @ w_up)) @ w_down

def rotary(x, pos):
    half = HEAD_DIM // 2
    inv = jnp.exp(-jnp.log(10000.0) * jnp.arange(half, dtype=F32) / half)
    ang = pos.astype(F32)[:, None] * inv[None, :]
    cos = jnp.cos(ang)[None, :, None, :]
    sin = jnp.sin(ang)[None, :, None, :]
    x1, x2 = x[..., :half], x[..., half:]
    return jnp.concatenate([x1 * cos - x2 * sin, x1 * sin + x2 * cos], -1)

def chunk_scan(fn, carry, xs):
    T = xs[0].shape[1]
    L = min(CHUNK, T)
    nc = T // L
    blocks = tuple(jnp.moveaxis(a.reshape((a.shape[0], nc, L) + a.shape[2:]), 1, 0) for a in xs)
    carry, ys = lax.scan(fn, carry, blocks)
    ys = jnp.moveaxis(ys, 0, 1)
    return carry, ys.reshape((ys.shape[0], T) + ys.shape[3:])

def attend(q, k, v, rel, valid, rel_bias):
    s = jnp.einsum('...qhd,...khd->...hqk', q.astype(F32), k.astype(F32)) * HEAD_DIM ** -0.5
    s = s + rel_bias.astype(F32)[:, jnp.clip(rel, -REL_CLIP, REL_CLIP) + REL_CLIP]
    if valid is not None:
        s = jnp.where(valid, s, -jnp.inf)
    p = jax.nn.softmax(s, axis=-1)
    return jnp.einsum('...hqk,...khd->...qhd', p, v.astype(F32))

def band_attention_prompt(q, k, v, rel_bias):
    B, T, H, dh = q.shape
    nc = T // CHUNK
    band = (A_BAND_CHUNKS + 1) * CHUNK
    qc = q.reshape(B, nc, CHUNK, H, dh)
    pad = jnp.zeros((B, A_BAND_CHUNKS * CHUNK, H, dh), k.dtype)
    kp = jnp.concatenate([pad, k], 1).reshape(B, nc + A_BAND_CHUNKS, CHUNK, H, dh)
    vp = jnp.concatenate([pad, v], 1).reshape(B, nc + A_BAND_CHUNKS, CHUNK, H, dh)
    kb = jnp.concatenate([kp[:, o:o + nc] for o in range(A_BAND_CHUNKS + 1)], axis=2)
    vb = jnp.concatenate([vp[:, o:o + nc] for o in range(A_BAND_CHUNKS + 1)], axis=2)
    key_off = jnp.arange(band) - A_BAND_CHUNKS * CHUNK
    rel = jnp.arange(CHUNK)[:, None] - key_off[None, :]
    chunk_id = jnp.arange(nc)[:, None] + jnp.arange(band)[None, :] // CHUNK - A_BAND_CHUNKS
    valid = (chunk_id >= 0)[None, :, None, None, :]
    o = attend(qc, kb, vb, rel, valid, rel_bias)
    return o.reshape(B, T, H * dh)

def band_attention_step(q, k, v, k_cache, v_cache, rel_bias):
    B, S, H, dh = q.shape
    R = k_cache.shape[1]
    kk = jnp.concatenate([k_cache.astype(k.dtype), k], 1)
    vv = jnp.concatenate([v_cache.astype(v.dtype), v], 1)
    rel = jnp.arange(S)[:, None] + R - jnp.arange(R + S)[None, :]
    o = attend(q, kk, vv, rel, None, rel_bias)
    return o.reshape(B, S, H * dh)

def retention_chunk(S0, xs):
    q, k, v = xs
    L = q.shape[1]
    log_g = jnp.log1p(-jnp.exp2(-5.0 - jnp.arange(H_B, dtype=F32)))
    idx = jnp.arange(L, dtype=F32)
    diff = idx[:, None] - idx[None, :]
    decay = jnp.exp(jnp.where((diff >= 0)[None], diff[None] * log_g[:, None, None], -jnp.inf))
    scores = jnp.einsum('blhd,bmhd->bhlm', q, k) * decay
    o = jnp.einsum('bhlm,bmhe->blhe', scores, v)
    q_dec = jnp.exp((idx[:, None] + 1.0) * log_g[None, :])
    o = o + jnp.einsum('blhd,bhde->blhe', q, S0) * q_dec[None, :, :, None]
    k_dec = jnp.exp((L - 1.0 - idx)[:, None] * log_g[None, :])
    S = jnp.exp(L * log_g)[None, :, None, None] * S0 + jnp.einsum('blhd,blhe->bhde', k * k_dec[None, :, :, None], v)
    return S, o

def mlstm_chunk(carry, xs):
    C0, n0, m0 = carry
    q, k, v, ig, lf = xs
    L = q.shape[1]
    b = jnp.cumsum(lf, axis=1).transpose(0, 2, 1)
    it = ig.transpose(0, 2, 1)
    causal = jnp.tril(jnp.ones((L, L), bool))
    log_d = jnp.where(causal, b[..., :, None] - b[..., None, :] + it[..., None, :], -jnp.inf)
    log_w0 = b + m0[..., None]
    m = jnp.maximum(log_w0, jnp.max(log_d, -1))
    d = jnp.exp(log_d - m[..., None])
    w0 = jnp.exp(log_w0 - m)
    qk = jnp.einsum('blhd,bmhd->bhlm', q, k) * d
    num = jnp.einsum('bhlm,bmhe->blhe', qk, v) + jnp.einsum('blhd,bhde->blhe', q, C0) * w0.transpose(0, 2, 1)[..., None]
    den = jnp.sum(qk, -1) + w0 * jnp.einsum('blhd,bhd->bhl', q, n0)
    den = jnp.maximum(jnp.abs(den), jnp.exp(-m))
    h = num / den.transpose(0, 2, 1)[..., None]
    m_last = m[..., -1]
    w_state = jnp.exp(log_w0[..., -1] - m_last)
    w_rows = jnp.exp(log_d[..., -1, :] - m_last[..., None])
    C = w_state[..., None, None] * C0 + jnp.einsum('bhl,blhd,blhe->bhde', w_rows, k, v)
    n = w_state[..., None] * n0 + jnp.einsum('bhl,blhd->bhd', w_rows, k)
    return (C, n, m_last), h

def _lin_combine(left, right):
    return (left[0] * right[0], right[0] * left[1] + right[1])

def rg_lru_block(xd, yd, conv_buf, h0, conv_w, conv_b, wa, ba, wi, bi, lam):
    B, T, W = xd.shape
    xp = jnp.concatenate([conv_buf.astype(xd.dtype), xd], 1)
    xc = conv_b.astype(F32) + sum(xp[:, j:j + T].astype(F32) * conv_w[j].astype(F32) for j in range(CONV_W))
    new_buf = xp[:, T:]
    xb = xc.reshape(B, T, H_D, LRU_BLOCK)
    r = jax.nn.sigmoid(jnp.einsum('bthc,hcd->bthd', xb, wa.astype(F32)).reshape(B, T, W) + ba.astype(F32))
    i = jax.nn.sigmoid(jnp.einsum('bthc,hcd->bthd', xb, wi.astype(F32)).reshape(B, T, W) + bi.astype(F32))
    log_a = -LRU_C * r * jax.nn.softplus(-lam.astype(F32))
    a = jnp.exp(log_a)
    u = jnp.sqrt(-jnp.expm1(2.0 * log_a)) * (i * xc)
    u = u.at[:, 0].add(a[:, 0] * h0)
    _, h = lax.associative_scan(_lin_combine, (a, u), axis=1)
    y = h * jax.nn.gelu(yd.astype(F32))
    return y, h[:, -1], new_buf

def parallel_mixer(x, pos, a_past, ret_s, ml_c, ml_n, ml_m, lru_h, conv_buf, lw):
    B, T, _ = x.shape
    proj = x @ lw['w_in'] + lw['b_in']
    (qa, ka, va, qb, kb, vb, gb, qc, kc, vc, oc, xd, yd, ic, fc) = jnp.split(proj, IN_SPLITS, axis=-1)
    heads = lambda t: t.reshape(B, T, -1, HEAD_DIM)
    qa, ka, va = heads(qa), heads(ka), heads(va)
    if a_past is None:
        ya = band_attention_prompt(qa, ka, va, lw['a_rel_bias'])
        keep = min(A_REACH, T)
        a_k, a_v = ka[:, T - keep:], va[:, T - keep:]
    else:
        ya = band_attention_step(qa, ka, va, a_past[0], a_past[1], lw['a_rel_bias'])
        a_k, a_v = ka, va
    qb_ = rotary(heads(qb).astype(F32), pos)
    kb_ = rotary(heads(kb).astype(F32), pos) * HEAD_DIM ** -0.5
    ret_new, ob = chunk_scan(retention_chunk, ret_s.astype(F32), (qb_, kb_, heads(vb).astype(F32)))
    yb = head_norm(ob).reshape(B, T, W_GROUP) * jax.nn.silu(gb.astype(F32))
    carry = (ml_c.astype(F32), ml_n.astype(F32), ml_m.astype(F32))
    (c_new, n_new, m_new), hc = chunk_scan(
        mlstm_chunk, carry,
        (heads(qc).astype(F32), heads(kc).astype(F32) * HEAD_DIM ** -0.5, heads(vc).astype(F32),
         ic.astype(F32), jax.nn.log_sigmoid(fc.astype(F32))))
    yc = head_norm(hc).reshape(B, T, W_GROUP) * jax.nn.sigmoid(oc.astype(F32))
    yd_, h_new, conv_new = rg_lru_block(xd, yd, conv_buf, lru_h.astype(F32), lw['conv_w'], lw['conv_b'],
                                        lw['lru_wa'], lw['lru_ba'], lw['lru_wi'], lw['lru_bi'], lw['lru_lambda'])
    y = jnp.concatenate([ya, yb, yc, yd_], -1).astype(x.dtype) @ lw['w_out']
    return y, (a_k, a_v, ret_new, c_new, n_new, m_new, h_new, conv_new)

def cross_attention(x, mem_k, mem_v, w_q, w_o):
    B, T, _ = x.shape
    q = (x @ w_q).reshape(B, T, H_X, HEAD_DIM).astype(F32)
    s = jnp.einsum('bthd,bmhd->bhtm', q, mem_k.astype(F32)) * HEAD_DIM ** -0.5
    p = jax.nn.softmax(s, axis=-1)
    o = jnp.einsum('bhtm,bmhd->bthd', p, mem_v.astype(F32)).reshape(B, T, D_X)
    return o.astype(x.dtype) @ w_o

def encoder_layer(x, pos, mem_k, mem_v, a_past, rec, lw):
    g, b = lw['ln_g'], lw['ln_b']
    x = layer_norm(ALPHA * x + 0.5 * swiglu(x, lw['ffn1_gate'], lw['ffn1_up'], lw['ffn1_down']), g[0], b[0])
    mix, state = parallel_mixer(x, pos, a_past, rec[0], rec[1], rec[2], rec[3], rec[4], rec[5], lw)
    x = layer_norm(ALPHA * x + mix, g[1], b[1])
    x = layer_norm(ALPHA * x + cross_attention(x, mem_k, mem_v, lw['x_wq'], lw['x_wo']), g[2], b[2])
    x = layer_norm(ALPHA * x + 0.5 * swiglu(x, lw['ffn2_gate'], lw['ffn2_up'], lw['ffn2_down']), g[3], b[3])
    return x, state

def setup_inputs(seed: int = 0) -> dict:
    key = jax.random.key(seed)
    ks = iter(jax.random.split(key, 48))
    nrm = lambda shape, scale=1.0: scale * jax.random.normal(next(ks), shape, F32)
    a_rows = min(A_REACH, PAST_LEN)
    x_prompt = nrm((BATCH, SEQ, D_MODEL))
    x_sample = nrm((DEC_BATCH, DEC_SEQ, D_MODEL))
    mem_prompt = nrm((BATCH, N_MEM, D_MODEL))
    cache_a_k = nrm((DEPTH, DEC_BATCH, a_rows, H_A, HEAD_DIM))
    cache_a_v = nrm((DEPTH, DEC_BATCH, a_rows, H_A, HEAD_DIM))
    state_ret = nrm((DEPTH, DEC_BATCH, H_B, HEAD_DIM, HEAD_DIM), 0.5)
    state_mlstm_c = nrm((DEPTH, DEC_BATCH, H_C, HEAD_DIM, HEAD_DIM), 0.5)
    state_mlstm_n = nrm((DEPTH, DEC_BATCH, H_C, HEAD_DIM), 0.5)
    state_mlstm_m = nrm((DEPTH, DEC_BATCH, H_C))
    state_lru_h = nrm((DEPTH, DEC_BATCH, W_GROUP), 0.5)
    state_conv = nrm((DEPTH, DEC_BATCH, CONV_W - 1, W_GROUP))
    cache_mem_k = nrm((DEPTH, DEC_BATCH, N_MEM, H_X, HEAD_DIM))
    cache_mem_v = nrm((DEPTH, DEC_BATCH, N_MEM, H_X, HEAD_DIM))
    ln_g = 1.0 + nrm((DEPTH, 4, D_MODEL), 0.02)
    ln_b = nrm((DEPTH, 4, D_MODEL), 0.02)
    ffn1_gate = nrm((DEPTH, D_MODEL, D_FF), D_MODEL ** -0.5)
    ffn1_up = nrm((DEPTH, D_MODEL, D_FF), D_MODEL ** -0.5)
    ffn1_down = nrm((DEPTH, D_FF, D_MODEL), BETA * D_FF ** -0.5)
    ffn2_gate = nrm((DEPTH, D_MODEL, D_FF), D_MODEL ** -0.5)
    ffn2_up = nrm((DEPTH, D_MODEL, D_FF), D_MODEL ** -0.5)
    ffn2_down = nrm((DEPTH, D_FF, D_MODEL), BETA * D_FF ** -0.5)
    w_in = nrm((DEPTH, D_MODEL, IN_COLS), D_MODEL ** -0.5)
    forget_bias = jnp.linspace(3.0, 6.0, H_C, dtype=F32)
    b_in = nrm((DEPTH, IN_COLS), 0.02).at[:, IN_COLS - H_C:].add(forget_bias)
    a_rel_bias = nrm((DEPTH, H_A, 2 * REL_CLIP + 1), 0.1)
    conv_w = nrm((DEPTH, CONV_W, W_GROUP), CONV_W ** -0.5)
    conv_b = nrm((DEPTH, W_GROUP), 0.02)
    lru_wa = nrm((DEPTH, H_D, LRU_BLOCK, LRU_BLOCK), LRU_BLOCK ** -0.5)
    lru_ba = nrm((DEPTH, W_GROUP), 0.02)
    lru_wi = nrm((DEPTH, H_D, LRU_BLOCK, LRU_BLOCK), LRU_BLOCK ** -0.5)
    lru_bi = nrm((DEPTH, W_GROUP), 0.02)
    a0 = jax.random.uniform(next(ks), (DEPTH, W_GROUP), F32, 0.9, 0.999)
    s0 = a0 ** (1.0 / LRU_C)
    lru_lambda = jnp.log(s0) - jnp.log1p(-s0)
    w_out = nrm((DEPTH, D_MIX, D_MODEL), BETA * D_MIX ** -0.5)
    x_wq = nrm((DEPTH, D_MODEL, D_X), D_MODEL ** -0.5)
    x_wk = nrm((DEPTH, D_MODEL, D_X), D_MODEL ** -0.5)
    x_wv = nrm((DEPTH, D_MODEL, D_X), D_MODEL ** -0.5)
    x_wo = nrm((DEPTH, D_X, D_MODEL), BETA * D_X ** -0.5)
    return {'x_prompt': x_prompt, 'x_sample': x_sample, 'mem_prompt': mem_prompt,
            'cache_a_k': cache_a_k, 'cache_a_v': cache_a_v, 'state_ret': state_ret,
            'state_mlstm_c': state_mlstm_c, 'state_mlstm_n': state_mlstm_n, 'state_mlstm_m': state_mlstm_m,
            'state_lru_h': state_lru_h, 'state_conv': state_conv,
            'cache_mem_k': cache_mem_k, 'cache_mem_v': cache_mem_v,
            'ln_g': ln_g, 'ln_b': ln_b,
            'ffn1_gate': ffn1_gate, 'ffn1_up': ffn1_up, 'ffn1_down': ffn1_down,
            'ffn2_gate': ffn2_gate, 'ffn2_up': ffn2_up, 'ffn2_down': ffn2_down,
            'w_in': w_in, 'b_in': b_in, 'a_rel_bias': a_rel_bias,
            'conv_w': conv_w, 'conv_b': conv_b,
            'lru_wa': lru_wa, 'lru_ba': lru_ba, 'lru_wi': lru_wi, 'lru_bi': lru_bi, 'lru_lambda': lru_lambda,
            'w_out': w_out, 'x_wq': x_wq, 'x_wk': x_wk, 'x_wv': x_wv, 'x_wo': x_wo}

def reference(x_prompt, x_sample, mem_prompt, cache_a_k, cache_a_v, state_ret, state_mlstm_c, state_mlstm_n,
              state_mlstm_m, state_lru_h, state_conv, cache_mem_k, cache_mem_v, ln_g, ln_b,
              ffn1_gate, ffn1_up, ffn1_down, ffn2_gate, ffn2_up, ffn2_down, w_in, b_in, a_rel_bias,
              conv_w, conv_b, lru_wa, lru_ba, lru_wi, lru_bi, lru_lambda, w_out, x_wq, x_wk, x_wv, x_wo):
    def layer_weights(l):
        return {'ln_g': ln_g[l], 'ln_b': ln_b[l],
                'ffn1_gate': ffn1_gate[l], 'ffn1_up': ffn1_up[l], 'ffn1_down': ffn1_down[l],
                'ffn2_gate': ffn2_gate[l], 'ffn2_up': ffn2_up[l], 'ffn2_down': ffn2_down[l],
                'w_in': w_in[l], 'b_in': b_in[l], 'a_rel_bias': a_rel_bias[l],
                'conv_w': conv_w[l], 'conv_b': conv_b[l],
                'lru_wa': lru_wa[l], 'lru_ba': lru_ba[l], 'lru_wi': lru_wi[l], 'lru_bi': lru_bi[l],
                'lru_lambda': lru_lambda[l], 'w_out': w_out[l], 'x_wq': x_wq[l], 'x_wo': x_wo[l]}

    bp, tp, _ = x_prompt.shape
    pos_p = jnp.arange(tp)
    h = x_prompt
    prompt_states = []
    for l in range(DEPTH):
        lw = layer_weights(l)
        mk = (mem_prompt @ x_wk[l]).reshape(bp, N_MEM, H_X, HEAD_DIM)
        mv = (mem_prompt @ x_wv[l]).reshape(bp, N_MEM, H_X, HEAD_DIM)
        rec0 = (jnp.zeros((bp, H_B, HEAD_DIM, HEAD_DIM), F32),
                jnp.zeros((bp, H_C, HEAD_DIM, HEAD_DIM), F32),
                jnp.zeros((bp, H_C, HEAD_DIM), F32),
                jnp.zeros((bp, H_C), F32),
                jnp.zeros((bp, W_GROUP), F32),
                jnp.zeros((bp, CONV_W - 1, W_GROUP), x_prompt.dtype))
        h, st = encoder_layer(h, pos_p, mk, mv, None, rec0, lw)
        prompt_states.append(st + (mk, mv))
    y_prompt = h
    (p_a_k, p_a_v, p_ret, p_mc, p_mn, p_mm, p_lru, p_conv, p_mem_k, p_mem_v) = [
        jnp.stack(f) for f in zip(*prompt_states)]

    ts = x_sample.shape[1]
    pos_s = PAST_LEN + jnp.arange(ts)
    h = x_sample
    sample_states = []
    for l in range(DEPTH):
        lw = layer_weights(l)
        rec = (state_ret[l], state_mlstm_c[l], state_mlstm_n[l], state_mlstm_m[l], state_lru_h[l], state_conv[l])
        h, st = encoder_layer(h, pos_s, cache_mem_k[l], cache_mem_v[l], (cache_a_k[l], cache_a_v[l]), rec, lw)
        sample_states.append(st)
    y_sample = h
    (s_a_k, s_a_v, s_ret, s_mc, s_mn, s_mm, s_lru, s_conv) = [jnp.stack(f) for f in zip(*sample_states)]

    return (y_prompt, y_sample,
            p_a_k, p_a_v, p_ret, p_mc, p_mn, p_mm, p_lru, p_conv, p_mem_k, p_mem_v,
            s_a_k, s_a_v, s_ret, s_mc, s_mn, s_mm, s_lru, s_conv)


_drawn_inputs = setup_inputs


def setup_inputs(seed=0):
    import zlib

    import numpy as np

    out = dict(_drawn_inputs(seed))
    spreads = {}
    factors = {'cache_a_k': 4.42, 'a_rel_bias': 8.0, 'lru_ba': 8.0, 'lru_bi': 8.0}
    for name, (base, spread) in spreads.items():
        noise = np.random.default_rng([zlib.crc32(name.encode()), seed]).standard_normal(out[name].shape)
        drawn = base * np.exp(spread * noise) if base else spread * noise
        out[name] = jnp.asarray(drawn.astype(out[name].dtype))
    for name, factor in factors.items():
        out[name] = (out[name] * factor).astype(out[name].dtype)
    return out
```

```python
from contextlib import ExitStack

import numpy as np
import concourse.bass as bass
from concourse import mybir

F32 = mybir.dt.float32
F32R = mybir.dt.float32r
ALU = mybir.AluOpType
ACT = mybir.ActivationFunctionType
AX = mybir.AxisListType

P = 128
DM = 1024
DEPTH = 2
TP = 512
TS = 64
TOK = TP + TS
HT = TOK // 2
CH = 128
NCH = TP // CH
KT = DM // P
DFF = 2816
FT = DFF // P
WG = 256
NMEM = 256
HD = 64
NH = 4
BAND = 384
ALPHA = (2.0 * DEPTH) ** 0.25
EPS = 1e-5
RING = 3
XPW = 3 + TP + 3 + TS
XCW = TP + 3 + TS

PROJ_D = [("xd", 0), ("xd", 1), ("yd", 0), ("yd", 1)]
PROJ_C = [("qc", 0), ("qc", 1), ("kc", 0), ("kc", 1), ("vc", 0), ("vc", 1), ("oc", 0), ("oc", 1)]
PROJ_A = [("qa", 0), ("qa", 1), ("ka", 0), ("ka", 1), ("va", 0), ("va", 1)]
PROJ_B = [("qb", 0), ("qb", 1), ("kb", 0), ("kb", 1), ("vb", 0), ("vb", 1), ("gb", 0), ("gb", 1)]
IN_ORDER = ["qa", "ka", "va", "qb", "kb", "vb", "gb", "qc", "kc", "vc", "oc", "xd", "yd"]
PROJ_ALL = PROJ_D + PROJ_C + PROJ_A + PROJ_B
BIAS_COL = {x: 64 + i for i, x in enumerate(PROJ_ALL)}
C_CONVW, C_CONVB, C_BA, C_BI, C_LAM, C_H0, C_CBUF = 90, 98, 100, 102, 104, 106, 108
C_GI, C_GF, C_M0 = 114, 115, 116
C_SC, C_SN, C_SR = 117, 117 + 128, 117 + 130
NPRM = C_SR + 128

FFN_UNITS = 3 * FT
MIX_UNITS = len(PROJ_ALL) + 8
X_UNITS = 8
UNITS = 2 * FFN_UNITS + MIX_UNITS + X_UNITS
FFN2_AT = FFN_UNITS + MIX_UNITS + X_UNITS
assert UNITS % 6 == 0 and FFN_UNITS % 6 == 0 and (MIX_UNITS + X_UNITS) % 6 == 0

CONST_COLS = [("ident", P), ("ones", P), ("avg", P), ("blk", P), ("perm", P), ("mask", P), ("cos", TOK), ("sin", TOK),
              ("dec", NH * P), ("qdec", 2 * P), ("kdec", 5 * NH), ("gl", 4), ("selh", NH * P), ("selp", 2 * P)]
A_STEPS = [(p, *x) for p in range(2) for x in [("t", t) for t in range(4)] + [("s", 0), ("s", 1)]]
X_STEPS = [(p, t) for p in range(2) for t in range(NCH + 1)]

COUNTS = {
    "pairA_full": 64, "pairA_free": 64, "pairB_full": 60, "pairB_free": 60, "pairD0_full": 160,
    "pairD0_free": 160, "pairD1_full": 158, "pairD1_free": 158, "x_hi_done": 32, "x_ready": 32,
    "h_hi_done": 54, "h_ready": 54, "sq_done": 32, "s2_added": 28, "mean_sq": 4, "var_done": 4,
    "rstd_done": 4, "ln_scaled": 32, "dve_step": 281, "act_step": 102, "stats_ready": 4, "gw_split": 1,
    "conv": 2, "rows": 1, "rowexp": 2, "c.states": 2, "c.sq": 2, "a.probs": 12, "a.pv": 10, "b.turned": 4,
    "b.states": 2, "b.sq": 2, "mem_split": 1, "x.probs": 10, "x.pv": 8, "xp_free": 1, "lam_ln": 1, "lam4": 1,
    "d.tanh": 2, "d.sqrt": 2, "d.out": 2, "rows_in": 1, "lf_ln": 1, "c.dT": 4, "c.rstd": 2, "c.out": 2,
    "a.nmax": 12, "a.exp": 12, "b.rstd": 2, "b.out": 2, "mem_hi": 1, "x.nmax": 10, "init": 0, "ysc": 20,
}


class Count:

    def __init__(self, sem, name, counts, pre=0):
        self.sem, self.name, self.pre = sem, name, pre
        self.per = counts.get(name, 1)
        self.n = 0

    def value(self, l, k):
        return l * self.per + (self.pre + k)


def build_program(nc, io, counts):
    made = {}
    with ExitStack() as ctx:
        sem_list = []

        def sem(name):
            return ctx.enter_context(nc.semaphore(name))

        def counted(name, pre=0):
            c = Count(sem(name), name, counts, pre)
            sem_list.append(c)
            return c

        def sb(name, shape, dt=F32, scope=None):
            return (scope or ctx).enter_context(nc.sbuf_tensor(name, shape, dt))

        x_hi = sb("x_hi", [P, KT, TOK], F32R)
        x_lo = sb("x_lo", [P, KT, TOK], F32R)
        y = sb("y", [P, KT, TOK])
        h_hi = sb("h_hi", [P, 2, TOK], F32R)
        h_lo = sb("h_lo", [P, 2, TOK], F32R)
        w_raw = sb("w_raw", [P, RING, 8, P])
        w_hi = sb("w_hi", [P, RING, 8, P], F32R)
        w_lo = sb("w_lo", [P, RING, 8, P], F32R)
        T = [sb(f"scratch{i}", [P, XPW]) for i in range(6)]
        sil = [T[0], T[1]]
        hf = T[2]
        s1, s2, rs = T[3], T[4], T[5]
        prm = sb("prm", [P, NPRM])
        cst = sb("cst", [P, io["consts"].shape[1]])
        gw_raw = sb("gw_raw", [P, KT, 36])
        gw_hi = sb("gw_hi", [P, KT, 36], F32R)
        gw_lo = sb("gw_lo", [P, KT, 36], F32R)
        lru_w = sb("lru_w", [P, 4, P])
        small = sb("small", [P, 64])
        n4 = sb("n4", [P, 2, 2, TS])
        aT = sb("aT", [P, 20])
        wr = sb("wr", [P, 5, NH])
        wst = sb("wst", [P, 2, 5])
        st_out = sb("st_out", [P, 2, 2, HD])
        cn_out = sb("cn_out", [P, 2, 2, HD + 1])
        ld_out = sb("ld_out", [P, 2, 8])
        m_out = sb("m_out", [NH, 2])
        ysc, eps = small[:, 0:1], small[:, 1:2]
        far = small[:, 4:8]
        mx, nmx, sm, rc = small[:, 8:12], small[:, 12:16], small[:, 16:20], small[:, 20:24]
        lam4 = small[:, 24:26]
        lamt = small[:, 26:30]

        with ExitStack() as s:
            pc = sb("pc", [P, 8, TOK], scope=s)
            pa = sb("pa", [P, 6, TOK], scope=s)
        with ExitStack() as s:
            mem_raw = sb("mem_raw", [P, KT, NMEM], scope=s)
            mem_hi = sb("mem_hi", [P, KT, NMEM], F32R, scope=s)
            mem_lo = sb("mem_lo", [P, KT, NMEM], F32R, scope=s)
            mkT = sb("mkT", [P, 2, NMEM], scope=s)
            mv = sb("mv", [P, 2, NMEM], scope=s)
        pad = sb("pad_pj", [P, 14 * TOK])
        with ExitStack() as s:
            pt = sb("pt", [P, 2, 2, TP], scope=s)
        xp = sb("xp", [P, 2, XPW])
        yd = sb("yd", [P, 2, TOK])
        with ExitStack() as s:
            vt = sb("vt", [P, 5, WG], scope=s)
            kw = sb("kw", [P, 5, WG], scope=s)
            dT = sb("dT", [P, NH, TOK], scope=s)
            cs = sb("cs", [P, 2, 6, P], scope=s)
            qw = sb("qw", [P, 2, TOK], scope=s)
        with ExitStack() as s:
            vta = sb("vta", [P, 5, WG], scope=s)
            tb = sb("tb", [P, NH, 256], scope=s)
            kc = sb("kc", [P, 2, TP], scope=s)
            vc = sb("vc", [P, 4, WG], scope=s)
            pr = sb("pr", [P, 2, 2, TOK], scope=s)
        with ExitStack() as s:
            qx = sb("qx", [P, 2, TOK], scope=s)
            prx = sb("prx", [P, 2, 2, NMEM], scope=s)
            ptx = sb("ptx", [P, 2, 2, NMEM], scope=s)
            kms = sb("kms", [P, 2, NMEM], scope=s)
            vms = sb("vms", [P, 2, NMEM], scope=s)
        pad2 = sb("pad_s", [P, 7552])

        co = {}
        at = 0
        for name, width in CONST_COLS:
            co[name] = cst[:, at:at + width]
            at += width
        ident, ones, avg, blk, perm, mask = (co[n] for n in ("ident", "ones", "avg", "blk", "perm", "mask"))
        cosT, sinT = co["cos"], co["sin"]
        dec = co["dec"].rearrange("p (h m) -> p h m", h=NH)
        qdec = co["qdec"].rearrange("p (a m) -> p a m", a=2)
        kdec = co["kdec"].rearrange("p (t h) -> p t h", t=5)
        gl = co["gl"].rearrange("p (a s) -> p a s", a=2)
        selh = co["selh"].rearrange("p (h m) -> p h m", h=NH)
        selp = co["selp"].rearrange("p (a m) -> p a m", a=2)

        class Pair:
            def __init__(self, name):
                self.name = name
                self.t = ctx.enter_context(nc.psum_tensor(name, [P, 2, 512], F32))
                self.full = counted(name + "_full")
                self.free = counted(name + "_free", 1)
                self.n = 0

            def halves(self):
                return self.t[:, :, 0:HT]

        A, B, D0, D1 = (Pair(n) for n in ("pairA", "pairB", "pairD0", "pairD1"))
        DD = [D0, D1]
        uses = {}

        landed = [sem(f"unit_landed{i}") for i in range(RING)]
        unit_split = sem("unit_split")
        unit_hi = sem("unit_hi")
        unit_begun = sem("unit_begun")
        x_hi_done = counted("x_hi_done", KT)
        x_ready = counted("x_ready", KT)
        h_hi_done = counted("h_hi_done")
        h_ready = counted("h_ready")
        sq_done = counted("sq_done")
        s2_added = counted("s2_added")
        mean_sq = counted("mean_sq")
        var_done = counted("var_done")
        rstd_done = counted("rstd_done")
        ln_scaled = counted("ln_scaled")
        dve_step = counted("dve_step")
        act_step = counted("act_step")
        stats_ready = counted("stats_ready")
        ev = {}

        def E(name):
            if name not in ev:
                ev[name] = counted(name)
            return ev[name]

        paced = {n: sem("paced_" + n) for n in ("pe", "act", "dve", "pool")}

        def hold(eng, name):
            eng.sem_inc(paced[name], 1)

        ld = {n: sem("ld_" + n) for n in ("const", "x", "prm", "gw", "lru", "attn", "mem", "memc", "band")}
        stored = {n: sem("st_" + n) for n in ("m", "ak", "ret", "mls", "lru", "mk", "mvv", "y")}

        tb_dram = nc.dram_tensor("tb_dram", (DEPTH, NH, P * BAND), F32, kind="Internal").ap()
        block = ctx.enter_context(nc.Block())

        def inc(ins, c):
            c.n += 1
            ins.then_inc(c.sem, 1)

        @block.tensor
        def _(pe):
            mm = nc.tensor.matmul
            for pair in (A, B, D0, D1):
                pe.sem_inc(pair.free.sem, 1)
            pe.wait_ge(ld["const"], 16)

            with pe.Fori(0, DEPTH) as l:
                def take(pair, label, at=0, index=None):
                    n = pair.n if index is None else index
                    pe.wait_ge(pair.free.sem, pair.free.value(l, n) + at)
                    if index is None:
                        uses[label] = (pair, n)
                        pair.n += 1
                    return pair.t

                def fill(ins, pair):
                    ins.then_inc(pair.full.sem, 1)

                def read_done(label):
                    pair, n = uses[label]
                    pe.wait_ge(pair.free.sem, pair.free.value(l, n + 1))

                def await_ev(name, k=1):
                    pe.wait_ge(E(name).sem, E(name).value(l, k))

                def unit_there(u, off=0):
                    pe.wait_ge(unit_split, l * UNITS + (u + 1) + off)

                def passes(out, s, b, hi, lo, start, stop, m=P, widths=(HT, HT), w=None):
                    wh, wl = w or (w_hi[:, s, b, 0:m], w_lo[:, s, b, 0:m])
                    ins = []
                    for i, (wt, mv_) in enumerate(((wh, hi), (wh, lo), (wl, hi))):
                        c = 0
                        for half, n in enumerate(widths):
                            ins.append(mm(out[0:m, half, 0:n], wt, mv_[:, c:c + n],
                                          start=(start and i == 0), stop=(stop and i == 2)))
                            c += n
                    return ins

                def proj(u, pair, label, off=0, use_off=0, index=None):
                    s = u % RING
                    unit_there(u, off)
                    out = take(pair, label, use_off, index)
                    for k in range(KT):
                        ins = passes(out, s, k, x_hi[:, k], x_lo[:, k], k == 0, k == KT - 1)
                        if k == 0:
                            ins[0].then_inc(unit_begun, 1)
                    ins[-1].then_inc(pair.full.sem, 1)

                def proj_two(u, x_stage, la, lb):
                    unit_there(u)
                    unit_there(u + 1)
                    oa, ob = take(A, la), take(B, lb)
                    for k in range(KT):
                        pe.wait_ge(x_ready.sem, l * x_ready.per + KT * x_stage + k + 1)
                        ia = passes(oa, u % RING, k, x_hi[:, k], x_lo[:, k], k == 0, k == KT - 1)
                        ib = passes(ob, (u + 1) % RING, k, x_hi[:, k], x_lo[:, k], k == 0, k == KT - 1)
                        if k == 0:
                            ia[0].then_inc(unit_begun, 1)
                        if k == KT - 1:
                            ib[0].then_inc(unit_begun, 1)
                            fill(ia[-1], A)
                            fill(ib[-1], B)

                def down(u, m, label=None, off=0, h_off=0, use_off=0, index=None):
                    pe.wait_ge(h_ready.sem, l * h_ready.per + 2 * (m + 1) + h_off)
                    for n in range(KT):
                        v = u + n // 4
                        if n % 4 == 0:
                            unit_there(v, off)
                        pair = DD[n % 2]
                        idx = None if index is None else index[n % 2] + n // 2
                        out = take(pair, (label, n), use_off, idx)
                        for kk in range(2):
                            ins = passes(out, v % RING, 2 * (n % 4) + kk, h_hi[:, kk], h_lo[:, kk],
                                         kk == 0, kk == 1)
                            if kk == 0 and n % 4 == 0:
                                ins[0].then_inc(unit_begun, 1)
                        ins[-1].then_inc(pair.full.sem, 1)

                def ffn(f, u0, x_stage, m0):
                    uses[("ffn", f, "A")], uses[("ffn", f, "B")] = A.n, B.n
                    proj_two(u0, x_stage, ("g", f, 0), ("u", f, 0))
                    proj(u0 + 2, A, ("g", f, 1))
                    proj(u0 + 3, B, ("u", f, 1))
                    a0, b0, d0, d1 = A.n, B.n, D0.n, D1.n
                    uses[("ffn", f, "D0")], uses[("ffn", f, "D1")] = d0, d1
                    with pe.Fori(0, FT // 2 - 1) as i:
                        u, o = u0 + 4, 6 * i
                        proj(u, A, None, o, 2 * i, a0)
                        proj(u + 1, B, None, o, 2 * i, b0)
                        down(u + 2, m0, None, o, 2 * i, 4 * i, (d0, d1))
                        proj(u + 4, A, None, o, 2 * i, a0 + 1)
                        proj(u + 5, B, None, o, 2 * i, b0 + 1)
                    n = FT // 2 - 1
                    for pair, k in ((A, 2), (B, 2), (D0, 4), (D1, 4)):
                        pair.n += k * n
                    down(u0 + FFN_UNITS - 2, m0 + n, ("ffn", f))

                def stats(j):
                    pe.wait_ge(stats_ready.sem, stats_ready.value(l, j + 1))
                    for pair, src, nm in ((D0, s1, "mean"), (D1, s2, "sq")):
                        out = take(pair, (nm, j))
                        for h in range(2):
                            i = mm(out[:, h, 0:HT], avg, src[:, h * HT:h * HT + HT], start=True, stop=True)
                        fill(i, pair)

                def wide(pair, label, lhsT, rhs, m=P):
                    out = take(pair, label)
                    mm(out[0:m, 0, 0:TP], lhsT, rhs[:, 0:TP], start=True, stop=True)
                    fill(mm(out[0:m, 1, 0:TS], lhsT, rhs[:, TP:TOK], start=True, stop=True), pair)

                def flat(pair, label, lhsT, rhs, w0=HT, w1=HT):
                    out = take(pair, label)
                    mm(out[:, 0, 0:w0], lhsT, rhs[:, 0:w0], start=True, stop=True)
                    fill(mm(out[:, 1, 0:w1], lhsT, rhs[:, w0:w0 + w1], start=True, stop=True), pair)

                def turn(pair, label, src):
                    out = take(pair, label)
                    for t in range(NCH):
                        nc.tensor.transpose(out[:, 0, t * P:t * P + P], src[:, t * P:t * P + P], ident)
                    fill(nc.tensor.transpose(out[0:TS, 1, 0:P], src[:, TP:TOK], ident), pair)

                def state_sums(pair, label, width):
                    g, p = label[0], label[2]
                    out = take(pair, label)
                    for t in range(NCH + 1):
                        rows = P if t < NCH else TS
                        bank, c = (0, t * width) if t < NCH else (1, 0)
                        for e in range(2):
                            h = 2 * p + e
                            k_ = kw[0:rows, t, h * HD:h * HD + HD]
                            i = mm(out[e * HD:e * HD + HD, bank, c:c + HD], k_,
                                   vt[0:rows, t, h * HD:h * HD + HD], start=True, stop=True)
                            if width == P:
                                i = mm(out[e * HD:e * HD + HD, bank, c + HD:c + P], k_,
                                       ones[0:rows, 0:HD], start=True, stop=True)
                    fill(i, pair)

                def scores(pair, label):
                    p = label[2]
                    out = take(pair, label)
                    for e in range(2):
                        r = slice(e * HD, e * HD + HD)
                        for t in range(NCH):
                            c = slice(t * P, t * P + P)
                            i = mm(out[:, e, c], pc[r, 2 + p, c], pc[r, p, c], start=True, stop=True)
                    fill(i, pair)

                def scores_sample(pair, label):
                    out = take(pair, label)
                    hold(pe, "pe")
                    for e in range(2):
                        r = slice(e * HD, e * HD + HD)
                        for p in range(2):
                            i = mm(out[0:TS, e, p * TS:p * TS + TS], pc[r, 2 + p, TP:TOK], pc[r, p, TP:TOK],
                                   start=True, stop=True)
                    fill(i, pair)

                def out_tile(o, p, e, t, cols, den):
                    h = 2 * p + e
                    r = slice(e * HD, e * HD + HD)
                    tok = slice(t * P, t * P + P) if t < NCH else slice(TP, TOK)
                    st = t if t < NCH else 0
                    lhs = ones[:, 0:HD] if den else vt[:, t, h * HD:h * HD + HD]
                    i = mm(o[r, cols], lhs, dT[:, h, tok], start=True, stop=(t == 0))
                    if t:
                        i = mm(o[r, cols], cs[r, p, st, HD:P] if den else cs[r, p, st, 0:HD], qw[r, p, tok],
                               start=False, stop=True)
                    return i

                ffn(0, 0, 0, 0)
                m_down = FT // 2
                stats(0)

                u = FFN_UNITS
                proj_two(u, 1, ("pj", "xd", 0), ("pj", "xd", 1))
                proj(u + 2, A, ("pj", "yd", 0))
                proj(u + 3, B, ("pj", "yd", 1))
                u += 4
                await_ev("gw_split")
                out = take(A, "gates")
                for k in range(KT):
                    ins = passes(out, 0, 0, x_hi[:, k], x_lo[:, k], k == 0, k == KT - 1, m=36,
                                 w=(gw_hi[:, k], gw_lo[:, k]))
                fill(ins[-1], A)

                def lru_gates(j):
                    await_ev("conv", j + 1)
                    flat(D0, ("d.r", j), lru_w[:, j], T[0], 290, XCW - 290)
                    flat(D1, ("d.i", j), lru_w[:, 2 + j], T[0], 290, XCW - 290)

                def proj_list(names, first_pair):
                    nonlocal u
                    for n, (g, j) in enumerate(names):
                        pair = (A, B)[(n + first_pair) % 2]
                        proj(u, pair, ("pj", g, j))
                        u += 1

                pe.wait_ge(ld["lru"], 16 * l + 16)
                proj_list(PROJ_C[0:2], 1)
                lru_gates(0)
                proj_list(PROJ_C[2:5], 1)
                lru_gates(1)
                proj_list(PROJ_C[5:8], 0)

                down(u, m_down, ("mix", 0))
                u += 2
                m_down += 1

                await_ev("rows")
                out = take(D0, "c.aT")
                hold(pe, "pe")
                for t in range(NCH):
                    nc.tensor.transpose(out[:, 0, 4 * t:4 * t + 4], T[0][0:NH, t * P:t * P + P], ident[0:NH, 0:NH])
                fill(nc.tensor.transpose(out[0:TS, 0, 16:20], T[0][0:NH, TP:TOK], ident[0:NH, 0:NH]), D0)
                for h in range(NH):
                    out = take(DD[(h + 1) % 2], ("c.M", h))
                    mm(out[:, 0, 0:TP], selh[0:NH, h], T[4][0:NH, 0:TP], start=True, stop=True)
                    fill(mm(out[0:TS, 1, 0:TS], selh[0:NH, h, 0:TS], T[4][0:NH, TP:TOK], start=True, stop=True),
                         DD[(h + 1) % 2])
                proj_list(PROJ_A[0:1], 0)
                await_ev("rowexp", 2)
                for p in range(2):
                    wide(D1, ("c.w0", p), selp[0:NH, p], T[5][0:NH])
                    read_done(("pj", "vc", p))
                    turn(D0, ("c.v", p), pc[:, 4 + p])
                proj_list(PROJ_A[1:2], 1)
                for p in range(2):
                    turn(D1, ("c.k", p), pc[:, 2 + p])
                    scores(D0, ("c", "S", p))
                scores_sample(D1, ("c", "S4", 0))
                proj_list(PROJ_A[2:3], 2)
                for p in range(2):
                    wide(DD[p], ("c.em", p), selp[0:NH, p], T[3][0:NH])
                read_done(("c.k", 1))
                read_done(("c.v", 1))
                for p in range(2):
                    state_sums(DD[p], ("c", "dC", p), P)
                proj_list(PROJ_A[3:4], 3)
                await_ev("c.states", 2)
                out = take(D0, "c.nd4")
                for p in range(2):
                    for e in range(2):
                        for den in range(2):
                            i = out_tile(out[:, den], p, e, NCH, slice(p * TS, p * TS + TS), den)
                fill(i, D0)

                def outs(g, p, pair):
                    out = take(pair, (g, "nd", p))
                    for e in range(2):
                        for t in range(NCH):
                            for den in range(2 if g == "c" else 1):
                                i = out_tile(out[:, den], p, e, t, slice(t * P, t * P + P), den)
                        if g == "b":
                            i = out_tile(out[:, 1], p, e, NCH, slice(0, TS), 0)
                    fill(i, pair)

                outs("c", 0, D1)
                proj_list(PROJ_A[4:5], 4)
                outs("c", 1, D0)

                def head_norm(g, p, pair):
                    read_done((g, "nd", p))
                    flat(pair, (g, "mu", p), blk, pc[:, p])

                def head_var(g, p, pair):
                    await_ev(g + ".sq", p + 1)
                    flat(pair, (g, "va", p), blk, T[4])

                head_norm("c", 0, D1)
                proj_list(PROJ_A[5:6], 5)
                head_var("c", 0, D0)
                head_norm("c", 1, D1)
                proj_list(PROJ_B[0:1], 0)
                head_var("c", 1, D0)
                proj_list(PROJ_B[1:2], 1)
                down(u, m_down, ("mix", 1))
                u += 2
                m_down += 1

                for p in range(2):
                    read_done(("pj", "va", p))
                    turn(DD[p], ("a.v", p), pa[:, 4 + p])
                pe.wait_ge(ld["attn"], 64 * (l + 1))

                def a_scores(n, p, kind, t):
                    out = take(D0, ("a.S", n))
                    if kind == "t":
                        for e in range(2):
                            r = slice(e * HD, e * HD + HD)
                            i = mm(out[:, e, 0:P * (t + 1)], pa[r, p, t * P:t * P + P], pa[r, 2 + p, 0:P * (t + 1)],
                                   start=True, stop=True)
                    else:
                        hold(pe, "pe")
                        r = slice(t * HD, t * HD + HD)
                        mm(out[0:TS, 0, :], pa[r, p, TP:TOK], kc[r, p, :], start=True, stop=True)
                        i = mm(out[0:TS, 1, 0:TS], pa[r, p, TP:TOK], pa[r, 2 + p, TP:TOK], start=True, stop=True)
                    fill(i, D0)

                def a_turn(n, p, kind, t):
                    await_ev("a.probs", n + 1)
                    out = take(D1, ("a.T", n))
                    b = n % 2
                    if kind == "t":
                        for e in range(2):
                            for k in range(t + 1):
                                i = nc.tensor.transpose(out[:, e, k * P:k * P + P], pr[:, b, e, k * P:k * P + P], ident)
                    else:
                        hold(pe, "pe")
                        for k in range(4):
                            nc.tensor.transpose(out[:, 0, k * TS:k * TS + TS], pr[0:TS, b, 0, k * P:k * P + P],
                                                ident[0:TS, 0:TS])
                        i = nc.tensor.transpose(out[0:TS, 0, 256:320], pr[0:TS, b, 0, TP:TOK], ident[0:TS, 0:TS])
                    fill(i, D1)

                def a_values(n, p, kind, t):
                    if n == 0:
                        read_done(("a.v", 0))
                    out = take(B, ("a.o", p)) if (kind, t) == ("t", 0) else B.t
                    read_done(("a.T", n))
                    b = n % 2
                    if kind == "t":
                        for e in range(2):
                            h = 2 * p + e
                            for k in range(t + 1):
                                i = mm(out[e * HD:e * HD + HD, 0, t * P:t * P + P], vta[:, k, h * HD:h * HD + HD],
                                       pt[:, b, e, k * P:k * P + P], start=(k == 0), stop=(k == t))
                    else:
                        h = 2 * p + t
                        o = out[t * HD:t * HD + HD, 1, 0:TS]
                        for k in range(4):
                            mm(o, vc[:, k, h * HD:h * HD + HD], pt[:, b, 0, k * TS:k * TS + TS],
                               start=(k == 0), stop=False)
                        i = mm(o, vta[0:TS, 4, h * HD:h * HD + HD], pt[0:TS, b, 0, 256:320], start=False, stop=True)
                    if (kind, t) == ("s", 1):
                        fill(i, B)
                    else:
                        inc(i, E("a.pv"))

                todo = iter(PROJ_B[2:8])
                for n, step in enumerate(A_STEPS + [None]):
                    if step:
                        a_scores(n, *step)
                    if n:
                        a_turn(n - 1, *A_STEPS[n - 1])
                    if n % 2 == 0 and n < 12:
                        g, j = next(todo)
                        proj(u, A, ("pj", g, j))
                        u += 1
                    if n:
                        a_values(n - 1, *A_STEPS[n - 1])

                for j in range(4):
                    read_done(("pj", "qk"[j // 2] + "b", j % 2))
                    flat(DD[j % 2], ("b.rot", j), perm, pc[:, j])
                down(u, m_down, ("mix", 2))
                u += 2
                m_down += 1
                for p in range(2):
                    read_done(("pj", "vb", p))
                    turn(DD[p], ("b.v", p), pc[:, 4 + p])
                await_ev("b.turned", 4)
                for p in range(2):
                    turn(DD[p], ("b.k", p), pc[:, 2 + p])
                for p in range(2):
                    scores(DD[p], ("b", "S", p))
                scores_sample(D0, ("b", "S4", 0))
                read_done(("b.k", 0))
                read_done(("b.k", 1))
                for p in range(2):
                    state_sums(DD[(p + 1) % 2], ("b", "dC", p), HD)
                await_ev("b.states", 2)
                for p in range(2):
                    outs("b", p, DD[(p + 1) % 2])
                for p in range(2):
                    head_norm("b", p, DD[(p + 1) % 2])
                    head_var("b", p, DD[p])
                down(u, m_down, ("mix", 3))
                u += 2
                m_down += 1

                await_ev("mem_split")
                for p in range(2):
                    unit_there(u)
                    out = take((A, B)[p], ("x.k", p))
                    for k in range(KT):
                        ins = passes(out, u % RING, k, mem_hi[:, k], mem_lo[:, k], k == 0, k == KT - 1,
                                     widths=(NMEM,))
                        if k == 0:
                            ins[0].then_inc(unit_begun, 1)
                    fill(ins[-1], (A, B)[p])
                    u += 1
                out = take(A, "x.v")
                for half in range(2):
                    unit_there(u)
                    s = u % RING
                    for b in range(4):
                        k = 4 * half + b
                        wv = [w_[:, s, 2 * b:2 * b + 2, :].rearrange("p a n -> p (a n)") for w_ in (w_hi, w_lo)]
                        for mt in range(2):
                            mh, ml = (m_[:, k, mt * P:mt * P + P] for m_ in (mem_hi, mem_lo))
                            for i_, (a_, b_) in enumerate(((mh, wv[0]), (mh, wv[1]), (ml, wv[0]))):
                                i = mm(out[:, mt, 0:NMEM], a_, b_, start=(k == 0 and i_ == 0),
                                       stop=(k == KT - 1 and i_ == 2))
                                if b == 0 and mt == 0 and i_ == 0:
                                    i.then_inc(unit_begun, 1)
                    u += 1
                fill(i, A)
                stats(1)
                proj_two(u, 2, ("x.q", 0), ("x.q", 1))
                u += 2

                pe.wait_ge(ld["memc"], 32 * (l + 1))
                read_done(("x.q", 0))
                read_done(("x.q", 1))

                def x_scores(n, p, t):
                    out = take(D0, ("x.S", n))
                    m = P if t < NCH else TS
                    keys = mkT if t < NCH else kms
                    if t == NCH:
                        hold(pe, "pe")
                    for e in range(2):
                        r = slice(e * HD, e * HD + HD)
                        i = mm(out[0:m, e, 0:NMEM], qx[r, p, t * P:t * P + m], keys[r, p, :], start=True, stop=True)
                    fill(i, D0)

                def x_turn(n, p, t):
                    await_ev("x.probs", n + 1)
                    out = take(D1, ("x.T", n))
                    m = P if t < NCH else TS
                    if t == NCH:
                        hold(pe, "pe")
                    for e in range(2):
                        for k in range(2):
                            i = nc.tensor.transpose(out[:, e, k * P:k * P + m], prx[0:m, n % 2, e, k * P:k * P + P],
                                                    ident[0:m, 0:m])
                    fill(i, D1)

                def x_values(n, p, t):
                    out = take(B, ("x.o", p)) if t == 0 else B.t
                    read_done(("x.T", n))
                    m = P if t < NCH else TS
                    vals = mv if t < NCH else vms
                    for e in range(2):
                        h = 2 * p + e
                        o = out[e * HD:e * HD + HD, 0, t * P:t * P + P] if t < NCH else out[e * HD:e * HD + HD, 1, 0:TS]
                        for k in range(2):
                            i = mm(o, vals[:, k, h * HD:h * HD + HD], ptx[:, n % 2, e, k * P:k * P + m],
                                   start=(k == 0), stop=(k == 1))
                    if t < NCH:
                        inc(i, E("x.pv"))
                    else:
                        fill(i, B)

                for n, step in enumerate(X_STEPS + [None]):
                    if step:
                        x_scores(n, *step)
                    if n:
                        x_turn(n - 1, *X_STEPS[n - 1])
                        x_values(n - 1, *X_STEPS[n - 1])
                down(u, m_down, ("cross", 0))
                m_down += 1
                u += 2
                stats(2)
                assert u == FFN2_AT

                ffn(1, FFN2_AT, 3, m_down)
                stats(3)

        def full_of(eng, l, label):
            pair, n = uses[label]
            eng.wait_ge(pair.full.sem, pair.full.value(l, n + 1))
            return pair

        def freed_of(eng, l, label):
            pair, n = uses[label]
            eng.wait_ge(pair.free.sem, pair.free.value(l, n + 1))

        @block.scalar
        def _(act):
            f = nc.scalar.activation
            act.dma_start(cst[:], io["consts"]).then_inc(ld["const"], 16)
            act.dma_start(y[:], io["x"]).then_inc(ld["x"], 16)
            for d in range(DEPTH):
                act.dma_start(tb_dram[d].rearrange("h (p j) -> h p j", p=P),
                              bass.AP(io["rel"].tensor, d * NH * BAND, [[BAND, NH], [0, P], [1, BAND]]))\
                    .then_inc(ld["band"], 16)
            act.wait_ge(ld["x"], 16)
            for k in range(KT):
                f(x_hi[:, k], y[:, k], ACT.Copy).then_inc(x_hi_done.sem, 1)
            act.wait_ge(ld["const"], 16)

            with act.Fori(0, DEPTH) as l:
                def step(ins):
                    act_step.n += 1
                    ins.then_inc(act_step.sem, 1)
                    act.wait_ge(act_step.sem, act_step.value(l, act_step.n))

                def free(ins, label):
                    ins.then_inc(uses[label][0].free.sem, 1)

                def full(label):
                    return full_of(act, l, label).t

                def await_ev(name, k=1):
                    act.wait_ge(E(name).sem, E(name).value(l, k))

                act.wait_ge(x_ready.sem, l * x_ready.per + KT)
                act.dma_start(prm[:], io["prm"][l]).then_inc(ld["prm"], 16)
                act.dma_start(gw_raw[:], io["gates"][l]).then_inc(ld["gw"], 16)
                act.dma_start(lru_w[:], io["lru"][l]).then_inc(ld["lru"], 16)

                def ffn(fi, h0):
                    a0, b0 = uses[("ffn", fi, "A")], uses[("ffn", fi, "B")]
                    nc.scalar.preload_act_table_set("silu_and_others")

                    def tile(j, reuse, au, hu):
                        act.wait_ge(A.full.sem, A.full.value(l, a0 + j + 1) + au)
                        if reuse:
                            act.wait_ge(B.free.sem, B.free.value(l, b0 + j - 1) + au)
                        f(sil[j % 2][:, 0:TOK].rearrange("p (a n) -> p a n", a=2), A.halves(), ACT.Silu)\
                            .then_inc(A.free.sem, 1)
                        act.wait_ge(B.free.sem, B.free.value(l, b0 + j + 1) + au)
                        f(h_hi[:, j % 2], hf[:, 0:TOK], ACT.Copy).then_inc(h_hi_done.sem, 1)
                    for j in range(2):
                        tile(j, False, 0, 0)
                    with act.Fori(0, FT // 2 - 1) as i:
                        for j in range(2):
                            tile(2 + j, True, 2 * i, 0)
                    h_hi_done.n += FT

                def squares(j, label):
                    nc.scalar.preload_act_table_set("natural_log_exp_and_others")
                    for n in range(KT):
                        freed_of(act, l, (label, n))
                        if n >= 2:
                            act.wait_ge(s2_added.sem, s2_added.value(l, (KT - 1) * j + n - 1))
                        inc(f(sil[n % 2][:, 0:TOK], y[:, n], ACT.Square), sq_done)

                def norm(j):
                    full(("mean", j))
                    inc(f(rs[:, 0:TOK].rearrange("p (a n) -> p a n", a=2), D0.halves(), ACT.Square), mean_sq)
                    act.wait_ge(var_done.sem, var_done.value(l, j + 1))
                    step(f(rs[:, 0:TOK], rs[:, 0:TOK], ACT.Ln, bias=eps))
                    inc(f(rs[:, 0:TOK], rs[:, 0:TOK], ACT.Exp, scale=-0.5), rstd_done)
                    for n in range(KT):
                        act.wait_ge(ln_scaled.sem, ln_scaled.value(l, KT * j + n + 1))
                        step(f(y[:, n], y[:, n], ACT.Identity, bias=prm[:, 32 + 8 * j + n:33 + 8 * j + n],
                               scale=prm[:, 8 * j + n:8 * j + n + 1]))
                        inc(f(x_hi[:, n], y[:, n], ACT.Copy), x_hi_done)

                def proj_out(g, j, dst, func=ACT.Identity):
                    full(("pj", g, j))
                    pair = uses[("pj", g, j)][0]
                    c = BIAS_COL[(g, j)]
                    free(f(dst.rearrange("p (a n) -> p a n", a=2), pair.halves(), func, bias=prm[:, c:c + 1]),
                         ("pj", g, j))

                def h_hi_of(srcs, k0, name):
                    for j in range(2):
                        await_ev(name, j + 1)
                        inc(f(h_hi[:, j], srcs[j], ACT.Copy), h_hi_done)

                act.wait_ge(ld["prm"], 16 * l + 16)
                hold(act, "act")
                ffn(0, 0)
                squares(0, ("ffn", 0))
                norm(0)

                for j in range(2):
                    full(("pj", "xd", j))
                    pair = uses[("pj", "xd", j)][0]
                    c = BIAS_COL[("xd", j)]
                    b = prm[:, c:c + 1]
                    if j == 0 :
                        act.wait_ge(E("xp_free").sem, E("xp_free").value(l, 1))
                    step(f(xp[:, j, 3:3 + HT], pair.t[:, 0, 0:HT], ACT.Identity, bias=b))
                    step(f(xp[:, j, 3 + HT:3 + TP], pair.t[:, 1, 0:TP - HT], ACT.Identity, bias=b))
                    free(f(xp[:, j, 6 + TP:XPW], pair.t[:, 1, TP - HT:HT], ACT.Identity, bias=b), ("pj", "xd", j))
                for j in range(2):
                    proj_out("yd", j, yd[:, j], ACT.Gelu_apprx_tanh)
                nc.scalar.preload_act_table_set("natural_log_exp_and_others")
                lam = prm[:, C_LAM:C_LAM + 2]
                step(f(lamt[:, 0:2], lam, ACT.Abs))
                step(f(lamt[:, 0:2], lamt[:, 0:2], ACT.Exp, scale=-1.0))
                inc(f(lamt[:, 0:2], lamt[:, 0:2], ACT.Ln, bias=ones[:, 0:1]), E("lam_ln"))
                for g, j in PROJ_C[0:2]:
                    proj_out(g, j, pc[:, j])
                for j in range(2):
                    for nm, c, dst in (("d.r", C_BA, T[1]), ("d.i", C_BI, T[2])):
                        full((nm, j))
                        pair = uses[(nm, j)][0]
                        step(f(dst[:, 0:290], pair.t[:, 0, 0:290], ACT.Sigmoid, bias=prm[:, c + j:c + j + 1]))
                        free(f(dst[:, 290:XCW], pair.t[:, 1, 0:XCW - 290], ACT.Sigmoid,
                               bias=prm[:, c + j:c + j + 1]), (nm, j))
                    freed_of(act, l, ("d.r", j))
                    await_ev("lam4")
                    inc(f(T[1][:, 0:XCW], T[1][:, 0:XCW], ACT.Tanh, scale=lam4[:, j:j + 1]), E("d.tanh"))
                    act.wait_ge(E("d.tanh").sem, E("d.tanh").value(l, j + 1))
                    inc(f(T[3][:, 0:XCW], T[1][:, 0:XCW], ACT.Sqrt), E("d.sqrt"))
                    more = PROJ_C[2:5] if j == 0 else PROJ_C[5:8]
                    for g, jj in more:
                        proj_out(g, jj, pc[:, 2 * "qkvo".index(g[0]) + jj],
                                 ACT.Sigmoid if g == "oc" else ACT.Identity)
                h_hi_of([yd[:, 0], yd[:, 1]], 0, "d.out")
                nc.scalar.preload_act_table_set("natural_log_exp_and_others")
                await_ev("rows_in")
                r4 = lambda t: t[0:NH, 0:TOK]
                step(f(r4(T[0]), r4(T[0]), ACT.Identity, bias=prm[0:NH, C_GI:C_GI + 1]))
                step(f(r4(T[1]), r4(T[1]), ACT.Identity, bias=prm[0:NH, C_GF:C_GF + 1]))
                step(f(r4(T[2]), r4(T[1]), ACT.Abs))
                step(f(r4(T[2]), r4(T[2]), ACT.Exp, scale=-1.0))
                inc(f(r4(T[2]), r4(T[2]), ACT.Ln, bias=ones[0:NH, 0:1]), E("lf_ln"))
                await_ev("rows")
                inc(f(r4(T[5]), r4(T[5]), ACT.Exp), E("rowexp"))
                inc(f(r4(T[3]), r4(T[2]), ACT.Exp, scale=-1.0), E("rowexp"))
                act.dma_start(io["out_m"][l], m_out[:]).then_inc(stored["m"], 16)
                proj_out("qa", 0, pa[:, 0])
                freed_of(act, l, "c.aT")
                for h in range(NH):
                    freed_of(act, l, ("c.M", h))
                    for t in range(NCH):
                        step(f(dT[:, h, t * P:t * P + P], dT[:, h, t * P:t * P + P], ACT.Exp,
                               bias=aT[:, 4 * t + h:4 * t + h + 1]))
                    inc(f(dT[0:TS, h, TP:TOK], dT[0:TS, h, TP:TOK], ACT.Exp, bias=aT[0:TS, 16 + h:17 + h]), E("c.dT"))

                def values_out(g, p, dst):
                    full((g + ".v", p))
                    pair = uses[(g + ".v", p)][0]
                    step(f(dst[:, 0:4, p * P:p * P + P], pair.t[:, 0, :].rearrange("p (t n) -> p t n", t=4), ACT.Copy))
                    free(f(dst[0:TS, 4, p * P:p * P + P], pair.t[0:TS, 1, 0:P], ACT.Copy), (g + ".v", p))

                for p in range(2):
                    values_out("c", p, vt)
                proj_out("qa", 1, pa[:, 1])
                proj_out("ka", 0, pa[:, 2])
                for p in range(2):
                    full(("c.em", p))
                    pair = uses[("c.em", p)][0]
                    step(f(T[p][:, 0:TP], pair.t[:, 0, :], ACT.Copy))
                    free(f(T[p][:, TP:TOK], pair.t[:, 1, 0:TS], ACT.Copy), ("c.em", p))
                proj_out("ka", 1, pa[:, 3])
                proj_out("va", 0, pa[:, 4])

                def norm_sq(g, p):
                    freed_of(act, l, (g, "mu", p))
                    inc(f(T[4][:, 0:TOK], pc[:, p], ACT.Square), E(g + ".sq"))

                def norm_rstd(g, p):
                    full((g, "va", p))
                    pair = uses[(g, "va", p)][0]
                    free(f(T[5][:, 0:TOK].rearrange("p (a n) -> p a n", a=2), pair.halves(), ACT.Ln, bias=eps),
                         (g, "va", p))
                    freed_of(act, l, (g, "va", p))
                    inc(f(T[5][:, 0:TOK], T[5][:, 0:TOK], ACT.Exp, scale=-0.5), E(g + ".rstd"))

                norm_sq("c", 0)
                proj_out("va", 1, pa[:, 5])
                norm_rstd("c", 0)
                norm_sq("c", 1)
                await_ev("c.out", 1)
                inc(f(h_hi[:, 0], pc[:, 0], ACT.Copy), h_hi_done)
                norm_rstd("c", 1)
                await_ev("c.out", 2)
                inc(f(h_hi[:, 1], pc[:, 1], ACT.Copy), h_hi_done)
                act.dma_start(io["out_ak"][l], pa[:, 2:6]).then_inc(stored["ak"], 16)
                act.dma_start(io["out_lru"][l], ld_out[:]).then_inc(stored["lru"], 16)
                act.dma_start(io["out_mls"][l], cn_out[:]).then_inc(stored["mls"], 16)
                freed_of(act, l, ("c", "nd", 1))
                act.wait_ge(ld["band"], 16 * DEPTH)
                act.dma_start(tb[:], tb_dram[l, :, P:].rearrange("h (p j) -> p h j", p=P)[:, :, 0:256])\
                    .then_inc(ld["attn"], 16)
                act.dma_start(kc[:], io["kc"][l]).then_inc(ld["attn"], 16)
                act.dma_start(vc[:], io["vc"][l]).then_inc(ld["attn"], 16)
                act.dma_start(far, io["far"][l].to_broadcast([P, NH])).then_inc(ld["attn"], 16)
                act.wait_ge(h_ready.sem, l * h_ready.per + FT + 4)
                proj_out("qb", 0, pc[:, 0])
                proj_out("qb", 1, pc[:, 1])
                for p in range(2):
                    values_out("a", p, vta)

                def a_exp(n, p, kind, t):
                    b = n % 2
                    await_ev("a.nmax", n + 1)
                    if kind == "t":
                        w = P * (t + 1)
                        for e in range(2):
                            i = f(pr[:, b, e, 0:w], pr[:, b, e, 0:w], ACT.Exp, bias=nmx[:, 2 * b + e:2 * b + e + 1],
                                  accum_out=sm[:, 2 * b + e:2 * b + e + 1])
                            step(i) if e == 0 else inc(i, E("a.exp"))
                    else:
                        inc(f(pr[0:TS, b, 0, :], pr[0:TS, b, 0, :], ACT.Exp, bias=nmx[0:TS, 2 * b:2 * b + 1],
                              accum_out=sm[0:TS, 2 * b:2 * b + 1]), E("a.exp"))

                def a_turned(n, p, kind, t):
                    b = n % 2
                    full(("a.T", n))
                    if n >= 2:
                        pv_before(n - 2)
                    if kind == "t":
                        w = P * (t + 1)
                        free(f(pt[:, b, :, 0:w], D1.t[:, :, 0:w], ACT.Copy), ("a.T", n))
                    else:
                        step(f(pt[:, b, 0, 0:256], D1.t[:, 0, 0:256], ACT.Copy))
                        free(f(pt[0:TS, b, 0, 256:320], D1.t[0:TS, 0, 256:320], ACT.Copy), ("a.T", n))

                def pv_before(n):
                    if A_STEPS[n][1:] == ("s", 1):
                        full_of(act, l, ("a.o", A_STEPS[n][0]))
                    else:
                        k = sum(1 for s in A_STEPS[:n + 1] if s[1:] != ("s", 1))
                        await_ev("a.pv", k)

                def a_out(p):
                    full(("a.o", p))
                    step(f(pa[:, p, 0:TP], B.t[:, 0, :], ACT.Copy))
                    free(f(pa[:, p, TP:TOK], B.t[:, 1, 0:TS], ACT.Copy), ("a.o", p))

                todo = iter(PROJ_B[2:8])
                nc.scalar.preload_act_table_set("exp_and_others")
                for n, s_ in enumerate(A_STEPS + [None]):
                    if s_:
                        a_exp(n, *s_)
                    if n:
                        a_turned(n - 1, *A_STEPS[n - 1])
                    if n % 2 == 0 and n < 12:
                        g, j = next(todo)
                        proj_out(g, j, pc[:, 2 * "qkvg".index(g[0]) + j], ACT.Silu if g == "gb" else ACT.Identity)
                    if n == 6:
                        a_out(0)
                a_out(1)
                for j in range(2):
                    freed_of(act, l, ("a.o", j))
                    inc(f(h_hi[:, j], pa[:, j], ACT.Copy), h_hi_done)
                nc.scalar.preload_act_table_set("natural_log_exp_and_others")
                for p in range(2):
                    values_out("b", p, vt)
                for p in range(2):
                    full(("b", "nd", p))
                    pair = uses[("b", "nd", p)][0]
                    step(f(pc[:, p, 0:TP], pair.t[:, 0, :], ACT.Copy))
                    free(f(pc[:, p, TP:TOK], pair.t[:, 1, 0:TS], ACT.Copy), ("b", "nd", p))
                for p in range(2):
                    norm_sq("b", p)
                    norm_rstd("b", p)
                    await_ev("b.out", p + 1)
                    inc(f(h_hi[:, p], pc[:, p], ACT.Copy), h_hi_done)
                act.dma_start(io["out_ret"][l], st_out[:]).then_inc(stored["ret"], 16)
                act.wait_ge(h_ready.sem, l * h_ready.per + FT + 8)
                act.wait_ge(stored["ak"], 16 * l + 16)
                act.dma_start(mem_raw[:], io["mem"]).then_inc(ld["mem"], 16)
                act.dma_start(kms[:], io["kms"][l]).then_inc(ld["memc"], 16)
                act.dma_start(vms[:], io["vms"][l]).then_inc(ld["memc"], 16)
                act.wait_ge(ld["mem"], 16 * l + 16)
                inc(f(mem_hi[:], mem_raw[:], ACT.Copy), E("mem_hi"))
                squares(1, ("mix", 3))
                for p in range(2):
                    full(("x.k", p))
                    free(f(mkT[:, p], (A, B)[p].t[:, 0, 0:NMEM], ACT.Copy), ("x.k", p))
                full("x.v")
                free(f(mv[:], A.t[:, :, 0:NMEM], ACT.Copy), "x.v")
                norm(1)
                for p in range(2):
                    full(("x.q", p))
                    free(f(qx[:, p].rearrange("p (a n) -> p a n", a=2), (A, B)[p].halves(), ACT.Copy), ("x.q", p))
                freed_of(act, l, "x.v")
                act.dma_start(io["out_mk"][l], mkT[:]).then_inc(stored["mk"], 16)
                act.dma_start(io["out_mv"][l], mv[:]).then_inc(stored["mvv"], 16)

                def x_exp(n, p, t):
                    m = P if t < NCH else TS
                    b = n % 2
                    await_ev("x.nmax", n + 1)
                    for e in range(2):
                        i = f(prx[0:m, b, e, :], D0.t[0:m, e, 0:NMEM], ACT.Exp, bias=nmx[0:m, 2 * b + e:2 * b + e + 1],
                              scale=HD ** -0.5, accum_out=sm[0:m, 2 * b + e:2 * b + e + 1])
                        if e == 0:
                            step(i)
                        else:
                            free(i, ("x.S", n))

                def x_turned(n, p, t):
                    full(("x.T", n))
                    m = P if t < NCH else TS
                    if n >= 2:
                        pp, tt = X_STEPS[n - 2]
                        if tt < NCH:
                            await_ev("x.pv", sum(1 for s in X_STEPS[:n - 1] if s[1] < NCH))
                        else:
                            full_of(act, l, ("x.o", pp))
                    src = D1.t[:, :, 0:NMEM].rearrange("p e (k m) -> p e k m", k=2)[:, :, :, 0:m]
                    dst = ptx[:, n % 2].rearrange("p e (k m) -> p e k m", k=2)[:, :, :, 0:m]
                    free(f(dst, src, ACT.Copy), ("x.T", n))

                def x_out(p):
                    full(("x.o", p))
                    step(f(qx[:, p, 0:TP], B.t[:, 0, :], ACT.Copy))
                    free(f(qx[:, p, TP:TOK], B.t[:, 1, 0:TS], ACT.Copy), ("x.o", p))

                for n, s_ in enumerate(X_STEPS + [None]):
                    if s_:
                        x_exp(n, *s_)
                    if n:
                        x_turned(n - 1, *X_STEPS[n - 1])
                    if n == 5:
                        x_out(0)
                x_out(1)
                for j in range(2):
                    freed_of(act, l, ("x.o", j))
                    inc(f(h_hi[:, j], qx[:, j], ACT.Copy), h_hi_done)
                squares(2, ("cross", 0))
                norm(2)
                act.wait_ge(stored["mk"], 16 * l + 16)
                act.wait_ge(stored["mvv"], 16 * l + 16)
                act.wait_ge(stored["mls"], 16 * l + 16)
                act.wait_ge(stored["ret"], 16 * l + 16)
                act.wait_ge(stored["lru"], 16 * l + 16)
                act.wait_ge(stored["m"], 16 * l + 16)
                hold(act, "act")
                ffn(1, 0)
                squares(3, ("ffn", 1))
                norm(3)
            act.wait_ge(x_hi_done.sem, x_hi_done.per * DEPTH + KT)
            act.dma_start(io["out_y"], y[:]).then_inc(stored["y"], 16)
            act.wait_ge(stored["y"], 16)

        @block.vector
        def _(dve):
            v = nc.vector
            v.memset(small[:, 0:64], 0.0).then_inc(E("init").sem, 1)
            dve.wait_ge(E("init").sem, 1)
            v.memset(eps, EPS).then_inc(E("init").sem, 1)
            dve.wait_ge(E("init").sem, 2)
            for k in range(KT):
                dve.wait_ge(x_hi_done.sem, k + 1)
                v.tensor_tensor(x_lo[:, k], y[:, k], x_hi[:, k].bitcast(F32), ALU.subtract).then_inc(x_ready.sem, 1)
            dve.wait_ge(ld["const"], 16)

            with dve.Fori(0, DEPTH) as l:
                def step(ins, ev_=None, off=0):
                    c = ev_ or dve_step
                    c.n += 1
                    ins.then_inc(c.sem, 1)
                    dve.wait_ge(c.sem, c.value(l, c.n) + off)

                def free(ins, label):
                    pair, n = uses[label]
                    ins.then_inc(pair.free.sem, 1)
                    dve.wait_ge(pair.free.sem, pair.free.value(l, n + 1))

                def full(label):
                    return full_of(dve, l, label).t

                def freed(label):
                    freed_of(dve, l, label)

                def await_ev(name, k=1):
                    dve.wait_ge(E(name).sem, E(name).value(l, k))

                def ffn(fi, m0):
                    b0, h0 = uses[("ffn", fi, "B")], 2 * m0
                    d0 = (uses[("ffn", fi, "D0")], uses[("ffn", fi, "D1")])
                    step(v.memset(ysc, ALPHA))

                    def hidden(j, off):
                        dve.wait_ge(B.full.sem, B.full.value(l, b0 + j + 1) + off)
                        dve.wait_ge(silu_free(fi, j)[0], silu_free(fi, j)[1] + off)
                        v.scalar_tensor_tensor(out=hf[:, 0:TOK].rearrange("p (a n) -> p a n", a=2),
                                               in0=sil[j % 2][:, 0:TOK].rearrange("p (a n) -> p a n", a=2), scalar=0.5,
                                               in1=B.halves(), op0=ALU.mult, op1=ALU.mult).then_inc(B.free.sem, 1)
                        dve.wait_ge(h_hi_done.sem, l * h_hi_done.per + (h0 + j + 1) + off)
                        v.tensor_tensor(h_lo[:, j % 2], hf[:, 0:TOK], h_hi[:, j % 2].bitcast(F32), ALU.subtract)\
                            .then_inc(h_ready.sem, 1)
                        dve.wait_ge(h_ready.sem, l * h_ready.per + (h0 + j + 1) + off)

                    def silu_free(fi, j):
                        a0 = uses[("ffn", fi, "A")]
                        return A.free.sem, A.free.value(l, a0 + j + 1)

                    for j in range(2):
                        hidden(j, 0)
                    hold(dve, "dve")
                    with dve.Fori(0, FT // 2 - 1) as i:
                        for n in range(KT):
                            pair = DD[n % 2]
                            k = d0[n % 2] + n // 2 + 1
                            dve.wait_ge(pair.full.sem, pair.full.value(l, k) + 4 * i)
                            v.scalar_tensor_tensor(out=y[:, n].rearrange("p (a n) -> p a n", a=2),
                                                   in0=y[:, n].rearrange("p (a n) -> p a n", a=2), scalar=ysc,
                                                   in1=pair.halves(), op0=ALU.mult, op1=ALU.add)\
                                .then_inc(pair.free.sem, 1)
                            if n == KT - 1:
                                for q in range(2):
                                    dve.wait_ge(DD[q].free.sem, DD[q].free.value(l, d0[q] + 4) + 4 * i)
                        v.memset(ysc, 1.0).then_inc(E("ysc").sem, 1)
                        dve.wait_ge(E("ysc").sem, E("ysc").value(l, 1 + (FT // 2 - 1) * fi) + i)
                        for j in range(2):
                            hidden(2 + j, 2 * i)
                    E("ysc").n += FT // 2 - 1
                    h_ready.n += FT

                def add_down(label):
                    for n in range(KT):
                        full((label, n))
                        free(v.scalar_tensor_tensor(out=y[:, n].rearrange("p (a n) -> p a n", a=2),
                                                    in0=y[:, n].rearrange("p (a n) -> p a n", a=2), scalar=ysc,
                                                    in1=DD[n % 2].halves(), op0=ALU.mult, op1=ALU.add), (label, n))

                def add_down_norm(j, label, between=None):
                    t576 = lambda t: t[:, 0:TOK]
                    for n in range(KT):
                        full((label, n))
                        free(v.scalar_tensor_tensor(out=y[:, n].rearrange("p (a n) -> p a n", a=2),
                                                    in0=y[:, n].rearrange("p (a n) -> p a n", a=2), scalar=ysc,
                                                    in1=DD[n % 2].halves(), op0=ALU.mult, op1=ALU.add), (label, n))
                        if n == 1:
                            step(v.tensor_tensor(t576(s1), y[:, 0], y[:, 1], ALU.add))
                        if n > 1:
                            step(v.tensor_tensor(t576(s1), t576(s1), y[:, n], ALU.add))
                        if n:
                            square(j, n - 1)
                        if n == 4 and between:
                            between()
                    square(j, KT - 1)
                    full(("mean", j))
                    full(("sq", j))
                    dve.wait_ge(mean_sq.sem, mean_sq.value(l, j + 1))
                    free(v.tensor_tensor(rs[:, 0:TOK].rearrange("p (a n) -> p a n", a=2), D1.halves(),
                                         rs[:, 0:TOK].rearrange("p (a n) -> p a n", a=2), ALU.subtract), ("sq", j))
                    step(v.tensor_scalar(t576(rs), t576(rs), 0.0, None, ALU.max), var_done)

                    def centre(n):
                        i = v.tensor_tensor(y[:, n].rearrange("p (a n) -> p a n", a=2),
                                            y[:, n].rearrange("p (a n) -> p a n", a=2), D0.halves(), ALU.subtract)
                        free(i, ("mean", j)) if n == KT - 1 else step(i)

                    def lo(n):
                        dve.wait_ge(x_hi_done.sem, x_hi_done.value(l, KT * j + n + 1))
                        step(v.tensor_tensor(x_lo[:, n], y[:, n], x_hi[:, n].bitcast(F32), ALU.subtract), x_ready)

                    centre(0)
                    centre(1)
                    dve.wait_ge(rstd_done.sem, rstd_done.value(l, j + 1))
                    for n in range(KT):
                        step(v.tensor_tensor(y[:, n], y[:, n], t576(rs), ALU.mult), ln_scaled)
                        if n + 2 < KT:
                            centre(n + 2)
                        if n:
                            lo(n - 1)
                    lo(KT - 1)

                def square(j, n):
                    dve.wait_ge(sq_done.sem, sq_done.value(l, KT * j + n + 1))
                    a, b = s2[:, 0:TOK], sil[n % 2][:, 0:TOK]
                    if n == 0:
                        i = v.tensor_copy(a, b)
                    else:
                        i = v.tensor_tensor(a, a, b, ALU.add)
                    step(i, stats_ready if n == KT - 1 else s2_added)

                def h_lo_of(srcs):
                    for j in range(2):
                        dve.wait_ge(h_hi_done.sem, h_hi_done.value(l, h_ready.n + 1))
                        step(v.tensor_tensor(h_lo[:, j], srcs[j], h_hi[:, j].bitcast(F32), ALU.subtract), h_ready)

                dve.wait_ge(ld["gw"], 16 * l + 16)
                step(v.tensor_copy(gw_hi[:], gw_raw[:]))
                step(v.tensor_tensor(gw_lo[:], gw_raw[:], gw_hi[:].bitcast(F32), ALU.subtract), E("gw_split"))
                dve.wait_ge(ld["prm"], 16 * l + 16)
                step(v.memset(xp[:, :, 0:3], 0.0))
                step(v.tensor_copy(xp[:, :, 3 + TP:6 + TP], prm[:, C_CBUF:C_CBUF + 6].rearrange("p (a n) -> p a n", a=2)),
                     E("xp_free"))
                ffn(0, 0)
                add_down_norm(0, ("ffn", 0))
                step(v.memset(ysc, ALPHA))

                def conv(j):
                    xc = T[0][:, 0:XCW]
                    w = lambda i: prm[:, C_CONVW + 4 * j + i:C_CONVW + 4 * j + i + 1]
                    freed(("pj", "xd", j))
                    step(v.tensor_scalar(xc, xp[:, j, 0:XCW], w(0), prm[:, C_CONVB + j:C_CONVB + j + 1],
                                         ALU.mult, ALU.add))
                    for i in range(1, 4):
                        step(v.scalar_tensor_tensor(out=xc, in0=xp[:, j, i:i + XCW], scalar=w(i), in1=xc,
                                                    op0=ALU.mult, op1=ALU.add), E("conv") if i == 3 else None)

                conv(0)
                full("gates")
                gi, gf = dT[:, 0], dT[:, 1]
                step(v.tensor_copy(gi[0:NH, :].rearrange("p (a n) -> p a n", a=2), A.t[0:NH, :, 0:HT]))
                free(v.tensor_copy(gf[0:NH, :].rearrange("p (a n) -> p a n", a=2), A.t[32:32 + NH, :, 0:HT]), "gates")
                await_ev("lam_ln")
                step(v.tensor_scalar(lamt[:, 2:4], prm[:, C_LAM:C_LAM + 2], -1.0, 0.0, ALU.mult, ALU.max))
                step(v.tensor_tensor(lamt[:, 2:4], lamt[:, 2:4], lamt[:, 0:2], ALU.add))
                step(v.tensor_scalar(lam4, lamt[:, 2:4], 4.0, None, ALU.mult), E("lam4"))
                for j in range(2):
                    xc, t_, i_, q_, a_ = (T[n][:, 0:XCW] for n in (0, 1, 2, 3, 4))
                    if j == 1:
                        conv(1)
                    freed(("d.i", j))
                    step(v.tensor_tensor(i_, i_, xc, ALU.mult))
                    await_ev("d.tanh", j + 1)
                    r_ = T[5][:, 0:XCW]
                    step(v.tensor_scalar(r_, t_, 1.0, None, ALU.add))
                    step(v.reciprocal(r_, r_))
                    step(v.tensor_tensor(i_, i_, r_, ALU.mult))
                    step(v.tensor_scalar(a_, t_, -1.0, 1.0, ALU.mult, ALU.add))
                    step(v.tensor_tensor(a_, a_, r_, ALU.mult))
                    await_ev("d.sqrt", j + 1)
                    step(v.scalar_tensor_tensor(out=q_, in0=q_, scalar=2.0, in1=i_, op0=ALU.mult, op1=ALU.mult))
                    step(v.tensor_tensor_scan(r_[:, 0:TP], a_[:, 0:TP], q_[:, 0:TP], 0.0, ALU.mult, ALU.add))
                    step(v.tensor_tensor_scan(r_[:, TP + 3:XCW], a_[:, TP + 3:XCW], q_[:, TP + 3:XCW],
                                              prm[:, C_H0 + j:C_H0 + j + 1], ALU.mult, ALU.add))
                    step(v.tensor_copy(ld_out[:, j, 0:1], r_[:, TP - 1:TP]))
                    step(v.tensor_copy(ld_out[:, j, 1:2], r_[:, XCW - 1:XCW]))
                    step(v.tensor_copy(ld_out[:, j, 2:5], xp[:, j, TP:TP + 3]))
                    step(v.tensor_copy(ld_out[:, j, 5:8], xp[:, j, XPW - 3:XPW]))
                    freed(("pj", "yd", j))
                    step(v.tensor_tensor(yd[:, j, 0:TP], yd[:, j, 0:TP], r_[:, 0:TP], ALU.mult))
                    step(v.tensor_tensor(yd[:, j, TP:TOK], yd[:, j, TP:TOK], r_[:, TP + 3:XCW], ALU.mult), E("d.out"))
                h_lo_of([yd[:, 0], yd[:, 1]])

                r4 = lambda t: t[0:NH, 0:TOK]
                step(v.tensor_copy(r4(T[0]), gi[0:NH, :]))
                step(v.tensor_copy(r4(T[1]), gf[0:NH, :]), E("rows_in"))
                await_ev("lf_ln")
                step(v.scalar_tensor_tensor(out=r4(T[1]), in0=r4(T[1]), scalar=0.0, in1=r4(T[2]), op0=ALU.min,
                                            op1=ALU.subtract))
                for t in range(NCH + 1):
                    c = slice(t * P, min(t * P + P, TOK))
                    step(v.tensor_tensor_scan(T[3][0:NH, c], ones[0:NH, 0:c.stop - c.start], T[1][0:NH, c], 0.0,
                                              ALU.mult, ALU.add))
                step(v.tensor_tensor_scan(T[2][0:NH, 0:TP], T[1][0:NH, 0:TP], T[0][0:NH, 0:TP], 0.0, ALU.add, ALU.max))
                step(v.tensor_tensor_scan(T[2][0:NH, TP:TOK], T[1][0:NH, TP:TOK], T[0][0:NH, TP:TOK],
                                          prm[0:NH, C_M0:C_M0 + 1], ALU.add, ALU.max))
                step(v.tensor_tensor(r4(T[0]), r4(T[0]), r4(T[3]), ALU.subtract))
                step(v.tensor_tensor(r4(T[4]), r4(T[3]), r4(T[2]), ALU.subtract))
                step(v.tensor_copy(T[5][0:NH, 0:P], T[4][0:NH, 0:P]))
                for t in range(1, NCH):
                    c = slice(t * P, t * P + P)
                    step(v.tensor_scalar(T[5][0:NH, c], T[4][0:NH, c], T[2][0:NH, t * P - 1:t * P], None, ALU.add))
                step(v.tensor_copy(m_out[:, 0:1], T[2][0:NH, TP - 1:TP]))
                step(v.tensor_copy(m_out[:, 1:2], T[2][0:NH, TOK - 1:TOK]))
                step(v.tensor_scalar(T[5][0:NH, TP:TOK], T[4][0:NH, TP:TOK], prm[0:NH, C_M0:C_M0 + 1], None, ALU.add),
                     E("rows"))
                add_down(("mix", 0))
                step(v.memset(ysc, 1.0))
                full("c.aT")
                step(v.tensor_copy(aT[:, 0:16], D0.t[:, 0, 0:16]))
                free(v.tensor_copy(aT[0:TS, 16:20], D0.t[0:TS, 0, 16:20]), "c.aT")
                for h in range(NH):
                    full(("c.M", h))
                    t_ = uses[("c.M", h)][0].t
                    step(v.tensor_tensor(dT[:, h, 0:TP].rearrange("p (t n) -> p t n", t=4),
                                         t_[:, 0, :].rearrange("p (t n) -> p t n", t=4),
                                         mask.rearrange("p (a n) -> p a n", a=1).to_broadcast([P, 4, P]), ALU.add))
                    free(v.tensor_tensor(dT[0:TS, h, TP:TOK], t_[0:TS, 1, 0:TS], mask[0:TS, 0:TS], ALU.add),
                         ("c.M", h))
                step(v.memset(dT[TS:P, :, TP:TOK], 0.0))
                step(v.memset(vt[TS:P, 4, :], 0.0))
                step(v.tensor_copy(cs[:, :, 0, 0:HD], prm[:, C_SC:C_SC + 128].rearrange("p (a n) -> p a n", a=2)))
                step(v.tensor_copy(cs[:, :, 0, HD:P],
                                   prm[:, C_SN:C_SN + 2].rearrange("p (a n) -> p a n", n=1).to_broadcast([P, 2, HD])))
                for p in range(2):
                    full(("c.w0", p))
                    t_ = uses[("c.w0", p)][0].t
                    freed(("pj", "qc", p))
                    step(v.tensor_tensor(qw[:, p, 0:TP], pc[:, p, 0:TP], t_[:, 0, :], ALU.mult))
                    step(v.tensor_tensor(qw[:, p, TP:TOK], pc[:, p, TP:TOK], t_[:, 1, 0:TS], ALU.mult))
                    step(v.tensor_copy(wst[:, p, 0:4], t_[:, 0, P - 1:TP:P]))
                    free(v.tensor_copy(wst[:, p, 4:5], t_[:, 1, TS - 1:TS]), ("c.w0", p))
                await_ev("c.dT", 4)
                for h in range(NH):
                    step(v.tensor_scalar(wr[:, 0:4, h], dT[:, h, P - 1:TP:P], HD ** -0.5, None, ALU.mult))
                    step(v.tensor_scalar(wr[0:TS, 4, h:h + 1], dT[0:TS, h, TOK - 1:TOK], HD ** -0.5, None, ALU.mult))

                def keys_out(g, p, w):
                    full((g + ".k", p))
                    t_ = uses[(g + ".k", p)][0].t
                    step(v.tensor_tensor(kw[:, 0:4, p * P:p * P + P].rearrange("p t (e d) -> p t e d", e=2),
                                         t_[:, 0, :].rearrange("p (t e d) -> p t e d", t=4, e=2),
                                         w[:, 0:4, 2 * p:2 * p + 2].rearrange("p t (e d) -> p t e d", d=1)
                                         .to_broadcast([P, 4, 2, HD]), ALU.mult))
                    free(v.tensor_tensor(kw[0:TS, 4, p * P:p * P + P].rearrange("p (e d) -> p e d", e=2),
                                         t_[0:TS, 1, 0:P].rearrange("p (e d) -> p e d", e=2),
                                         w[0:TS, 4, 2 * p:2 * p + 2].rearrange("p (e d) -> p e d", d=1)
                                         .to_broadcast([TS, 2, HD]), ALU.mult), (g + ".k", p))

                for p in range(2):
                    keys_out("c", p, wr)
                    full(("c", "S", p))
                    free(v.scalar_tensor_tensor(out=dT[:, 2 * p:2 * p + 2, 0:TP], in0=D0.t[:, :, :], scalar=HD ** -0.5,
                                                in1=dT[:, 2 * p:2 * p + 2, 0:TP], op0=ALU.mult, op1=ALU.mult),
                         ("c", "S", p))
                full(("c", "S4", 0))
                for e in range(2):
                    d_ = dT[0:TS, e:NH:2, TP:TOK]
                    i = v.scalar_tensor_tensor(out=d_, in0=D1.t[0:TS, e, 0:2 * TS].rearrange("p (a n) -> p a n", a=2),
                                               scalar=HD ** -0.5, in1=d_, op0=ALU.mult, op1=ALU.mult)
                    step(i) if e == 0 else free(i, ("c", "S4", 0))

                def states(g, p, w, out_p, out_s, wp, ws):
                    full((g, "dC", p))
                    pair = uses[(g, "dC", p)][0]
                    t_ = pair.t
                    step(v.tensor_copy(cs[:, p, 1, 0:w], t_[:, 0, 0:w]))
                    for t in range(1, NCH):
                        step(v.scalar_tensor_tensor(out=cs[:, p, t + 1, 0:w], in0=cs[:, p, t, 0:w], scalar=wp(t),
                                                    in1=t_[:, 0, t * w:t * w + w], op0=ALU.mult, op1=ALU.add))
                    free(v.scalar_tensor_tensor(out=cs[:, p, 5, 0:w], in0=cs[:, p, 0, 0:w], scalar=ws,
                                                in1=t_[:, 1, 0:w], op0=ALU.mult, op1=ALU.add), (g, "dC", p))
                    wo = min(w, HD + 1)
                    step(v.tensor_copy(out_p, cs[:, p, 4, 0:wo]))
                    step(v.tensor_copy(out_s, cs[:, p, 5, 0:wo]), E(g + ".states"))

                for p in range(2):
                    states("c", p, P, cn_out[:, p, 0, :], cn_out[:, p, 1, :], lambda t: wst[:, p, t:t + 1],
                           wst[:, p, 4:5])
                full("c.nd4")
                free(v.tensor_copy(n4[:], D0.t[:, :, 0:2 * TS].rearrange("p d (a n) -> p d a n", a=2)), "c.nd4")
                for p in range(2):
                    full(("c", "nd", p))
                    t_ = uses[("c", "nd", p)][0].t
                    freed(("c.em", p))
                    e_, q_ = T[p], hf
                    step(v.scalar_tensor_tensor(out=q_[:, 0:TP], in0=t_[:, 1, :], scalar=-1.0, in1=e_[:, 0:TP],
                                                op0=ALU.mult, op1=ALU.max))
                    step(v.tensor_tensor(q_[:, 0:TP], t_[:, 1, :], q_[:, 0:TP], ALU.max))
                    step(v.scalar_tensor_tensor(out=q_[:, TP:TOK], in0=n4[:, 1, p], scalar=-1.0, in1=e_[:, TP:TOK],
                                                op0=ALU.mult, op1=ALU.max))
                    step(v.tensor_tensor(q_[:, TP:TOK], n4[:, 1, p], q_[:, TP:TOK], ALU.max))
                    step(v.reciprocal(q_[:, 0:TOK], q_[:, 0:TOK]))
                    step(v.tensor_tensor(pc[:, p, TP:TOK], n4[:, 0, p], q_[:, TP:TOK], ALU.mult))
                    free(v.tensor_tensor(pc[:, p, 0:TP], t_[:, 0, :], q_[:, 0:TP], ALU.mult), ("c", "nd", p))

                def head_centre(g, p):
                    full((g, "mu", p))
                    pair = uses[(g, "mu", p)][0]
                    free(v.tensor_tensor(pc[:, p].rearrange("p (a n) -> p a n", a=2),
                                         pc[:, p].rearrange("p (a n) -> p a n", a=2), pair.halves(), ALU.subtract),
                         (g, "mu", p))

                def head_scale(g, p):
                    await_ev(g + ".rstd", p + 1)
                    step(v.tensor_tensor(pc[:, p], pc[:, p], T[5][:, 0:TOK], ALU.mult))
                    step(v.tensor_tensor(pc[:, p], pc[:, p], pc[:, 6 + p], ALU.mult), E(g + ".out"))

                freed(("pj", "oc", 1))
                for p in range(2):
                    head_centre("c", p)
                    head_scale("c", p)
                h_lo_of([pc[:, 0], pc[:, 1]])
                add_down(("mix", 1))

                dve.wait_ge(ld["attn"], 64 * (l + 1))
                SC = HD ** -0.5

                def a_rows(n, p, kind, t):
                    b = n % 2
                    full(("a.S", n))
                    if n >= 2:
                        full(("a.T", n - 2))
                    S = D0.t
                    if kind == "t":
                        w = P * (t + 1)
                        near = min(w, 256)
                        hs = slice(2 * p, 2 * p + 2)
                        if w > near:
                            for e in range(2):
                                step(v.tensor_scalar(pr[:, b, e, 0:w - near], S[:, e, 0:w - near], SC,
                                                     far[:, 2 * p + e:2 * p + e + 1], ALU.mult, ALU.add))
                        free(v.scalar_tensor_tensor(out=pr[:, b, :, w - near:w], in0=S[:, :, w - near:w], scalar=SC,
                                                    in1=tb[:, hs, 256 - near:256], op0=ALU.mult, op1=ALU.add),
                             ("a.S", n))
                        step(v.tensor_scalar(pr[0:TS, b, :, w - TS:w], pr[0:TS, b, :, w - TS:w], -1e30, None, ALU.min))
                        step(v.tensor_reduce(mx[:, 2 * b:2 * b + 2], pr[:, b, :, 0:w], AX.X, ALU.max))
                        step(v.tensor_scalar(nmx[:, 2 * b:2 * b + 2], mx[:, 2 * b:2 * b + 2], -1.0, None, ALU.mult),
                             E("a.nmax"))
                    else:
                        h = 2 * p + t
                        r = slice(0, TS)
                        step(v.tensor_scalar(pr[r, b, 0, 0:TP - P], S[r, 0, 0:TP - P], SC, far[r, h:h + 1],
                                             ALU.mult, ALU.add))
                        step(v.scalar_tensor_tensor(out=pr[r, b, 0, TP - P:TP], in0=S[r, 0, TP - P:TP], scalar=SC,
                                                    in1=tb[r, h, 0:P], op0=ALU.mult, op1=ALU.add))
                        free(v.scalar_tensor_tensor(out=pr[r, b, 0, TP:TOK], in0=S[r, 1, 0:TS], scalar=SC,
                                                    in1=tb[r, h, P:P + TS], op0=ALU.mult, op1=ALU.add), ("a.S", n))
                        step(v.tensor_reduce(mx[r, 2 * b:2 * b + 1], pr[r, b, 0, :], AX.X, ALU.max))
                        step(v.tensor_scalar(nmx[r, 2 * b:2 * b + 1], mx[r, 2 * b:2 * b + 1], -1.0, None, ALU.mult),
                             E("a.nmax"))

                def a_probs(n, p, kind, t):
                    b = n % 2
                    await_ev("a.exp", n + 1)
                    m, k, w = (P, 2, P * (t + 1)) if kind == "t" else (TS, 1, TOK)
                    step(v.reciprocal(rc[0:m, 2 * b:2 * b + k], sm[0:m, 2 * b:2 * b + k]))
                    for e in range(k):
                        step(v.tensor_scalar(pr[0:m, b, e, 0:w], pr[0:m, b, e, 0:w], rc[0:m, 2 * b + e:2 * b + e + 1],
                                             None, ALU.mult), E("a.probs") if e == k - 1 else None)

                for n, s_ in enumerate(A_STEPS + [None]):
                    if s_:
                        a_rows(n, *s_)
                    if n:
                        a_probs(n - 1, *A_STEPS[n - 1])
                h_lo_of([pa[:, 0], pa[:, 1]])

                for j in range(4):
                    full(("b.rot", j))
                    pair = uses[("b.rot", j)][0]
                    hv = lambda t: t.rearrange("p (a n) -> p a n", a=2)
                    free(v.tensor_tensor(hv(T[0][:, 0:TOK]), pair.halves(), hv(sinT), ALU.mult), ("b.rot", j))
                    step(v.tensor_tensor(pc[:, j], pc[:, j], cosT, ALU.mult))
                    step(v.tensor_tensor(pc[:, j], pc[:, j], T[0][:, 0:TOK], ALU.add), E("b.turned"))
                add_down(("mix", 2))
                step(v.memset(dT[TS:P, :, TP:TOK], 0.0))
                step(v.memset(vt[TS:P, 4, :], 0.0))
                step(v.tensor_copy(cs[:, :, 0, 0:HD], prm[:, C_SR:C_SR + 128].rearrange("p (a n) -> p a n", a=2)))
                for p in range(2):
                    step(v.tensor_tensor(qw[:, p, 0:TP].rearrange("p (t n) -> p t n", t=4),
                                         pc[:, p, 0:TP].rearrange("p (t n) -> p t n", t=4),
                                         qdec[:, p:p + 1, :].to_broadcast([P, 4, P]), ALU.mult))
                    step(v.tensor_tensor(qw[:, p, TP:TOK], pc[:, p, TP:TOK], qdec[:, p, 0:TS], ALU.mult))
                for p in range(2):
                    keys_out("b", p, kdec)
                for p in range(2):
                    full(("b", "S", p))
                    t_ = uses[("b", "S", p)][0].t
                    for e in range(2):
                        h = 2 * p + e
                        i = v.tensor_tensor(dT[:, h, 0:TP].rearrange("p (t n) -> p t n", t=4),
                                            t_[:, e, :].rearrange("p (t n) -> p t n", t=4),
                                            dec[:, h:h + 1, :].to_broadcast([P, 4, P]), ALU.mult)
                        step(i) if e == 0 else free(i, ("b", "S", p))
                full(("b", "S4", 0))
                for e in range(2):
                    i = v.tensor_tensor(dT[0:TS, e:NH:2, TP:TOK],
                                        D0.t[0:TS, e, 0:2 * TS].rearrange("p (a n) -> p a n", a=2),
                                        dec[0:TS, e:NH:2, 0:TS], ALU.mult)
                    step(i) if e == 0 else free(i, ("b", "S4", 0))
                for p in range(2):
                    states("b", p, HD, st_out[:, p, 0, :], st_out[:, p, 1, :], lambda t: gl[:, p, 0:1], gl[:, p, 1:2])
                freed(("pj", "gb", 1))
                for p in range(2):
                    head_centre("b", p)
                    head_scale("b", p)
                h_lo_of([pc[:, 0], pc[:, 1]])
                def memory_lo():
                    await_ev("mem_hi")
                    step(v.tensor_tensor(mem_lo[:], mem_raw[:], mem_hi[:].bitcast(F32), ALU.subtract), E("mem_split"))

                add_down_norm(1, ("mix", 3), memory_lo)
                step(v.memset(ysc, ALPHA))

                def x_rows(n, p, t):
                    m = P if t < NCH else TS
                    b = n % 2
                    full(("x.S", n))
                    step(v.tensor_reduce(mx[0:m, 2 * b:2 * b + 2], D0.t[0:m, :, 0:NMEM], AX.X, ALU.max))
                    step(v.tensor_scalar(nmx[0:m, 2 * b:2 * b + 2], mx[0:m, 2 * b:2 * b + 2], -SC, None, ALU.mult),
                         E("x.nmax"))

                def x_probs(n, p, t):
                    m = P if t < NCH else TS
                    b = n % 2
                    freed(("x.S", n))
                    step(v.reciprocal(rc[0:m, 2 * b:2 * b + 2], sm[0:m, 2 * b:2 * b + 2]))
                    for e in range(2):
                        step(v.tensor_scalar(prx[0:m, b, e, :], prx[0:m, b, e, :], rc[0:m, 2 * b + e:2 * b + e + 1],
                                             None, ALU.mult), E("x.probs") if e else None)

                for n, s_ in enumerate(X_STEPS):
                    if n >= 2:
                        full(("x.T", n - 2))
                    x_rows(n, *s_)
                    x_probs(n, *s_)
                h_lo_of([qx[:, 0], qx[:, 1]])
                add_down_norm(2, ("cross", 0))
                ffn(1, FT // 2 + 5)
                add_down_norm(3, ("ffn", 1))

        @block.gpsimd
        def _(pool):
            def unit(j, landings, begun, number):
                pool.wait_ge(landed[j], landings)
                if begun is not None:
                    pool.wait_ge(unit_begun, begun)
                    hold(pool, "pool")
                pool.tensor_scalar(w_hi[:, j], w_raw[:, j], 1.0, 0.0, ALU.mult, ALU.add).then_inc(unit_hi, 1)
                pool.wait_ge(unit_hi, number)
                pool.tensor_tensor(w_lo[:, j], w_raw[:, j], w_hi[:, j].bitcast(F32), ALU.subtract)\
                    .then_inc(unit_split, 1)

            for j in range(RING):
                unit(j, 16, None, j + 1)
            with pool.Fori(0, DEPTH * UNITS // RING - 1) as i:
                for j in range(RING):
                    unit(j, 16 * i + 32, RING * i + (RING + j - 1), RING * i + (RING + j + 1))

        @block.sync
        def _(sp):
            for j in range(RING):
                sp.dma_start(w_raw[:, j], io["stream"][j]).then_inc(landed[j], 16)
            with sp.Fori(0, DEPTH * UNITS // RING - 1) as i:
                for j in range(RING):
                    sp.wait_ge(unit_split, RING * i + j + 1)
                    sp.dma_start(w_raw[:, j], io["stream"][RING * i + (RING + j)]).then_inc(landed[j], 16)

        for c in sem_list:
            made[c.name] = c.n
        for pair in (A, B, D0, D1):
            made[pair.full.name] = made[pair.free.name] = pair.n
    return made


def constants():
    f = np.float64
    c = {}
    i = np.arange(P)
    c["ident"] = np.eye(P)
    c["ones"] = np.ones((P, P))
    c["avg"] = np.full((P, P), 1.0 / DM)
    c["blk"] = (i[:, None] // HD == i[None] // HD) / float(HD)
    c["perm"] = (i[:, None] == (i[None] ^ 32)).astype(f)
    c["mask"] = np.where(i[:, None] <= i[None], 0.0, -1e30)
    pos = np.arange(TOK, dtype=f)
    inv = np.exp(-np.log(10000.0) * (i % 32) / 32.0)
    ang = inv[:, None] * pos[None]
    c["cos"] = np.cos(ang)
    c["sin"] = np.sin(ang) * np.where(i % HD < 32, -1.0, 1.0)[:, None]
    lg = np.log1p(-np.exp2(-5.0 - np.arange(NH)))
    diff = (i[None] - i[:, None]).astype(f)
    c["dec"] = np.concatenate([np.where(diff >= 0, np.exp(np.maximum(diff, 0) * lg[h]), 0) * HD ** -0.5
                               for h in range(NH)], 1)
    head = lambda p: 2 * p + i // HD
    c["qdec"] = np.concatenate([np.exp((i[None] + 1.0) * lg[head(p)][:, None]) for p in range(2)], 1)
    kd = np.zeros((P, 5, NH))
    for t in range(5):
        n = P if t < NCH else TS
        kd[:n, t] = np.exp((n - 1.0 - np.arange(n))[:, None] * lg[None]) * HD ** -0.5
    c["kdec"] = kd.reshape(P, -1)
    c["gl"] = np.stack([np.exp(n * lg[head(p)]) for p in range(2) for n in (CH, TS)], 1)
    c["selh"] = np.concatenate([np.repeat((i == h).astype(f)[:, None], P, 1) for h in range(NH)], 1)
    c["selp"] = np.concatenate([(i[:, None] == head(p)[None]).astype(f) for p in range(2)], 1)
    return np.concatenate([c[n] for n, _ in CONST_COLS], 1).astype(np.float32)


def weight_stream(a):
    stream = np.zeros((DEPTH * UNITS, P, 8, P), np.float32)
    first = {g: i * WG for i, g in enumerate(IN_ORDER)}
    n = 0

    def cols(w, c):
        nonlocal n
        stream[n] = w[:, c:c + P].reshape(KT, P, P).transpose(1, 0, 2)
        n += 1

    def rows(w, m):
        nonlocal n
        b = w[2 * m * P:(2 * m + 2) * P].reshape(2, P, KT, P).transpose(1, 2, 0, 3).reshape(P, 2, 8, P)
        stream[n:n + 2] = b.transpose(1, 0, 2, 3)
        n += 2

    def ffn(k, l):
        gate, up, down = (a[f"ffn{k}_{x}"][l] for x in ("gate", "up", "down"))
        for t in range(FT):
            cols(gate, t * P)
            cols(up, t * P)
            if t and t % 2 == 0:
                rows(down, t // 2 - 1)
        rows(down, FT // 2 - 1)

    for l in range(DEPTH):
        ffn(1, l)

        def proj(names):
            for g, j in names:
                cols(a["w_in"][l], first[g] + j * P)

        proj(PROJ_D + PROJ_C)
        rows(a["w_out"][l], 3)
        proj(PROJ_A)
        proj(PROJ_B[0:2])
        rows(a["w_out"][l], 2)
        proj(PROJ_B[2:8])
        rows(a["w_out"][l], 0)
        rows(a["w_out"][l], 1)
        for p in range(2):
            cols(a["x_wk"][l], p * P)
        stream[n:n + 2] = a["x_wv"][l].reshape(2, 4, P, 2, P).transpose(0, 2, 1, 3, 4).reshape(2, P, 8, P)
        n += 2
        for p in range(2):
            cols(a["x_wq"][l], p * P)
        rows(a["x_wo"][l], 0)
        ffn(2, l)
    assert n == DEPTH * UNITS
    return stream


def parameters(a):
    prm = np.zeros((DEPTH, P, NPRM), np.float32)
    tiles = lambda v: v.reshape(-1, P).T
    first = {g: i * WG for i, g in enumerate(IN_ORDER)}
    for l in range(DEPTH):
        q = prm[l]
        for j in range(4):
            q[:, 8 * j:8 * j + 8] = tiles(a["ln_g"][l, j])
            q[:, 32 + 8 * j:40 + 8 * j] = tiles(a["ln_b"][l, j])
        for g, j in PROJ_ALL:
            c = first[g] + j * P
            q[:, BIAS_COL[(g, j)]] = a["b_in"][l, c:c + P]
        for j in range(2):
            c = slice(j * P, j * P + P)
            q[:, C_CONVW + 4 * j:C_CONVW + 4 * j + 4] = a["conv_w"][l, :, c].T
            q[:, C_CBUF + 3 * j:C_CBUF + 3 * j + 3] = a["state_conv"][l, 0, :, c].T
            for at, n in ((C_CONVB, "conv_b"), (C_BA, "lru_ba"), (C_BI, "lru_bi"), (C_LAM, "lru_lambda")):
                q[:, at + j] = a[n][l, c]
            q[:, C_H0 + j] = a["state_lru_h"][l, 0, c]
        q[:NH, C_GI] = a["b_in"][l, 13 * WG:13 * WG + NH]
        q[:NH, C_GF] = a["b_in"][l, 13 * WG + NH:]
        q[:NH, C_M0] = a["state_mlstm_m"][l, 0]
        q[:, C_SC:C_SC + 128] = a["state_mlstm_c"][l, 0].reshape(2, P, HD).transpose(1, 0, 2).reshape(P, 128)
        q[:, C_SN:C_SN + 2] = a["state_mlstm_n"][l, 0].reshape(2, P).T
        q[:, C_SR:C_SR + 128] = a["state_ret"][l, 0].reshape(2, P, HD).transpose(1, 0, 2).reshape(P, 128)
    return prm


def device_inputs(a):
    gates = np.zeros((DEPTH, P, KT, 36), np.float32)
    g = a["w_in"][:, :, 13 * WG:].reshape(DEPTH, KT, P, 2 * NH).transpose(0, 2, 1, 3)
    gates[..., 0:NH], gates[..., 32:36] = g[..., 0:NH], g[..., NH:]
    lru = np.zeros((DEPTH, P, 4, P), np.float32)
    for n, w in enumerate((a["lru_wa"], a["lru_wi"])):
        for b in range(4):
            r = slice((b % 2) * HD, (b % 2) * HD + HD)
            lru[:, r, 2 * n + b // 2, r] = w[:, b]
    rel = a["a_rel_bias"][:, :, ::-1]
    keys = lambda k: k[:, 0].transpose(0, 2, 3, 1).reshape(DEPTH, 2, P, -1).transpose(0, 2, 1, 3)
    vals = lambda v: v[:, 0].reshape(DEPTH, -1, P, WG).transpose(0, 2, 1, 3)
    x = np.concatenate([a["x_prompt"][0], a["x_sample"][0]], 0)
    return {
        "x": x.T.reshape(KT, P, TOK).transpose(1, 0, 2),
        "consts": constants(),
        "stream": weight_stream(a),
        "prm": parameters(a),
        "gates": gates,
        "lru": lru,
        "rel": np.pad(rel, ((0, 0), (0, 0), (P, 0)), mode="edge")[:, :, :BAND],
        "far": rel[:, None, :, 0],
        "kc": keys(a["cache_a_k"]),
        "vc": vals(a["cache_a_v"]),
        "kms": keys(a["cache_mem_k"]),
        "vms": vals(a["cache_mem_v"]),
        "mem": a["mem_prompt"][0].T.reshape(KT, P, NMEM).transpose(1, 0, 2),
    }


OUTS = {
    "out_y": (P, KT, TOK),
    "out_ak": (DEPTH, P, 4, TOK),
    "out_ret": (DEPTH, P, 2, 2, HD),
    "out_mls": (DEPTH, P, 2, 2, HD + 1),
    "out_m": (DEPTH, NH, 2),
    "out_lru": (DEPTH, P, 2, 8),
    "out_mk": (DEPTH, P, 2, NMEM),
    "out_mv": (DEPTH, P, 2, NMEM),
}


def results(o):
    y = o["out_y"].transpose(1, 0, 2).reshape(DM, TOK).T
    heads = lambda z: z.transpose(0, 3, 2, 1).reshape(DEPTH, 1, -1, NH, HD)
    per_head = lambda z: z.transpose(0, 2, 1, 3).reshape(DEPTH, 1, NH, HD, HD)
    ak = o["out_ak"]
    found = [np.ascontiguousarray(y[:TP])[None], np.ascontiguousarray(y[TP:])[None]]
    side = []
    for s, tok in ((0, slice(0, TP)), (1, slice(TP, TOK))):
        c = o["out_mls"][:, :, :, s]
        lru = o["out_lru"]
        side.append([
            heads(ak[:, :, 0:2, tok]), heads(ak[:, :, 2:4, tok]),
            per_head(o["out_ret"][:, :, :, s]), per_head(c[..., 0:HD]),
            c[..., HD].transpose(0, 2, 1).reshape(DEPTH, 1, NH, HD),
            o["out_m"][:, :, s].reshape(DEPTH, 1, NH),
            lru[..., s].transpose(0, 2, 1).reshape(DEPTH, 1, WG),
            lru[..., 2 + 3 * s:5 + 3 * s].transpose(0, 3, 2, 1).reshape(DEPTH, 1, 3, WG),
        ])
    mk = heads(o["out_mk"])
    mv = o["out_mv"].transpose(0, 2, 1, 3).reshape(DEPTH, 1, NMEM, NH, HD)
    return tuple(np.ascontiguousarray(z) for z in found + side[0] + [mk, mv] + side[1])


def new_program(nc, arrays, counts):
    io = {n: nc.dram_tensor("in_" + n, v.shape, F32, kind="ExternalInput").ap() for n, v in arrays.items()}
    io |= {n: nc.dram_tensor(n, shape, F32, kind="ExternalOutput").ap() for n, shape in OUTS.items()}
    return build_program(nc, io, counts)


def kernel(**inputs):
    import concourse.bacc as bacc
    from concourse.bass_utils import run_bass_kernel_spmd as run

    nc = bacc.Bacc("TRN2", target_bir_lowering=False, num_devices=1)
    laid = device_inputs({k: np.asarray(v) for k, v in inputs.items()})
    arrays = {n: np.ascontiguousarray(v) for n, v in laid.items()}
    made = new_program(nc, arrays, COUNTS)
    assert made == COUNTS, made
    r = run(nc, [{"in_" + n: v for n, v in arrays.items()}], core_ids=[0])
    return results(r.results[0])
```

```python
from contextlib import ExitStack

import numpy as np
import concourse.bass as bass
from concourse import mybir

F32 = mybir.dt.float32
F32R = mybir.dt.float32r
ALU = mybir.AluOpType
ACT = mybir.ActivationFunctionType
AX = mybir.AxisListType

P = 128
DM = 1024
DEPTH = 2
TP = 512
TS = 64
TOK = TP + TS
HT = TOK // 2
CH = 128
NCH = TP // CH
KT = DM // P
DFF = 2816
FT = DFF // P
WG = 256
NMEM = 256
HD = 64
NH = 4
BAND = 384
ALPHA = (2.0 * DEPTH) ** 0.25
EPS = 1e-5
RING = 3
LAG = 6
XPW = 3 + TP + 3 + TS
XCW = TP + 3 + TS

PROJ_D = [("xd", 0), ("xd", 1), ("yd", 0), ("yd", 1)]
PROJ_C = [("qc", 0), ("qc", 1), ("kc", 0), ("kc", 1), ("vc", 0), ("vc", 1), ("oc", 0), ("oc", 1)]
PROJ_A = [("qa", 0), ("qa", 1), ("ka", 0), ("ka", 1), ("va", 0), ("va", 1)]
PROJ_B = [("qb", 0), ("qb", 1), ("kb", 0), ("kb", 1), ("vb", 0), ("vb", 1), ("gb", 0), ("gb", 1)]
IN_ORDER = ["qa", "ka", "va", "qb", "kb", "vb", "gb", "qc", "kc", "vc", "oc", "xd", "yd"]
PROJ_ALL = PROJ_D + PROJ_C + PROJ_A + PROJ_B
BIAS_COL = {x: 64 + i for i, x in enumerate(PROJ_ALL)}
C_CONVW, C_CONVB, C_BA, C_BI, C_LAM, C_H0, C_CBUF = 90, 98, 100, 102, 104, 106, 108
C_GI, C_GF, C_M0 = 114, 115, 116
C_SC, C_SN, C_SR = 117, 117 + 128, 117 + 130
NPRM = C_SR + 128

FFN_UNITS = 3 * FT
MIX_UNITS = len(PROJ_ALL) + 8 + 3
X_UNITS = 5
UNITS = 2 * FFN_UNITS + MIX_UNITS + X_UNITS
FFN2_AT = FFN_UNITS + MIX_UNITS + X_UNITS
assert UNITS % 6 == 0 and FFN_UNITS % 6 == 0 and (MIX_UNITS + X_UNITS) % 6 == 0

CONST_COLS = [("ident", P), ("ones", P), ("avg", P), ("blk", P), ("perm", P), ("mask", P), ("cos", TOK), ("sin", TOK),
              ("dec", NH * P), ("qdec", 2 * P), ("kdec", 5 * NH), ("gl", 4), ("selh", NH * P), ("selp", 2 * P)]
A_STEPS = [(p, *x) for p in range(2) for x in [("t", t) for t in range(4)] + [("s", 0), ("s", 1)]]
A_ROWS, A_PROJ = (1, 5), (2, 3, 7, 8, 9, 11)
X_STEPS = [(p, t) for p in range(2) for t in range(NCH + 1)]

COUNTS = {
    "pairA_full": 70, "pairA_free": 70, "pairB_full": 60, "pairB_free": 60, "pairD0_full": 175,
    "pairD0_free": 175, "pairD1_full": 173, "pairD1_free": 173, "x_hi_done": 64, "x_ready": 64,
    "h_hi_done": 54, "h_ready": 54, "sq_done": 64, "s2_added": 48, "var_done": 8, "rstd_done": 8,
    "ln_scaled": 64, "dve_step": 349, "act_step": 74, "stats_ready": 8, "y_summed": 8, "gw_split": 1,
    "conv": 2, "rows": 1, "rowexp": 2, "c.states": 2, "c.sq": 2, "a.probs": 12, "a.pv": 10, "b.turned": 4,
    "b.states": 2, "b.sq": 2, "x.probs": 10, "x.pv": 8, "xp_free": 1, "lam_ln": 1, "lam4": 1, "d.tanh": 2,
    "d.sqrt": 2, "d.out": 2, "rows_in": 1, "lf_ln": 1, "c.dT": 4, "c.rstd": 2, "c.out": 2, "a.nmax": 12,
    "a.exp": 12, "b.rstd": 2, "b.out": 2, "x.nmax": 10, "init": 0, "ysc": 20,
}


class Count:

    def __init__(self, sem, name, counts, pre=0):
        self.sem, self.name, self.pre = sem, name, pre
        self.per = counts.get(name, 1)
        self.n = 0

    def value(self, l, k):
        return l * self.per + (self.pre + k)


def build_program(nc, io, counts):
    made = {}
    with ExitStack() as ctx:
        sem_list = []

        def sem(name):
            return ctx.enter_context(nc.semaphore(name))

        def counted(name, pre=0):
            c = Count(sem(name), name, counts, pre)
            sem_list.append(c)
            return c

        def sb(name, shape, dt=F32, scope=None):
            return (scope or ctx).enter_context(nc.sbuf_tensor(name, shape, dt))

        x_hi = sb("x_hi", [P, KT, TOK], F32R)
        x_lo = sb("x_lo", [P, KT, TOK], F32R)
        y = sb("y", [P, KT, TOK])
        h_hi = sb("h_hi", [P, 2, TOK], F32R)
        h_lo = sb("h_lo", [P, 2, TOK], F32R)
        w_raw = sb("w_raw", [P, RING, 8, P])
        w_hi = sb("w_hi", [P, RING, 8, P], F32R)
        w_lo = sb("w_lo", [P, RING, 8, P], F32R)
        T = [sb(f"scratch{i}", [P, XPW]) for i in range(6)]
        sil = [T[0], T[1]]
        hf = T[2]
        s1, s2, rs = T[3], T[4], T[5]
        mu = T[2]
        prm = sb("prm", [P, NPRM])
        cst = sb("cst", [P, io["consts"].shape[1]])
        gw_raw = sb("gw_raw", [P, KT, 36])
        gw_hi = sb("gw_hi", [P, KT, 36], F32R)
        gw_lo = sb("gw_lo", [P, KT, 36], F32R)
        lru_w = sb("lru_w", [P, 4, P])
        small = sb("small", [P, 64])
        n4 = sb("n4", [P, 2, 2, TS])
        aT = sb("aT", [P, 20])
        wr = sb("wr", [P, 5, NH])
        wst = sb("wst", [P, 2, 5])
        st_out = sb("st_out", [P, 2, 2, HD])
        cn_out = sb("cn_out", [P, 2, 2, HD + 1])
        ld_out = sb("ld_out", [P, 2, 8])
        m_out = sb("m_out", [NH, 2])
        ysc, eps = small[:, 0:1], small[:, 1:2]
        far = small[:, 4:8]
        mx, nmx, sm, rc = small[:, 8:12], small[:, 12:16], small[:, 16:20], small[:, 20:24]
        lam4 = small[:, 24:26]
        lamt = small[:, 26:30]

        with ExitStack() as s:
            pc = sb("pc", [P, 8, TOK], scope=s)
            pa = sb("pa", [P, 6, TOK], scope=s)
            xp = sb("xp", [P, 2, XPW], scope=s)
            yd = sb("yd", [P, 2, TOK], scope=s)
        with ExitStack() as s:
            beside_b = sb("beside_b", [P, 8 * TOK], scope=s)
            mem_hi = sb("mem_hi", [P, KT, NMEM], F32R, scope=s)
            mem_lo = sb("mem_lo", [P, KT, NMEM], F32R, scope=s)
            mkT = sb("mkT", [P, 2, NMEM], scope=s)
            mv = sb("mv", [P, 2, NMEM], scope=s)
        with ExitStack() as s:
            mem_raw = sb("mem_raw", [P, KT, NMEM], scope=s)
        with ExitStack() as s:
            beside_pa = sb("beside_pa", [P, 14 * TOK], scope=s)
            pt = sb("pt", [P, 2, 2, TP], scope=s)
        pad = sb("pad_pj", [P, 16 * TOK + 2 * XPW])
        with ExitStack() as s:
            vt = sb("vt", [P, 5, WG], scope=s)
            kw = sb("kw", [P, 5, WG], scope=s)
            dT = sb("dT", [P, NH, TOK], scope=s)
            cs = sb("cs", [P, 2, 6, P], scope=s)
            qw = sb("qw", [P, 2, TOK], scope=s)
        with ExitStack() as s:
            vta = sb("vta", [P, 5, WG], scope=s)
            tb = sb("tb", [P, NH, 256], scope=s)
            kc = sb("kc", [P, 2, TP], scope=s)
            vc = sb("vc", [P, 4, WG], scope=s)
            pr = sb("pr", [P, 2, 2, TOK], scope=s)
        with ExitStack() as s:
            qx = sb("qx", [P, 2, TOK], scope=s)
            prx = sb("prx", [P, 2, 2, NMEM], scope=s)
            ptx = sb("ptx", [P, 2, 2, NMEM], scope=s)
            kms = sb("kms", [P, 2, NMEM], scope=s)
            vms = sb("vms", [P, 2, NMEM], scope=s)
        pad2 = sb("pad_s", [P, 7552])

        co = {}
        at = 0
        for name, width in CONST_COLS:
            co[name] = cst[:, at:at + width]
            at += width
        ident, ones, avg, blk, perm, mask = (co[n] for n in ("ident", "ones", "avg", "blk", "perm", "mask"))
        cosT, sinT = co["cos"], co["sin"]
        dec = co["dec"].rearrange("p (h m) -> p h m", h=NH)
        qdec = co["qdec"].rearrange("p (a m) -> p a m", a=2)
        kdec = co["kdec"].rearrange("p (t h) -> p t h", t=5)
        gl = co["gl"].rearrange("p (a s) -> p a s", a=2)
        selh = co["selh"].rearrange("p (h m) -> p h m", h=NH)
        selp = co["selp"].rearrange("p (a m) -> p a m", a=2)

        class Pair:
            def __init__(self, name):
                self.name = name
                self.t = ctx.enter_context(nc.psum_tensor(name, [P, 2, 512], F32))
                self.full = counted(name + "_full")
                self.free = counted(name + "_free", 1)
                self.n = 0

            def halves(self):
                return self.t[:, :, 0:HT]

        A, B, D0, D1 = (Pair(n) for n in ("pairA", "pairB", "pairD0", "pairD1"))
        DD = [D0, D1]
        uses = {}

        landed = [sem(f"unit_landed{i}") for i in range(RING)]
        unit_split = sem("unit_split")
        unit_hi = sem("unit_hi")
        unit_begun = sem("unit_begun")
        x_hi_done = counted("x_hi_done", 2 * KT)
        x_ready = counted("x_ready", 2 * KT)
        h_hi_done = counted("h_hi_done")
        h_ready = counted("h_ready")
        sq_done = counted("sq_done")
        s2_added = counted("s2_added")
        var_done = counted("var_done")
        rstd_done = counted("rstd_done")
        ln_scaled = counted("ln_scaled")
        dve_step = counted("dve_step")
        act_step = counted("act_step")
        stats_ready = counted("stats_ready")
        mem_hi_done, mem_split = sem("mem_hi_done"), sem("mem_split")
        ev = {}

        def E(name):
            if name not in ev:
                ev[name] = counted(name)
            return ev[name]

        paced = {n: sem("paced_" + n) for n in ("pe", "act", "dve", "pool")}

        def hold(eng, name):
            eng.sem_inc(paced[name], 1)

        ld = {n: sem("ld_" + n) for n in ("const", "x0", "x1", "prm", "gw", "lru", "attn", "mem", "memc", "ms", "band")}
        stored = {n: sem("st_" + n) for n in ("m", "ak", "ret", "mls", "lru", "mk", "mvv", "y", "mem")}

        tb_dram = nc.dram_tensor("tb_dram", (DEPTH, NH, P * BAND), F32, kind="Internal").ap()
        mem_dram = nc.dram_tensor("mem_dram", (2, P, KT, NMEM), F32, kind="Internal").ap()
        block = ctx.enter_context(nc.Block())

        def inc(ins, c):
            c.n += 1
            ins.then_inc(c.sem, 1)

        @block.tensor
        def _(pe):
            mm = nc.tensor.matmul
            for pair in (A, B, D0, D1):
                pe.sem_inc(pair.free.sem, 1)
            pe.sem_inc(unit_begun, RING)
            with pe.Fori(0, DEPTH) as l:
                def take(pair, label, at=0, index=None):
                    n = pair.n if index is None else index
                    pe.wait_ge(pair.free.sem, pair.free.value(l, n) + at)
                    if index is None:
                        uses[label] = (pair, n)
                        pair.n += 1
                    return pair.t

                def fill(ins, pair):
                    ins.then_inc(pair.full.sem, 1)

                def read_done(label):
                    pair, n = uses[label]
                    pe.wait_ge(pair.free.sem, pair.free.value(l, n + 1))

                def await_ev(name, k=1):
                    pe.wait_ge(E(name).sem, E(name).value(l, k))

                def unit_there(u, off=0):
                    pe.wait_ge(unit_split, l * UNITS + (u + 1) + off)

                def passes(out, s, b, hi, lo, start, stop, m=P, widths=(HT, HT), w=None):
                    wh, wl = w or (w_hi[:, s, b, 0:m], w_lo[:, s, b, 0:m])
                    ins = []
                    for i, (wt, mv_) in enumerate(((wh, hi), (wh, lo), (wl, hi))):
                        c = 0
                        for half, n in enumerate(widths):
                            ins.append(mm(out[0:m, half, 0:n], wt, mv_[:, c:c + n],
                                          start=(start and i == 0), stop=(stop and i == 2)))
                            c += n
                    return ins

                def proj(u, pair, label, off=0, use_off=0, index=None):
                    s = u % RING
                    unit_there(u, off)
                    out = take(pair, label, use_off, index)
                    for k in range(KT):
                        ins = passes(out, s, k, x_hi[:, k], x_lo[:, k], k == 0, k == KT - 1)
                        if k == 0:
                            ins[0].then_inc(unit_begun, 1)
                    ins[-1].then_inc(pair.full.sem, 1)

                def passes_half(out, s, b, hi, lo, h, start, stop):
                    c = slice(h * HT, h * HT + HT)
                    ins = []
                    for i, (wt, mv_) in enumerate(((w_hi, hi), (w_hi, lo), (w_lo, hi))):
                        ins.append(mm(out[:, h, 0:HT], wt[:, s, b], mv_[:, c],
                                      start=(start and i == 0), stop=(stop and i == 2)))
                    return ins

                def proj_first(u, x_stage, labels, second_stats=None, filler=None):
                    three = len(labels) == 3
                    for i in range(2):
                        unit_there(u + i)
                    outs_ = [take(pair, label) for pair, label in zip((A, B, D1), labels)]

                    def block(i, h, k):
                        return passes_half(outs_[i], (u + i) % RING, k, x_hi[:, k], x_lo[:, k], h, k == 0, k == KT - 1)

                    for h in range(2):
                        for k in range(KT):
                            pe.wait_ge(x_ready.sem, l * x_ready.per + KT * (2 * x_stage + h) + k + 1)
                            ia, ib = block(0, h, k), block(1, h, k)
                            if h == 0 and k == 0:
                                ia[0].then_inc(unit_begun, 1)
                            if three and k >= LAG:
                                if h == 0 and k == LAG:
                                    unit_there(u + 2)
                                block(2, h, k - LAG)
                        if h:
                            ib[0].then_inc(unit_begun, 1)
                            fill(ia[-1], A)
                            fill(ib[-1], B)
                        elif second_stats is not None:
                            stats(second_stats, 1)
                        if three:
                            for k in range(KT - LAG, KT):
                                ic = block(2, h, k)
                        if h == 0 and filler:
                            filler()
                    if three:
                        ic[0].then_inc(unit_begun, 1)
                        fill(ic[-1], D1)

                def down_last(u, m, label, j):
                    pe.wait_ge(h_ready.sem, l * h_ready.per + 2 * (m + 1))
                    for h in range(2):
                        for n in range(KT):
                            if (h, n) == (1, 2):
                                stats(j, 0)
                            v = u + n // 4
                            if h == 0 and n % 4 == 0:
                                unit_there(v)
                            pair = DD[n % 2]
                            out = take(pair, (label, h, n))
                            for kk in range(2):
                                ins = passes_half(out, v % RING, 2 * (n % 4) + kk, h_hi[:, kk], h_lo[:, kk], h,
                                                  kk == 0, kk == 1)
                                if kk == 0 and (h, n) in ((0, 0), (1, 4)):
                                    ins[0].then_inc(unit_begun, 1)
                            fill(ins[-1], pair)

                def down(u, m, label=None, off=0, h_off=0, use_off=0, index=None, tiles=range(KT)):
                    if tiles[0] == 0:
                        pe.wait_ge(h_ready.sem, l * h_ready.per + 2 * (m + 1) + h_off)
                    for n in tiles:
                        v = u + n // 4
                        if n % 4 == 0:
                            unit_there(v, off)
                        pair = DD[n % 2]
                        idx = None if index is None else index[n % 2] + n // 2
                        out = take(pair, (label, n), use_off, idx)
                        s = v % RING
                        for kk in range(2):
                            ins = passes(out, s, 2 * (n % 4) + kk, h_hi[:, kk], h_lo[:, kk],
                                         kk == 0, kk == 1)
                            if kk == 0 and n % 4 == 0:
                                ins[0].then_inc(unit_begun, 1)
                        ins[-1].then_inc(pair.full.sem, 1)

                def ffn(f, u0, x_stage, m0, second_stats, j):
                    uses[("ffn", f, "A")], uses[("ffn", f, "B")] = A.n, B.n
                    proj_first(u0, x_stage, [("g", f, 0), ("u", f, 0), ("g", f, 1)], second_stats)
                    proj(u0 + 3, B, ("u", f, 1))
                    a0, b0, d0, d1 = A.n, B.n, D0.n, D1.n
                    uses[("ffn", f, "D0")], uses[("ffn", f, "D1")] = d0, d1
                    with pe.Fori(0, FT // 2 - 1) as i:
                        u, o = u0 + 4, 6 * i
                        proj(u, A, None, o, 2 * i, a0)
                        proj(u + 1, B, None, o, 2 * i, b0)
                        down(u + 2, m0, None, o, 2 * i, 4 * i, (d0, d1))
                        proj(u + 4, A, None, o, 2 * i, a0 + 1)
                        proj(u + 5, B, None, o, 2 * i, b0 + 1)
                    n = FT // 2 - 1
                    for pair, k in ((A, 2), (B, 2), (D0, 4), (D1, 4)):
                        pair.n += k * n
                    down_last(u0 + FFN_UNITS - 2, m0 + n, ("ffn", f), j)

                def stats(j, h):
                    if (j, h) == (0, 0):
                        pe.wait_ge(ld["const"], 16)
                    await_ev("y_summed", 2 * j + h + 1)
                    pe.wait_ge(stats_ready.sem, stats_ready.value(l, 2 * j + h + 1))
                    c = slice(h * HT, h * HT + HT)
                    if h == 0:
                        for pair, src, nm in ((D0, s1, "mean"), (D1, s2, "sq")):
                            out = take(pair, (nm, j, h))
                            fill(mm(out[:, 0, 0:HT], avg, src[:, c], start=True, stop=True), pair)
                    else:
                        out = take(D0, ("mean and sq", j))
                        mm(out[:, 0, 0:HT], avg, s1[:, c], start=True, stop=True)
                        fill(mm(out[:, 1, 0:HT], avg, s2[:, c], start=True, stop=True), D0)

                def wide(pair, label, lhsT, rhs, m=P):
                    out = take(pair, label)
                    mm(out[0:m, 0, 0:TP], lhsT, rhs[:, 0:TP], start=True, stop=True)
                    fill(mm(out[0:m, 1, 0:TS], lhsT, rhs[:, TP:TOK], start=True, stop=True), pair)

                def flat(pair, label, lhsT, rhs, w0=HT, w1=HT):
                    out = take(pair, label)
                    mm(out[:, 0, 0:w0], lhsT, rhs[:, 0:w0], start=True, stop=True)
                    fill(mm(out[:, 1, 0:w1], lhsT, rhs[:, w0:w0 + w1], start=True, stop=True), pair)

                def turn(pair, label, src):
                    out = take(pair, label)
                    for t in range(NCH):
                        nc.tensor.transpose(out[:, 0, t * P:t * P + P], src[:, t * P:t * P + P], ident)
                    fill(nc.tensor.transpose(out[0:TS, 1, 0:P], src[:, TP:TOK], ident), pair)

                def state_sums(pair, label, width):
                    g, p = label[0], label[2]
                    out = take(pair, label)
                    for t in range(NCH + 1):
                        rows = P if t < NCH else TS
                        bank, c = (0, t * width) if t < NCH else (1, 0)
                        for e in range(2):
                            h = 2 * p + e
                            k_ = kw[0:rows, t, h * HD:h * HD + HD]
                            i = mm(out[e * HD:e * HD + HD, bank, c:c + HD], k_,
                                   vt[0:rows, t, h * HD:h * HD + HD], start=True, stop=True)
                            if width == P:
                                i = mm(out[e * HD:e * HD + HD, bank, c + HD:c + P], k_,
                                       ones[0:rows, 0:HD], start=True, stop=True)
                    fill(i, pair)

                def scores(pair, label):
                    p = label[2]
                    out = take(pair, label)
                    for e in range(2):
                        r = slice(e * HD, e * HD + HD)
                        for t in range(NCH):
                            c = slice(t * P, t * P + P)
                            i = mm(out[:, e, c], pc[r, 2 + p, c], pc[r, p, c], start=True, stop=True)
                    fill(i, pair)

                def scores_sample(pair, label):
                    out = take(pair, label)
                    hold(pe, "pe")
                    for e in range(2):
                        r = slice(e * HD, e * HD + HD)
                        for p in range(2):
                            i = mm(out[0:TS, e, p * TS:p * TS + TS], pc[r, 2 + p, TP:TOK], pc[r, p, TP:TOK],
                                   start=True, stop=True)
                    fill(i, pair)

                def out_tile(o, p, e, t, cols, den):
                    h = 2 * p + e
                    r = slice(e * HD, e * HD + HD)
                    tok = slice(t * P, t * P + P) if t < NCH else slice(TP, TOK)
                    st = t if t < NCH else 0
                    lhs = ones[:, 0:HD] if den else vt[:, t, h * HD:h * HD + HD]
                    i = mm(o[r, cols], lhs, dT[:, h, tok], start=True, stop=(t == 0))
                    if t:
                        i = mm(o[r, cols], cs[r, p, st, HD:P] if den else cs[r, p, st, 0:HD], qw[r, p, tok],
                               start=False, stop=True)
                    return i

                ffn(0, 0, 0, 0, None, 0)
                m_down = FT // 2

                u = FFN_UNITS
                proj_first(u, 1, [("pj", "xd", 0), ("pj", "xd", 1), ("pj", "yd", 0)], 0)
                proj(u + 3, B, ("pj", "yd", 1))
                u += 4
                await_ev("gw_split")
                out = take(A, "gates")
                for k in range(KT):
                    ins = passes(out, 0, 0, x_hi[:, k], x_lo[:, k], k == 0, k == KT - 1, m=36,
                                 w=(gw_hi[:, k], gw_lo[:, k]))
                fill(ins[-1], A)

                def lru_gates(j):
                    await_ev("conv", j + 1)
                    flat(D0, ("d.r", j), lru_w[:, j], T[0], 290, XCW - 290)
                    flat(D1, ("d.i", j), lru_w[:, 2 + j], T[0], 290, XCW - 290)

                def proj_list(names, first_pair):
                    nonlocal u
                    for n, (g, j) in enumerate(names):
                        pair = (A, B)[(n + first_pair) % 2]
                        proj(u, pair, ("pj", g, j))
                        u += 1

                pe.wait_ge(ld["lru"], 16 * l + 16)
                proj_list(PROJ_C[0:2], 1)
                lru_gates(0)
                proj_list(PROJ_C[2:5], 1)
                lru_gates(1)
                proj_list(PROJ_C[5:8], 0)

                down(u, m_down, ("mix", 0))
                u += 2
                m_down += 1

                proj_list(PROJ_A[0:1], 0)
                await_ev("rows")
                out = take(D0, "c.aT")
                hold(pe, "pe")
                for t in range(NCH):
                    nc.tensor.transpose(out[:, 0, 4 * t:4 * t + 4], T[0][0:NH, t * P:t * P + P], ident[0:NH, 0:NH])
                fill(nc.tensor.transpose(out[0:TS, 0, 16:20], T[0][0:NH, TP:TOK], ident[0:NH, 0:NH]), D0)
                for h in range(NH):
                    out = take(DD[(h + 1) % 2], ("c.M", h))
                    mm(out[:, 0, 0:TP], selh[0:NH, h], T[4][0:NH, 0:TP], start=True, stop=True)
                    fill(mm(out[0:TS, 1, 0:TS], selh[0:NH, h, 0:TS], T[4][0:NH, TP:TOK], start=True, stop=True),
                         DD[(h + 1) % 2])
                await_ev("rowexp", 2)
                for p in range(2):
                    wide(D1, ("c.w0", p), selp[0:NH, p], T[5][0:NH])
                    read_done(("pj", "vc", p))
                    turn(D0, ("c.v", p), pc[:, 4 + p])
                proj_list(PROJ_A[1:2], 1)
                for p in range(2):
                    turn(D1, ("c.k", p), pc[:, 2 + p])
                    scores(D0, ("c", "S", p))
                scores_sample(D1, ("c", "S4", 0))
                proj_list(PROJ_A[2:3], 2)
                for p in range(2):
                    wide(DD[p], ("c.em", p), selp[0:NH, p], T[3][0:NH])
                read_done(("c.k", 1))
                for p in range(2):
                    state_sums(DD[p], ("c", "dC", p), P)
                proj_list(PROJ_A[3:4], 3)
                await_ev("c.states", 2)
                out = take(D0, "c.nd4")
                for p in range(2):
                    for e in range(2):
                        for den in range(2):
                            i = out_tile(out[:, den], p, e, NCH, slice(p * TS, p * TS + TS), den)
                fill(i, D0)

                def outs(g, p, pair):
                    out = take(pair, (g, "nd", p))
                    for e in range(2):
                        for t in range(NCH):
                            for den in range(2 if g == "c" else 1):
                                i = out_tile(out[:, den], p, e, t, slice(t * P, t * P + P), den)
                        if g == "b":
                            i = out_tile(out[:, 1], p, e, NCH, slice(0, TS), 0)
                    fill(i, pair)

                outs("c", 0, D1)
                proj_list(PROJ_A[4:5], 4)
                outs("c", 1, D0)

                def head_norm(g, p, pair):
                    read_done((g, "nd", p))
                    flat(pair, (g, "mu", p), blk, pc[:, p])

                def head_var(g, p, pair):
                    await_ev(g + ".sq", p + 1)
                    flat(pair, (g, "va", p), blk, T[4])

                head_norm("c", 0, D1)
                proj_list(PROJ_A[5:6], 5)
                head_var("c", 0, D0)
                head_norm("c", 1, D1)
                proj_list(PROJ_B[0:1], 0)
                head_var("c", 1, D0)
                proj_list(PROJ_B[1:2], 1)
                for p in range(2):
                    read_done(("pj", "va", p))
                    turn(DD[p], ("a.v", p), pa[:, 4 + p])
                pe.wait_ge(ld["attn"], 64 * (l + 1))

                def a_scores(n, p, kind, t):
                    out = take(D0, ("a.S", n))
                    if kind == "t":
                        for e in range(2):
                            r = slice(e * HD, e * HD + HD)
                            i = mm(out[:, e, 0:P * (t + 1)], pa[r, p, t * P:t * P + P], pa[r, 2 + p, 0:P * (t + 1)],
                                   start=True, stop=True)
                    else:
                        hold(pe, "pe")
                        r = slice(t * HD, t * HD + HD)
                        mm(out[0:TS, 0, :], pa[r, p, TP:TOK], kc[r, p, :], start=True, stop=True)
                        i = mm(out[0:TS, 1, 0:TS], pa[r, p, TP:TOK], pa[r, 2 + p, TP:TOK], start=True, stop=True)
                    fill(i, D0)

                def a_turn(n, p, kind, t):
                    await_ev("a.probs", n + 1)
                    out = take(D1, ("a.T", n))
                    b = n % 2
                    if kind == "t":
                        for e in range(2):
                            for k in range(t + 1):
                                i = nc.tensor.transpose(out[:, e, k * P:k * P + P], pr[:, b, e, k * P:k * P + P], ident)
                    else:
                        hold(pe, "pe")
                        for k in range(4):
                            nc.tensor.transpose(out[:, 0, k * TS:k * TS + TS], pr[0:TS, b, 0, k * P:k * P + P],
                                                ident[0:TS, 0:TS])
                        i = nc.tensor.transpose(out[0:TS, 0, 256:320], pr[0:TS, b, 0, TP:TOK], ident[0:TS, 0:TS])
                    fill(i, D1)

                def a_values(n, p, kind, t):
                    if n == 0:
                        read_done(("a.v", 0))
                    out = take(B, ("a.o", p)) if (kind, t) == ("t", 0) else B.t
                    read_done(("a.T", n))
                    b = n % 2
                    if kind == "t":
                        for e in range(2):
                            h = 2 * p + e
                            for k in range(t + 1):
                                i = mm(out[e * HD:e * HD + HD, 0, t * P:t * P + P], vta[:, k, h * HD:h * HD + HD],
                                       pt[:, b, e, k * P:k * P + P], start=(k == 0), stop=(k == t))
                    else:
                        h = 2 * p + t
                        o = out[t * HD:t * HD + HD, 1, 0:TS]
                        for k in range(4):
                            mm(o, vc[:, k, h * HD:h * HD + HD], pt[:, b, 0, k * TS:k * TS + TS],
                               start=(k == 0), stop=False)
                        i = mm(o, vta[0:TS, 4, h * HD:h * HD + HD], pt[0:TS, b, 0, 256:320], start=False, stop=True)
                    if (kind, t) == ("s", 1):
                        fill(i, B)
                    else:
                        inc(i, E("a.pv"))

                a_scores(0, *A_STEPS[0])
                for n in range(len(A_STEPS) + 2):
                    if n in A_ROWS:
                        first = 4 * A_ROWS.index(n)
                        down(u - first // 4, m_down, ("mix", 1), tiles=range(first, first + 4))
                        u += 1
                    if n in A_PROJ:
                        proj(u, A, ("pj", *PROJ_B[2 + A_PROJ.index(n)]))
                        u += 1
                    if n + 1 < len(A_STEPS):
                        a_scores(n + 1, *A_STEPS[n + 1])
                    if n >= 2:
                        a_values(n - 2, *A_STEPS[n - 2])
                    if 1 <= n <= len(A_STEPS):
                        a_turn(n - 1, *A_STEPS[n - 1])

                for j in range(4):
                    read_done(("pj", "qk"[j // 2] + "b", j % 2))
                    flat(DD[j % 2], ("b.rot", j), perm, pc[:, j])
                m_down += 1

                def rows_a(first, end):
                    down(u, m_down, ("mix", 2), tiles=range(first, end))

                rows_a(0, 2)
                for p in range(2):
                    read_done(("pj", "vb", p))
                    turn(DD[p], ("b.v", p), pc[:, 4 + p])
                rows_a(2, 4)
                await_ev("b.turned", 4)
                for p in range(2):
                    turn(DD[p], ("b.k", p), pc[:, 2 + p])
                rows_a(4, 5)
                for p in range(2):
                    scores(DD[p], ("b", "S", p))
                scores_sample(D0, ("b", "S4", 0))
                read_done(("b.k", 0))
                for p in range(2):
                    state_sums(DD[(p + 1) % 2], ("b", "dC", p), HD)
                rows_a(5, 6)
                await_ev("b.states", 2)
                for p in range(2):
                    outs("b", p, DD[(p + 1) % 2])
                head_norm("b", 0, D1)
                rows_a(6, 8)
                head_var("b", 0, D0)
                u += 2
                m_down += 1

                def mem_keys(v, p, pair, begun):
                    unit_there(v)
                    out = take(pair, ("x.k", p))
                    for k in range(KT):
                        ins = passes(out, v % RING, k, mem_hi[:, k], mem_lo[:, k], k == 0, k == KT - 1,
                                     widths=(NMEM,))
                        if k == 0 and begun:
                            ins[0].then_inc(unit_begun, begun)
                    fill(ins[-1], pair)

                def mem_values(v, half, out):
                    unit_there(v)
                    s = v % RING
                    for b in range(4):
                        k = 4 * half + b
                        wv = [w_[:, s, 2 * b:2 * b + 2, :].rearrange("p a n -> p (a n)") for w_ in (w_hi, w_lo)]
                        for mt in range(2):
                            mh, ml = (m_[:, k, mt * P:mt * P + P] for m_ in (mem_hi, mem_lo))
                            for i_, (a_, b_) in enumerate(((mh, wv[0]), (mh, wv[1]), (ml, wv[0]))):
                                i = mm(out[:, mt, 0:NMEM], a_, b_, start=(k == 0 and i_ == 0),
                                       stop=(k == KT - 1 and i_ == 2))
                                if b == 0 and mt == 0 and i_ == 0:
                                    i.then_inc(unit_begun, 1)
                    if half:
                        fill(i, A)

                head_norm("b", 1, D0)
                pe.wait_ge(ld["memc"], 32 * (l + 1))
                xv = take(A, "x.v")
                mem_values(u, 0, xv)
                head_var("b", 1, D1)
                mem_values(u + 1, 1, xv)
                mem_keys(u + 2, 0, B, 1)
                u += 3
                down_last(u, m_down, ("mix", 3), 1)
                u += 2
                m_down += 1

                proj_first(u, 2, [("x.q", 0), ("x.q", 1)], 1, lambda: mem_keys(u + 2, 1, D1, 0))
                u += 3

                read_done(("x.q", 0))
                read_done(("x.q", 1))

                def x_scores(n, p, t):
                    out = take(DD[n % 2], ("x.S", n))
                    m = P if t < NCH else TS
                    keys = mkT if t < NCH else kms
                    if t == NCH:
                        pe.wait_ge(ld["ms"], 32 * (l + 1))
                        hold(pe, "pe")
                    for e in range(2):
                        r = slice(e * HD, e * HD + HD)
                        i = mm(out[0:m, e, 0:NMEM], qx[r, p, t * P:t * P + m], keys[r, p, :], start=True, stop=True)
                        if (n, e) == (0, 0):
                            i.then_inc(unit_begun, 1)
                    fill(i, DD[n % 2])

                def x_turn(n, p, t):
                    await_ev("x.probs", n + 1)
                    out = take(A, ("x.T", n))
                    m = P if t < NCH else TS
                    if t == NCH:
                        hold(pe, "pe")
                    for e in range(2):
                        for k in range(2):
                            i = nc.tensor.transpose(out[:, e, k * P:k * P + m], prx[0:m, n % 2, e, k * P:k * P + P],
                                                    ident[0:m, 0:m])
                    fill(i, A)

                def x_values(n, p, t):
                    out = take(B, ("x.o", p)) if t == 0 else B.t
                    read_done(("x.T", n))
                    m = P if t < NCH else TS
                    vals = mv if t < NCH else vms
                    for e in range(2):
                        h = 2 * p + e
                        o = out[e * HD:e * HD + HD, 0, t * P:t * P + P] if t < NCH else out[e * HD:e * HD + HD, 1, 0:TS]
                        for k in range(2):
                            i = mm(o, vals[:, k, h * HD:h * HD + HD], ptx[:, n % 2, e, k * P:k * P + m],
                                   start=(k == 0), stop=(k == 1))
                    if t < NCH:
                        inc(i, E("x.pv"))
                    else:
                        fill(i, B)

                x_scores(0, *X_STEPS[0])
                for n in range(len(X_STEPS) + 2):
                    if n + 1 < len(X_STEPS):
                        x_scores(n + 1, *X_STEPS[n + 1])
                    if n >= 2:
                        x_values(n - 2, *X_STEPS[n - 2])
                    if 1 <= n <= len(X_STEPS):
                        x_turn(n - 1, *X_STEPS[n - 1])
                down_last(u, m_down, ("cross", 0), 2)
                m_down += 1
                u += 2
                assert u == FFN2_AT

                ffn(1, FFN2_AT, 3, m_down, 2, 3)
                stats(3, 1)

        def full_of(eng, l, label):
            pair, n = uses[label]
            eng.wait_ge(pair.full.sem, pair.full.value(l, n + 1))
            return pair

        def gate_use(fi, j):
            return uses[("g", fi, j)] if j < 2 else (A, uses[("ffn", fi, "A")] + j - 1)

        def freed_of(eng, l, label):
            pair, n = uses[label]
            eng.wait_ge(pair.free.sem, pair.free.value(l, n + 1))

        @block.scalar
        def _(act):
            f = nc.scalar.activation
            for h in range(2):
                act.dma_start(y[:, :, h * HT:h * HT + HT], io["x"][:, :, h * HT:h * HT + HT]).then_inc(ld[f"x{h}"], 16)
            for h in range(2):
                act.wait_ge(ld[f"x{h}"], 16)
                for k in range(KT):
                    c = slice(h * HT, h * HT + HT)
                    f(x_hi[:, k, c], y[:, k, c], ACT.Copy).then_inc(x_hi_done.sem, 1)
            act.wait_ge(ld["mem"], 16)
            f(mem_hi[:], mem_raw[:], ACT.Copy).then_inc(mem_hi_done, 1)
            act.wait_ge(mem_split, 1)
            act.dma_start(mem_dram[0], mem_hi[:].bitcast(F32)).then_inc(stored["mem"], 16)
            act.dma_start(mem_dram[1], mem_lo[:].bitcast(F32)).then_inc(stored["mem"], 16)
            for d in range(DEPTH):
                act.dma_start(tb_dram[d].rearrange("h (p j) -> h p j", p=P),
                              bass.AP(io["rel"].tensor, d * NH * BAND, [[BAND, NH], [0, P], [1, BAND]]))\
                    .then_inc(ld["band"], 16)
            with act.Fori(0, DEPTH) as l:
                def step(ins):
                    act_step.n += 1
                    ins.then_inc(act_step.sem, 1)
                    act.wait_ge(act_step.sem, act_step.value(l, act_step.n))

                def free(ins, label):
                    ins.then_inc(uses[label][0].free.sem, 1)

                def full(label):
                    return full_of(act, l, label).t

                def await_ev(name, k=1):
                    act.wait_ge(E(name).sem, E(name).value(l, k))

                act.wait_ge(x_ready.sem, l * x_ready.per + 2 * KT)
                act.dma_start(prm[:], io["prm"][l]).then_inc(ld["prm"], 16)
                act.dma_start(gw_raw[:], io["gates"][l]).then_inc(ld["gw"], 16)
                act.dma_start(lru_w[:], io["lru"][l]).then_inc(ld["lru"], 16)

                def ffn(fi, h0):
                    b0 = uses[("ffn", fi, "B")]
                    nc.scalar.preload_act_table_set("silu_and_others")

                    def tile(j, reuse, au, hu):
                        gate, k = gate_use(fi, j)
                        act.wait_ge(gate.full.sem, gate.full.value(l, k + 1) + au)
                        if reuse:
                            act.wait_ge(B.free.sem, B.free.value(l, b0 + j - 1) + au)
                        f(sil[j % 2][:, 0:TOK].rearrange("p (a n) -> p a n", a=2), gate.halves(), ACT.Silu)\
                            .then_inc(gate.free.sem, 1)
                        act.wait_ge(B.free.sem, B.free.value(l, b0 + j + 1) + au)
                        f(h_hi[:, j % 2], hf[:, 0:TOK], ACT.Copy).then_inc(h_hi_done.sem, 1)
                    for j in range(2):
                        tile(j, False, 0, 0)
                    with act.Fori(0, FT // 2 - 1) as i:
                        for j in range(2):
                            tile(2 + j, True, 2 * i, 0)
                    h_hi_done.n += FT

                def square(j, label, h, n):
                    freed_of(act, l, (label, h, n))
                    if n >= 2:
                        act.wait_ge(s2_added.sem, s2_added.value(l, (KT - 2) * (2 * j + h) + max(1, n - 2)))
                    c = slice(h * HT, h * HT + HT)
                    inc(f(sil[n % 2][:, c], y[:, n, c], ACT.Square), sq_done)

                def rstd(j, h):
                    c = slice(h * HT, h * HT + HT)
                    act.wait_ge(var_done.sem, var_done.value(l, 2 * j + h + 1))
                    step(f(rs[:, c], rs[:, c], ACT.Ln, bias=eps))
                    inc(f(rs[:, c], rs[:, c], ACT.Exp, scale=-0.5), rstd_done)

                def affine(j, h, n):
                    c = slice(h * HT, h * HT + HT)
                    act.wait_ge(ln_scaled.sem, ln_scaled.value(l, KT * (2 * j + h) + n + 1))
                    for dst in (x_hi, y):
                        i = f(dst[:, n, c], y[:, n, c], ACT.Identity, bias=prm[:, 32 + 8 * j + n:33 + 8 * j + n],
                              scale=prm[:, 8 * j + n:8 * j + n + 1])
                    inc(i, x_hi_done)

                def norm(j, label, early=False):
                    nc.scalar.preload_act_table_set("natural_log_exp_and_others")
                    for n in range(KT):
                        square(j, label, 0, n)
                    for n in range(2):
                        square(j, label, 1, n)
                    rstd(j, 0)
                    if early:
                        for n in range(2, KT):
                            square(j, label, 1, n)
                    for n in range(KT):
                        affine(j, 0, n)
                        if not early and 1 <= n < 4:
                            square(j, label, 1, 2 * n)
                            square(j, label, 1, 2 * n + 1)
                    rstd(j, 1)
                    for n in range(KT):
                        affine(j, 1, n)

                def proj_out(g, j, dst, func=ACT.Identity):
                    full(("pj", g, j))
                    pair = uses[("pj", g, j)][0]
                    c = BIAS_COL[(g, j)]
                    free(f(dst.rearrange("p (a n) -> p a n", a=2), pair.halves(), func, bias=prm[:, c:c + 1]),
                         ("pj", g, j))

                def h_hi_of(srcs, k0, name):
                    for j in range(2):
                        await_ev(name, j + 1)
                        inc(f(h_hi[:, j], srcs[j], ACT.Copy), h_hi_done)

                ffn(0, 0)
                act.wait_ge(stored["mem"], 32)
                act.wait_ge(ld["prm"], 16 * l + 16)
                act.wait_ge(ld["const"], 16)
                hold(act, "act")
                norm(0, ("ffn", 0))

                for j in range(2):
                    full(("pj", "xd", j))
                    pair = uses[("pj", "xd", j)][0]
                    c = BIAS_COL[("xd", j)]
                    b = prm[:, c:c + 1]
                    if j == 0 :
                        act.wait_ge(E("xp_free").sem, E("xp_free").value(l, 1))
                    step(f(xp[:, j, 3:3 + HT], pair.t[:, 0, 0:HT], ACT.Identity, bias=b))
                    step(f(xp[:, j, 3 + HT:3 + TP], pair.t[:, 1, 0:TP - HT], ACT.Identity, bias=b))
                    free(f(xp[:, j, 6 + TP:XPW], pair.t[:, 1, TP - HT:HT], ACT.Identity, bias=b), ("pj", "xd", j))
                for j in range(2):
                    proj_out("yd", j, yd[:, j], ACT.Gelu_apprx_tanh)
                nc.scalar.preload_act_table_set("natural_log_exp_and_others")
                lam = prm[:, C_LAM:C_LAM + 2]
                step(f(lamt[:, 0:2], lam, ACT.Abs))
                step(f(lamt[:, 0:2], lamt[:, 0:2], ACT.Exp, scale=-1.0))
                inc(f(lamt[:, 0:2], lamt[:, 0:2], ACT.Ln, bias=ones[:, 0:1]), E("lam_ln"))
                for g, j in PROJ_C[0:2]:
                    proj_out(g, j, pc[:, j])
                for j in range(2):
                    for nm, c, dst in (("d.r", C_BA, T[1]), ("d.i", C_BI, T[2])):
                        full((nm, j))
                        pair = uses[(nm, j)][0]
                        step(f(dst[:, 0:290], pair.t[:, 0, 0:290], ACT.Sigmoid, bias=prm[:, c + j:c + j + 1]))
                        free(f(dst[:, 290:XCW], pair.t[:, 1, 0:XCW - 290], ACT.Sigmoid,
                               bias=prm[:, c + j:c + j + 1]), (nm, j))
                    freed_of(act, l, ("d.r", j))
                    await_ev("lam4")
                    inc(f(T[1][:, 0:XCW], T[1][:, 0:XCW], ACT.Tanh, scale=lam4[:, j:j + 1]), E("d.tanh"))
                    act.wait_ge(E("d.tanh").sem, E("d.tanh").value(l, j + 1))
                    inc(f(T[3][:, 0:XCW], T[1][:, 0:XCW], ACT.Sqrt), E("d.sqrt"))
                    more = PROJ_C[2:5] if j == 0 else PROJ_C[5:8]
                    for g, jj in more:
                        proj_out(g, jj, pc[:, 2 * "qkvo".index(g[0]) + jj],
                                 ACT.Sigmoid if g == "oc" else ACT.Identity)
                h_hi_of([yd[:, 0], yd[:, 1]], 0, "d.out")
                nc.scalar.preload_act_table_set("natural_log_exp_and_others")
                await_ev("rows_in")
                r4 = lambda t: t[0:NH, 0:TOK]
                step(f(r4(T[0]), r4(T[0]), ACT.Identity, bias=prm[0:NH, C_GI:C_GI + 1]))
                step(f(r4(T[1]), r4(T[1]), ACT.Identity, bias=prm[0:NH, C_GF:C_GF + 1]))
                step(f(r4(T[2]), r4(T[1]), ACT.Abs))
                step(f(r4(T[2]), r4(T[2]), ACT.Exp, scale=-1.0))
                inc(f(r4(T[2]), r4(T[2]), ACT.Ln, bias=ones[0:NH, 0:1]), E("lf_ln"))
                proj_out("qa", 0, pa[:, 0])
                await_ev("rows")
                inc(f(r4(T[5]), r4(T[5]), ACT.Exp), E("rowexp"))
                inc(f(r4(T[3]), r4(T[2]), ACT.Exp, scale=-1.0), E("rowexp"))
                act.dma_start(io["out_m"][l], m_out[:]).then_inc(stored["m"], 16)
                freed_of(act, l, "c.aT")
                for h in range(NH):
                    freed_of(act, l, ("c.M", h))
                    for t in range(NCH):
                        step(f(dT[:, h, t * P:t * P + P], dT[:, h, t * P:t * P + P], ACT.Exp,
                               bias=aT[:, 4 * t + h:4 * t + h + 1]))
                    inc(f(dT[0:TS, h, TP:TOK], dT[0:TS, h, TP:TOK], ACT.Exp, bias=aT[0:TS, 16 + h:17 + h]), E("c.dT"))

                def values_out(g, p, dst):
                    full((g + ".v", p))
                    pair = uses[(g + ".v", p)][0]
                    step(f(dst[:, 0:4, p * P:p * P + P], pair.t[:, 0, :].rearrange("p (t n) -> p t n", t=4), ACT.Copy))
                    free(f(dst[0:TS, 4, p * P:p * P + P], pair.t[0:TS, 1, 0:P], ACT.Copy), (g + ".v", p))

                for p in range(2):
                    values_out("c", p, vt)
                proj_out("qa", 1, pa[:, 1])
                proj_out("ka", 0, pa[:, 2])
                for p in range(2):
                    full(("c.em", p))
                    pair = uses[("c.em", p)][0]
                    step(f(T[p][:, 0:TP], pair.t[:, 0, :], ACT.Copy))
                    free(f(T[p][:, TP:TOK], pair.t[:, 1, 0:TS], ACT.Copy), ("c.em", p))
                proj_out("ka", 1, pa[:, 3])
                proj_out("va", 0, pa[:, 4])

                def norm_sq(g, p):
                    freed_of(act, l, (g, "mu", p))
                    inc(f(T[4][:, 0:TOK], pc[:, p], ACT.Square), E(g + ".sq"))

                def norm_rstd(g, p):
                    full((g, "va", p))
                    pair = uses[(g, "va", p)][0]
                    free(f(T[5][:, 0:TOK].rearrange("p (a n) -> p a n", a=2), pair.halves(), ACT.Ln, bias=eps),
                         (g, "va", p))
                    freed_of(act, l, (g, "va", p))
                    inc(f(T[5][:, 0:TOK], T[5][:, 0:TOK], ACT.Exp, scale=-0.5), E(g + ".rstd"))

                freed_of(act, l, ("c", "nd", 1))
                act.wait_ge(ld["band"], 16 * DEPTH)
                act.dma_start(tb[:], tb_dram[l, :, P:].rearrange("h (p j) -> p h j", p=P)[:, :, 0:256])\
                    .then_inc(ld["attn"], 16)
                act.dma_start(kc[:], io["kc"][l]).then_inc(ld["attn"], 16)
                act.dma_start(vc[:], io["vc"][l]).then_inc(ld["attn"], 16)
                act.dma_start(far, io["far"][l].to_broadcast([P, NH])).then_inc(ld["attn"], 16)
                norm_sq("c", 0)
                proj_out("va", 1, pa[:, 5])
                norm_rstd("c", 0)
                norm_sq("c", 1)
                await_ev("c.out", 1)
                inc(f(h_hi[:, 0], pc[:, 0], ACT.Copy), h_hi_done)
                norm_rstd("c", 1)
                await_ev("c.out", 2)
                inc(f(h_hi[:, 1], pc[:, 1], ACT.Copy), h_hi_done)
                act.dma_start(io["out_ak"][l], pa[:, 2:6]).then_inc(stored["ak"], 16)
                act.dma_start(io["out_lru"][l], ld_out[:]).then_inc(stored["lru"], 16)
                act.dma_start(io["out_mls"][l], cn_out[:]).then_inc(stored["mls"], 16)
                act.wait_ge(h_ready.sem, l * h_ready.per + FT + 4)
                proj_out("qb", 0, pc[:, 0])
                proj_out("qb", 1, pc[:, 1])
                for p in range(2):
                    values_out("a", p, vta)

                def a_exp(n, p, kind, t):
                    b = n % 2
                    await_ev("a.nmax", n + 1)
                    if kind == "t":
                        w = P * (t + 1)
                        for e in range(2):
                            i = f(pr[:, b, e, 0:w], pr[:, b, e, 0:w], ACT.Exp, bias=nmx[:, 2 * b + e:2 * b + e + 1],
                                  accum_out=sm[:, 2 * b + e:2 * b + e + 1])
                            step(i) if e == 0 else inc(i, E("a.exp"))
                    else:
                        inc(f(pr[0:TS, b, 0, :], pr[0:TS, b, 0, :], ACT.Exp, bias=nmx[0:TS, 2 * b:2 * b + 1],
                              accum_out=sm[0:TS, 2 * b:2 * b + 1]), E("a.exp"))

                def a_turned(n, p, kind, t):
                    b = n % 2
                    full(("a.T", n))
                    if n >= 2:
                        pv_before(n - 2)
                    if kind == "t":
                        w = P * (t + 1)
                        free(f(pt[:, b, :, 0:w], D1.t[:, :, 0:w], ACT.Copy), ("a.T", n))
                    else:
                        step(f(pt[:, b, 0, 0:256], D1.t[:, 0, 0:256], ACT.Copy))
                        free(f(pt[0:TS, b, 0, 256:320], D1.t[0:TS, 0, 256:320], ACT.Copy), ("a.T", n))

                def pv_before(n):
                    if A_STEPS[n][1:] == ("s", 1):
                        full_of(act, l, ("a.o", A_STEPS[n][0]))
                    else:
                        k = sum(1 for s in A_STEPS[:n + 1] if s[1:] != ("s", 1))
                        await_ev("a.pv", k)

                def a_out(p):
                    full(("a.o", p))
                    step(f(pa[:, p, 0:TP], B.t[:, 0, :], ACT.Copy))
                    free(f(pa[:, p, TP:TOK], B.t[:, 1, 0:TS], ACT.Copy), ("a.o", p))

                nc.scalar.preload_act_table_set("exp_and_others")
                for n, s_ in enumerate(A_STEPS + [None]):
                    if s_:
                        a_exp(n, *s_)
                    if n == 7:
                        a_out(0)
                    if n in A_PROJ:
                        g, j = PROJ_B[2 + A_PROJ.index(n)]
                        proj_out(g, j, pc[:, 2 * "qkvg".index(g[0]) + j], ACT.Silu if g == "gb" else ACT.Identity)
                    if n:
                        a_turned(n - 1, *A_STEPS[n - 1])
                a_out(1)
                for j in range(2):
                    freed_of(act, l, ("a.o", j))
                    inc(f(h_hi[:, j], pa[:, j], ACT.Copy), h_hi_done)
                act.wait_ge(h_ready.sem, l * h_ready.per + FT + 6)
                act.wait_ge(stored["ak"], 16 * l + 16)
                act.dma_start(mem_hi[:].bitcast(F32), mem_dram[0]).then_inc(ld["memc"], 16)
                act.dma_start(mem_lo[:].bitcast(F32), mem_dram[1]).then_inc(ld["memc"], 16)
                nc.scalar.preload_act_table_set("natural_log_exp_and_others")
                for p in range(2):
                    values_out("b", p, vt)
                for p in range(2):
                    full(("b", "nd", p))
                    pair = uses[("b", "nd", p)][0]
                    step(f(pc[:, p, 0:TP], pair.t[:, 0, :], ACT.Copy))
                    free(f(pc[:, p, TP:TOK], pair.t[:, 1, 0:TS], ACT.Copy), ("b", "nd", p))
                for p in range(2):
                    norm_sq("b", p)
                    norm_rstd("b", p)
                    await_ev("b.out", p + 1)
                    inc(f(h_hi[:, p], pc[:, p], ACT.Copy), h_hi_done)

                def mem_keys(p):
                    pair = uses[("x.k", p)][0]
                    full(("x.k", p))
                    free(f(mkT[:, p], pair.t[:, 0, 0:NMEM], ACT.Copy), ("x.k", p))

                full("x.v")
                free(f(mv[:], A.t[:, :, 0:NMEM], ACT.Copy), "x.v")
                mem_keys(0)
                norm(1, ("mix", 3))
                act.dma_start(kms[:], io["kms"][l]).then_inc(ld["ms"], 16)
                act.dma_start(vms[:], io["vms"][l]).then_inc(ld["ms"], 16)
                mem_keys(1)
                act.dma_start(io["out_ret"][l], st_out[:]).then_inc(stored["ret"], 16)
                for p in range(2):
                    full(("x.q", p))
                    free(f(qx[:, p].rearrange("p (a n) -> p a n", a=2), (A, B)[p].halves(), ACT.Copy), ("x.q", p))
                freed_of(act, l, ("x.k", 1))
                act.dma_start(io["out_mk"][l], mkT[:]).then_inc(stored["mk"], 16)
                act.dma_start(io["out_mv"][l], mv[:]).then_inc(stored["mvv"], 16)

                def x_exp(n, p, t):
                    m = P if t < NCH else TS
                    b = n % 2
                    await_ev("x.nmax", n + 1)
                    for e in range(2):
                        i = f(prx[0:m, b, e, :], DD[n % 2].t[0:m, e, 0:NMEM], ACT.Exp, bias=nmx[0:m, 2 * b + e:2 * b + e + 1],
                              scale=HD ** -0.5, accum_out=sm[0:m, 2 * b + e:2 * b + e + 1])
                        if e == 0:
                            step(i)
                        else:
                            free(i, ("x.S", n))

                def x_turned(n, p, t):
                    full(("x.T", n))
                    m = P if t < NCH else TS
                    if n >= 2:
                        pp, tt = X_STEPS[n - 2]
                        if tt < NCH:
                            await_ev("x.pv", sum(1 for s in X_STEPS[:n - 1] if s[1] < NCH))
                        else:
                            full_of(act, l, ("x.o", pp))
                    src = A.t[:, :, 0:NMEM].rearrange("p e (k m) -> p e k m", k=2)[:, :, :, 0:m]
                    dst = ptx[:, n % 2].rearrange("p e (k m) -> p e k m", k=2)[:, :, :, 0:m]
                    free(f(dst, src, ACT.Copy), ("x.T", n))

                def x_out(p):
                    full(("x.o", p))
                    step(f(qx[:, p, 0:TP], B.t[:, 0, :], ACT.Copy))
                    free(f(qx[:, p, TP:TOK], B.t[:, 1, 0:TS], ACT.Copy), ("x.o", p))

                for n, s_ in enumerate(X_STEPS + [None]):
                    if s_:
                        x_exp(n, *s_)
                    if n:
                        x_turned(n - 1, *X_STEPS[n - 1])
                    if n == 6:
                        x_out(0)
                x_out(1)
                for j in range(2):
                    freed_of(act, l, ("x.o", j))
                    inc(f(h_hi[:, j], qx[:, j], ACT.Copy), h_hi_done)
                norm(2, ("cross", 0))
                act.wait_ge(stored["mk"], 16 * l + 16)
                act.wait_ge(stored["mvv"], 16 * l + 16)
                act.wait_ge(stored["mls"], 16 * l + 16)
                act.wait_ge(stored["ret"], 16 * l + 16)
                act.wait_ge(stored["lru"], 16 * l + 16)
                act.wait_ge(stored["m"], 16 * l + 16)
                hold(act, "act")
                ffn(1, 0)
                norm(3, ("ffn", 1), early=True)

        @block.vector
        def _(dve):
            v = nc.vector
            v.memset(small[:, 0:64], 0.0).then_inc(E("init").sem, 1)
            dve.wait_ge(E("init").sem, 1)
            v.memset(eps, EPS).then_inc(E("init").sem, 1)
            dve.wait_ge(E("init").sem, 2)
            for h in range(2):
                for k in range(KT):
                    dve.wait_ge(x_hi_done.sem, KT * h + k + 1)
                    c = slice(h * HT, h * HT + HT)
                    v.tensor_tensor(x_lo[:, k, c], y[:, k, c], x_hi[:, k, c].bitcast(F32), ALU.subtract)\
                        .then_inc(x_ready.sem, 1)
            dve.wait_ge(mem_hi_done, 1)
            v.tensor_tensor(mem_lo[:], mem_raw[:], mem_hi[:].bitcast(F32), ALU.subtract).then_inc(mem_split, 1)
            with dve.Fori(0, DEPTH) as l:
                def step(ins, ev_=None, off=0):
                    c = ev_ or dve_step
                    c.n += 1
                    ins.then_inc(c.sem, 1)
                    dve.wait_ge(c.sem, c.value(l, c.n) + off)

                def free(ins, label):
                    pair, n = uses[label]
                    ins.then_inc(pair.free.sem, 1)
                    dve.wait_ge(pair.free.sem, pair.free.value(l, n + 1))

                def full(label):
                    return full_of(dve, l, label).t

                def freed(label):
                    freed_of(dve, l, label)

                def await_ev(name, k=1):
                    dve.wait_ge(E(name).sem, E(name).value(l, k))

                def ffn(fi, m0):
                    b0, h0 = uses[("ffn", fi, "B")], 2 * m0
                    d0 = (uses[("ffn", fi, "D0")], uses[("ffn", fi, "D1")])
                    step(v.memset(ysc, ALPHA))

                    def hidden(j, off):
                        dve.wait_ge(B.full.sem, B.full.value(l, b0 + j + 1) + off)
                        dve.wait_ge(silu_free(fi, j)[0], silu_free(fi, j)[1] + off)
                        v.scalar_tensor_tensor(out=hf[:, 0:TOK].rearrange("p (a n) -> p a n", a=2),
                                               in0=sil[j % 2][:, 0:TOK].rearrange("p (a n) -> p a n", a=2), scalar=0.5,
                                               in1=B.halves(), op0=ALU.mult, op1=ALU.mult).then_inc(B.free.sem, 1)
                        dve.wait_ge(h_hi_done.sem, l * h_hi_done.per + (h0 + j + 1) + off)
                        v.tensor_tensor(h_lo[:, j % 2], hf[:, 0:TOK], h_hi[:, j % 2].bitcast(F32), ALU.subtract)\
                            .then_inc(h_ready.sem, 1)
                        dve.wait_ge(h_ready.sem, l * h_ready.per + (h0 + j + 1) + off)

                    def silu_free(fi, j):
                        gate, k = gate_use(fi, j)
                        return gate.free.sem, gate.free.value(l, k + 1)

                    for j in range(2):
                        hidden(j, 0)
                    hold(dve, "dve")
                    with dve.Fori(0, FT // 2 - 1) as i:
                        for n in range(KT):
                            pair = DD[n % 2]
                            k = d0[n % 2] + n // 2 + 1
                            dve.wait_ge(pair.full.sem, pair.full.value(l, k) + 4 * i)
                            v.scalar_tensor_tensor(out=y[:, n].rearrange("p (a n) -> p a n", a=2),
                                                   in0=y[:, n].rearrange("p (a n) -> p a n", a=2), scalar=ysc,
                                                   in1=pair.halves(), op0=ALU.mult, op1=ALU.add)\
                                .then_inc(pair.free.sem, 1)
                            if n == KT - 1:
                                for q in range(2):
                                    dve.wait_ge(DD[q].free.sem, DD[q].free.value(l, d0[q] + 4) + 4 * i)
                        v.memset(ysc, 1.0).then_inc(E("ysc").sem, 1)
                        dve.wait_ge(E("ysc").sem, E("ysc").value(l, 1 + (FT // 2 - 1) * fi) + i)
                        for j in range(2):
                            hidden(2 + j, 2 * i)
                    E("ysc").n += FT // 2 - 1
                    h_ready.n += FT

                def add_down(label, tiles=range(KT)):
                    for n in tiles:
                        full((label, n))
                        free(v.scalar_tensor_tensor(out=y[:, n].rearrange("p (a n) -> p a n", a=2),
                                                    in0=y[:, n].rearrange("p (a n) -> p a n", a=2), scalar=ysc,
                                                    in1=DD[n % 2].halves(), op0=ALU.mult, op1=ALU.add), (label, n))

                def add_down_norm(j, label, early=False):
                    half = lambda t, h: t[:, h * HT:h * HT + HT]

                    done = {}

                    def mark(ins, what):
                        inc(ins, dve_step)
                        done[what] = dve_step.n

                    def need(what):
                        dve.wait_ge(dve_step.sem, dve_step.value(l, done[what]))

                    def add(h, n):
                        full((label, h, n))
                        v.scalar_tensor_tensor(out=half(y[:, n], h), in0=half(y[:, n], h), scalar=ysc,
                                               in1=DD[n % 2].t[:, h, 0:HT], op0=ALU.mult, op1=ALU.add)\
                            .then_inc(DD[n % 2].free.sem, 1)

                    def sum_y(h, n):
                        if n:
                            if n == 1:
                                freed((label, h, 0))
                            else:
                                need(("sum", h, n - 1))
                            freed((label, h, n))
                            a = y[:, 0] if n == 1 else s1
                            i = v.tensor_tensor(half(s1, h), half(a, h), half(y[:, n], h), ALU.add)
                            inc(i, E("y_summed")) if n == KT - 1 else mark(i, ("sum", h, n))

                    def variance(h):
                        mean, sq = (("mean", j, 0), ("sq", j, 0)) if h == 0 else (("mean and sq", j),) * 2
                        full(mean)
                        i = v.tensor_copy(half(mu, h), D0.t[:, 0, 0:HT])
                        free(i, mean) if h == 0 else step(i)
                        step(v.tensor_tensor(half(rs, h), half(mu, h), half(mu, h), ALU.mult))
                        if h == 0:
                            full(sq)
                        t_ = D1.t[:, 0, 0:HT] if h == 0 else D0.t[:, 1, 0:HT]
                        free(v.tensor_tensor(half(rs, h), t_, half(rs, h), ALU.subtract), sq)
                        inc(v.tensor_scalar(half(rs, h), half(rs, h), 0.0, None, ALU.max), var_done)

                    def centre(h, n):
                        mark(v.tensor_tensor(half(y[:, n], h), half(y[:, n], h), half(mu, h), ALU.subtract),
                             ("centre", h, n))

                    def scale(h, n):
                        if n == 0:
                            dve.wait_ge(rstd_done.sem, rstd_done.value(l, 2 * j + h + 1))
                        need(("centre", h, n))
                        inc(v.tensor_tensor(half(y[:, n], h), half(y[:, n], h), half(rs, h), ALU.mult), ln_scaled)

                    def lo(h, n):
                        dve.wait_ge(x_hi_done.sem, x_hi_done.value(l, KT * (2 * j + h) + n + 1))
                        inc(v.tensor_tensor(half(x_lo[:, n], h), half(y[:, n], h), half(x_hi[:, n], h).bitcast(F32),
                                            ALU.subtract), x_ready)

                    for n in range(KT):
                        add(0, n)
                        if n:
                            sum_y(0, n - 1)
                    sum_y(0, KT - 1)
                    add(1, 0)
                    add(1, 1)
                    variance(0)
                    if early:
                        for n in range(2, KT):
                            add(1, n)
                            sum_y(1, n - 1)
                        sum_y(1, KT - 1)
                        centre(0, 0)
                        centre(0, 1)
                        scale(0, 0)
                        scale(0, 1)
                        centre(0, 2)
                        lo(0, 0)
                    else:
                        for n, work in ((2, (centre, 0)), (3, (centre, 1)), (4, (scale, 0)), (5, (scale, 1)),
                                        (6, (centre, 2)), (7, (lo, 0))):
                            add(1, n)
                            work[0](0, work[1])
                    for n in range(2, KT):
                        scale(0, n)
                        if n + 1 < KT:
                            centre(0, n + 1)
                        if not early:
                            sum_y(1, n - 1)
                        lo(0, n - 1)
                    lo(0, KT - 1)
                    if not early:
                        sum_y(1, KT - 1)
                    variance(1)
                    centre(1, 0)
                    centre(1, 1)
                    for n in range(KT):
                        scale(1, n)
                        if n + 2 < KT:
                            centre(1, n + 2)
                        if n:
                            lo(1, n - 1)
                    lo(1, KT - 1)
                    dve.wait_ge(x_ready.sem, x_ready.value(l, KT * (2 * j + 2)))

                def h_lo_of(srcs):
                    for j in range(2):
                        dve.wait_ge(h_hi_done.sem, h_hi_done.value(l, h_ready.n + 1))
                        step(v.tensor_tensor(h_lo[:, j], srcs[j], h_hi[:, j].bitcast(F32), ALU.subtract), h_ready)

                ffn(0, 0)
                dve.wait_ge(ld["const"], 16)
                add_down_norm(0, ("ffn", 0))
                step(v.memset(ysc, ALPHA))
                dve.wait_ge(ld["prm"], 16 * l + 16)
                step(v.memset(xp[:, :, 0:3], 0.0))
                step(v.tensor_copy(xp[:, :, 3 + TP:6 + TP], prm[:, C_CBUF:C_CBUF + 6].rearrange("p (a n) -> p a n", a=2)),
                     E("xp_free"))
                dve.wait_ge(ld["gw"], 16 * l + 16)
                step(v.tensor_copy(gw_hi[:], gw_raw[:]))
                step(v.tensor_tensor(gw_lo[:], gw_raw[:], gw_hi[:].bitcast(F32), ALU.subtract), E("gw_split"))

                def conv(j):
                    xc = T[0][:, 0:XCW]
                    w = lambda i: prm[:, C_CONVW + 4 * j + i:C_CONVW + 4 * j + i + 1]
                    freed(("pj", "xd", j))
                    step(v.tensor_scalar(xc, xp[:, j, 0:XCW], w(0), prm[:, C_CONVB + j:C_CONVB + j + 1],
                                         ALU.mult, ALU.add))
                    for i in range(1, 4):
                        step(v.scalar_tensor_tensor(out=xc, in0=xp[:, j, i:i + XCW], scalar=w(i), in1=xc,
                                                    op0=ALU.mult, op1=ALU.add), E("conv") if i == 3 else None)

                conv(0)
                full("gates")
                gi, gf = dT[:, 0], dT[:, 1]
                step(v.tensor_copy(gi[0:NH, :].rearrange("p (a n) -> p a n", a=2), A.t[0:NH, :, 0:HT]))
                free(v.tensor_copy(gf[0:NH, :].rearrange("p (a n) -> p a n", a=2), A.t[32:32 + NH, :, 0:HT]), "gates")
                await_ev("lam_ln")
                step(v.tensor_scalar(lamt[:, 2:4], prm[:, C_LAM:C_LAM + 2], -1.0, 0.0, ALU.mult, ALU.max))
                step(v.tensor_tensor(lamt[:, 2:4], lamt[:, 2:4], lamt[:, 0:2], ALU.add))
                step(v.tensor_scalar(lam4, lamt[:, 2:4], 4.0, None, ALU.mult), E("lam4"))
                for j in range(2):
                    xc, t_, i_, q_, a_ = (T[n][:, 0:XCW] for n in (0, 1, 2, 3, 4))
                    if j == 1:
                        conv(1)
                    freed(("d.i", j))
                    step(v.tensor_tensor(i_, i_, xc, ALU.mult))
                    await_ev("d.tanh", j + 1)
                    r_ = T[5][:, 0:XCW]
                    step(v.tensor_scalar(r_, t_, 1.0, None, ALU.add))
                    step(v.reciprocal(r_, r_))
                    step(v.tensor_tensor(i_, i_, r_, ALU.mult))
                    step(v.tensor_scalar(a_, t_, -1.0, 1.0, ALU.mult, ALU.add))
                    step(v.tensor_tensor(a_, a_, r_, ALU.mult))
                    await_ev("d.sqrt", j + 1)
                    step(v.scalar_tensor_tensor(out=q_, in0=q_, scalar=2.0, in1=i_, op0=ALU.mult, op1=ALU.mult))
                    step(v.tensor_tensor_scan(r_[:, 0:TP], a_[:, 0:TP], q_[:, 0:TP], 0.0, ALU.mult, ALU.add))
                    step(v.tensor_tensor_scan(r_[:, TP + 3:XCW], a_[:, TP + 3:XCW], q_[:, TP + 3:XCW],
                                              prm[:, C_H0 + j:C_H0 + j + 1], ALU.mult, ALU.add))
                    step(v.tensor_copy(ld_out[:, j, 0:1], r_[:, TP - 1:TP]))
                    step(v.tensor_copy(ld_out[:, j, 1:2], r_[:, XCW - 1:XCW]))
                    step(v.tensor_copy(ld_out[:, j, 2:5], xp[:, j, TP:TP + 3]))
                    step(v.tensor_copy(ld_out[:, j, 5:8], xp[:, j, XPW - 3:XPW]))
                    freed(("pj", "yd", j))
                    step(v.tensor_tensor(yd[:, j, 0:TP], yd[:, j, 0:TP], r_[:, 0:TP], ALU.mult))
                    step(v.tensor_tensor(yd[:, j, TP:TOK], yd[:, j, TP:TOK], r_[:, TP + 3:XCW], ALU.mult), E("d.out"))
                h_lo_of([yd[:, 0], yd[:, 1]])

                r4 = lambda t: t[0:NH, 0:TOK]
                step(v.tensor_copy(r4(T[0]), gi[0:NH, :]))
                step(v.tensor_copy(r4(T[1]), gf[0:NH, :]), E("rows_in"))
                add_down(("mix", 0), range(0, 3))
                await_ev("lf_ln")
                step(v.scalar_tensor_tensor(out=r4(T[1]), in0=r4(T[1]), scalar=0.0, in1=r4(T[2]), op0=ALU.min,
                                            op1=ALU.subtract))
                for t in range(NCH + 1):
                    c = slice(t * P, min(t * P + P, TOK))
                    step(v.tensor_tensor_scan(T[3][0:NH, c], ones[0:NH, 0:c.stop - c.start], T[1][0:NH, c], 0.0,
                                              ALU.mult, ALU.add))
                add_down(("mix", 0), range(3, 4))
                step(v.tensor_tensor_scan(T[2][0:NH, 0:TP], T[1][0:NH, 0:TP], T[0][0:NH, 0:TP], 0.0, ALU.add, ALU.max))
                step(v.tensor_tensor_scan(T[2][0:NH, TP:TOK], T[1][0:NH, TP:TOK], T[0][0:NH, TP:TOK],
                                          prm[0:NH, C_M0:C_M0 + 1], ALU.add, ALU.max))
                add_down(("mix", 0), range(4, 5))
                step(v.tensor_tensor(r4(T[0]), r4(T[0]), r4(T[3]), ALU.subtract))
                step(v.tensor_tensor(r4(T[4]), r4(T[3]), r4(T[2]), ALU.subtract))
                step(v.tensor_copy(T[5][0:NH, 0:P], T[4][0:NH, 0:P]))
                for t in range(1, NCH):
                    c = slice(t * P, t * P + P)
                    step(v.tensor_scalar(T[5][0:NH, c], T[4][0:NH, c], T[2][0:NH, t * P - 1:t * P], None, ALU.add))
                step(v.tensor_copy(m_out[:, 0:1], T[2][0:NH, TP - 1:TP]))
                step(v.tensor_copy(m_out[:, 1:2], T[2][0:NH, TOK - 1:TOK]))
                step(v.tensor_scalar(T[5][0:NH, TP:TOK], T[4][0:NH, TP:TOK], prm[0:NH, C_M0:C_M0 + 1], None, ALU.add),
                     E("rows"))
                add_down(("mix", 0), range(5, KT))
                step(v.memset(ysc, 1.0))
                full("c.aT")
                step(v.tensor_copy(aT[:, 0:16], D0.t[:, 0, 0:16]))
                free(v.tensor_copy(aT[0:TS, 16:20], D0.t[0:TS, 0, 16:20]), "c.aT")
                for h in range(NH):
                    full(("c.M", h))
                    t_ = uses[("c.M", h)][0].t
                    step(v.tensor_tensor(dT[:, h, 0:TP].rearrange("p (t n) -> p t n", t=4),
                                         t_[:, 0, :].rearrange("p (t n) -> p t n", t=4),
                                         mask.rearrange("p (a n) -> p a n", a=1).to_broadcast([P, 4, P]), ALU.add))
                    free(v.tensor_tensor(dT[0:TS, h, TP:TOK], t_[0:TS, 1, 0:TS], mask[0:TS, 0:TS], ALU.add),
                         ("c.M", h))
                step(v.memset(dT[TS:P, :, TP:TOK], 0.0))
                step(v.memset(vt[TS:P, 4, :], 0.0))
                step(v.tensor_copy(cs[:, :, 0, 0:HD], prm[:, C_SC:C_SC + 128].rearrange("p (a n) -> p a n", a=2)))
                step(v.tensor_copy(cs[:, :, 0, HD:P],
                                   prm[:, C_SN:C_SN + 2].rearrange("p (a n) -> p a n", n=1).to_broadcast([P, 2, HD])))
                for p in range(2):
                    full(("c.w0", p))
                    t_ = uses[("c.w0", p)][0].t
                    freed(("pj", "qc", p))
                    step(v.tensor_tensor(qw[:, p, 0:TP], pc[:, p, 0:TP], t_[:, 0, :], ALU.mult))
                    step(v.tensor_tensor(qw[:, p, TP:TOK], pc[:, p, TP:TOK], t_[:, 1, 0:TS], ALU.mult))
                    step(v.tensor_copy(wst[:, p, 0:4], t_[:, 0, P - 1:TP:P]))
                    free(v.tensor_copy(wst[:, p, 4:5], t_[:, 1, TS - 1:TS]), ("c.w0", p))
                await_ev("c.dT", 4)
                for h in range(NH):
                    step(v.tensor_scalar(wr[:, 0:4, h], dT[:, h, P - 1:TP:P], HD ** -0.5, None, ALU.mult))
                    step(v.tensor_scalar(wr[0:TS, 4, h:h + 1], dT[0:TS, h, TOK - 1:TOK], HD ** -0.5, None, ALU.mult))

                def keys_out(g, p, w):
                    full((g + ".k", p))
                    t_ = uses[(g + ".k", p)][0].t
                    step(v.tensor_tensor(kw[:, 0:4, p * P:p * P + P].rearrange("p t (e d) -> p t e d", e=2),
                                         t_[:, 0, :].rearrange("p (t e d) -> p t e d", t=4, e=2),
                                         w[:, 0:4, 2 * p:2 * p + 2].rearrange("p t (e d) -> p t e d", d=1)
                                         .to_broadcast([P, 4, 2, HD]), ALU.mult))
                    free(v.tensor_tensor(kw[0:TS, 4, p * P:p * P + P].rearrange("p (e d) -> p e d", e=2),
                                         t_[0:TS, 1, 0:P].rearrange("p (e d) -> p e d", e=2),
                                         w[0:TS, 4, 2 * p:2 * p + 2].rearrange("p (e d) -> p e d", d=1)
                                         .to_broadcast([TS, 2, HD]), ALU.mult), (g + ".k", p))

                for p in range(2):
                    keys_out("c", p, wr)
                    full(("c", "S", p))
                    free(v.scalar_tensor_tensor(out=dT[:, 2 * p:2 * p + 2, 0:TP], in0=D0.t[:, :, :], scalar=HD ** -0.5,
                                                in1=dT[:, 2 * p:2 * p + 2, 0:TP], op0=ALU.mult, op1=ALU.mult),
                         ("c", "S", p))
                full(("c", "S4", 0))
                for e in range(2):
                    d_ = dT[0:TS, e:NH:2, TP:TOK]
                    i = v.scalar_tensor_tensor(out=d_, in0=D1.t[0:TS, e, 0:2 * TS].rearrange("p (a n) -> p a n", a=2),
                                               scalar=HD ** -0.5, in1=d_, op0=ALU.mult, op1=ALU.mult)
                    step(i) if e == 0 else free(i, ("c", "S4", 0))

                def states(g, p, w, out_p, out_s, wp, ws):
                    full((g, "dC", p))
                    pair = uses[(g, "dC", p)][0]
                    t_ = pair.t
                    step(v.tensor_copy(cs[:, p, 1, 0:w], t_[:, 0, 0:w]))
                    for t in range(1, NCH):
                        step(v.scalar_tensor_tensor(out=cs[:, p, t + 1, 0:w], in0=cs[:, p, t, 0:w], scalar=wp(t),
                                                    in1=t_[:, 0, t * w:t * w + w], op0=ALU.mult, op1=ALU.add))
                    free(v.scalar_tensor_tensor(out=cs[:, p, 5, 0:w], in0=cs[:, p, 0, 0:w], scalar=ws,
                                                in1=t_[:, 1, 0:w], op0=ALU.mult, op1=ALU.add), (g, "dC", p))
                    wo = min(w, HD + 1)
                    step(v.tensor_copy(out_p, cs[:, p, 4, 0:wo]))
                    step(v.tensor_copy(out_s, cs[:, p, 5, 0:wo]), E(g + ".states"))

                for p in range(2):
                    states("c", p, P, cn_out[:, p, 0, :], cn_out[:, p, 1, :], lambda t: wst[:, p, t:t + 1],
                           wst[:, p, 4:5])
                full("c.nd4")
                free(v.tensor_copy(n4[:], D0.t[:, :, 0:2 * TS].rearrange("p d (a n) -> p d a n", a=2)), "c.nd4")
                for p in range(2):
                    full(("c", "nd", p))
                    t_ = uses[("c", "nd", p)][0].t
                    freed(("c.em", p))
                    e_, q_ = T[p], hf
                    step(v.scalar_tensor_tensor(out=q_[:, 0:TP], in0=t_[:, 1, :], scalar=-1.0, in1=e_[:, 0:TP],
                                                op0=ALU.mult, op1=ALU.max))
                    step(v.tensor_tensor(q_[:, 0:TP], t_[:, 1, :], q_[:, 0:TP], ALU.max))
                    step(v.scalar_tensor_tensor(out=q_[:, TP:TOK], in0=n4[:, 1, p], scalar=-1.0, in1=e_[:, TP:TOK],
                                                op0=ALU.mult, op1=ALU.max))
                    step(v.tensor_tensor(q_[:, TP:TOK], n4[:, 1, p], q_[:, TP:TOK], ALU.max))
                    step(v.reciprocal(q_[:, 0:TOK], q_[:, 0:TOK]))
                    step(v.tensor_tensor(pc[:, p, TP:TOK], n4[:, 0, p], q_[:, TP:TOK], ALU.mult))
                    free(v.tensor_tensor(pc[:, p, 0:TP], t_[:, 0, :], q_[:, 0:TP], ALU.mult), ("c", "nd", p))

                def head_centre(g, p):
                    full((g, "mu", p))
                    pair = uses[(g, "mu", p)][0]
                    free(v.tensor_tensor(pc[:, p].rearrange("p (a n) -> p a n", a=2),
                                         pc[:, p].rearrange("p (a n) -> p a n", a=2), pair.halves(), ALU.subtract),
                         (g, "mu", p))

                def head_scale(g, p):
                    await_ev(g + ".rstd", p + 1)
                    step(v.tensor_tensor(pc[:, p], pc[:, p], T[5][:, 0:TOK], ALU.mult))
                    step(v.tensor_tensor(pc[:, p], pc[:, p], pc[:, 6 + p], ALU.mult), E(g + ".out"))

                freed(("pj", "oc", 1))
                for p in range(2):
                    head_centre("c", p)
                    head_scale("c", p)
                h_lo_of([pc[:, 0], pc[:, 1]])

                dve.wait_ge(ld["attn"], 64 * (l + 1))
                SC = HD ** -0.5

                def a_rows(n, p, kind, t):
                    b = n % 2
                    full(("a.S", n))
                    if n >= 2:
                        full(("a.T", n - 2))
                    S = D0.t
                    if kind == "t":
                        w = P * (t + 1)
                        near = min(w, 256)
                        hs = slice(2 * p, 2 * p + 2)
                        if w > near:
                            for e in range(2):
                                inc(v.tensor_scalar(pr[:, b, e, 0:w - near], S[:, e, 0:w - near], SC,
                                                     far[:, 2 * p + e:2 * p + e + 1], ALU.mult, ALU.add), dve_step)
                        free(v.scalar_tensor_tensor(out=pr[:, b, :, w - near:w], in0=S[:, :, w - near:w], scalar=SC,
                                                    in1=tb[:, hs, 256 - near:256], op0=ALU.mult, op1=ALU.add),
                             ("a.S", n))
                        step(v.tensor_scalar(pr[0:TS, b, :, w - TS:w], pr[0:TS, b, :, w - TS:w], -1e30, None, ALU.min))
                        step(v.tensor_reduce(mx[:, 2 * b:2 * b + 2], pr[:, b, :, 0:w], AX.X, ALU.max))
                        step(v.tensor_scalar(nmx[:, 2 * b:2 * b + 2], mx[:, 2 * b:2 * b + 2], -1.0, None, ALU.mult),
                             E("a.nmax"))
                    else:
                        h = 2 * p + t
                        r = slice(0, TS)
                        inc(v.tensor_scalar(pr[r, b, 0, 0:TP - P], S[r, 0, 0:TP - P], SC, far[r, h:h + 1],
                                            ALU.mult, ALU.add), dve_step)
                        step(v.scalar_tensor_tensor(out=pr[r, b, 0, TP - P:TP], in0=S[r, 0, TP - P:TP], scalar=SC,
                                                    in1=tb[r, h, 0:P], op0=ALU.mult, op1=ALU.add))
                        free(v.scalar_tensor_tensor(out=pr[r, b, 0, TP:TOK], in0=S[r, 1, 0:TS], scalar=SC,
                                                    in1=tb[r, h, P:P + TS], op0=ALU.mult, op1=ALU.add), ("a.S", n))
                        step(v.tensor_reduce(mx[r, 2 * b:2 * b + 1], pr[r, b, 0, :], AX.X, ALU.max))
                        step(v.tensor_scalar(nmx[r, 2 * b:2 * b + 1], mx[r, 2 * b:2 * b + 1], -1.0, None, ALU.mult),
                             E("a.nmax"))

                def a_probs(n, p, kind, t):
                    b = n % 2
                    await_ev("a.exp", n + 1)
                    m, k, w = (P, 2, P * (t + 1)) if kind == "t" else (TS, 1, TOK)
                    step(v.reciprocal(rc[0:m, 2 * b:2 * b + k], sm[0:m, 2 * b:2 * b + k]))
                    for e in range(k):
                        i = v.tensor_scalar(pr[0:m, b, e, 0:w], pr[0:m, b, e, 0:w], rc[0:m, 2 * b + e:2 * b + e + 1],
                                            None, ALU.mult)
                        inc(i, dve_step) if e < k - 1 else step(i, E("a.probs"))

                for n, s_ in enumerate(A_STEPS + [None]):
                    if n:
                        a_probs(n - 1, *A_STEPS[n - 1])
                    if s_:
                        a_rows(n, *s_)
                    if n in A_ROWS:
                        first = 4 * A_ROWS.index(n)
                        add_down(("mix", 1), range(first, first + 4))
                h_lo_of([pa[:, 0], pa[:, 1]])

                for j in range(4):
                    full(("b.rot", j))
                    pair = uses[("b.rot", j)][0]
                    hv = lambda t: t.rearrange("p (a n) -> p a n", a=2)
                    free(v.tensor_tensor(hv(T[0][:, 0:TOK]), pair.halves(), hv(sinT), ALU.mult), ("b.rot", j))
                    step(v.tensor_tensor(pc[:, j], pc[:, j], cosT, ALU.mult))
                    step(v.tensor_tensor(pc[:, j], pc[:, j], T[0][:, 0:TOK], ALU.add), E("b.turned"))
                add_down(("mix", 2), range(0, 2))
                step(v.memset(dT[TS:P, :, TP:TOK], 0.0))
                step(v.memset(vt[TS:P, 4, :], 0.0))
                step(v.tensor_copy(cs[:, :, 0, 0:HD], prm[:, C_SR:C_SR + 128].rearrange("p (a n) -> p a n", a=2)))
                for p in range(2):
                    step(v.tensor_tensor(qw[:, p, 0:TP].rearrange("p (t n) -> p t n", t=4),
                                         pc[:, p, 0:TP].rearrange("p (t n) -> p t n", t=4),
                                         qdec[:, p:p + 1, :].to_broadcast([P, 4, P]), ALU.mult))
                    step(v.tensor_tensor(qw[:, p, TP:TOK], pc[:, p, TP:TOK], qdec[:, p, 0:TS], ALU.mult))
                add_down(("mix", 2), range(2, 4))
                for p in range(2):
                    keys_out("b", p, kdec)
                add_down(("mix", 2), range(4, 5))
                for p in range(2):
                    full(("b", "S", p))
                    t_ = uses[("b", "S", p)][0].t
                    for e in range(2):
                        h = 2 * p + e
                        i = v.tensor_tensor(dT[:, h, 0:TP].rearrange("p (t n) -> p t n", t=4),
                                            t_[:, e, :].rearrange("p (t n) -> p t n", t=4),
                                            dec[:, h:h + 1, :].to_broadcast([P, 4, P]), ALU.mult)
                        step(i) if e == 0 else free(i, ("b", "S", p))
                full(("b", "S4", 0))
                for e in range(2):
                    i = v.tensor_tensor(dT[0:TS, e:NH:2, TP:TOK],
                                        D0.t[0:TS, e, 0:2 * TS].rearrange("p (a n) -> p a n", a=2),
                                        dec[0:TS, e:NH:2, 0:TS], ALU.mult)
                    step(i) if e == 0 else free(i, ("b", "S4", 0))
                for p in range(2):
                    states("b", p, HD, st_out[:, p, 0, :], st_out[:, p, 1, :], lambda t: gl[:, p, 0:1], gl[:, p, 1:2])
                add_down(("mix", 2), range(5, 6))
                freed(("pj", "gb", 1))
                for p in range(2):
                    head_centre("b", p)
                    if p == 0:
                        add_down(("mix", 2), range(6, 8))
                    head_scale("b", p)
                h_lo_of([pc[:, 0], pc[:, 1]])
                add_down_norm(1, ("mix", 3))
                step(v.memset(ysc, ALPHA))

                def x_rows(n, p, t):
                    m = P if t < NCH else TS
                    b = n % 2
                    full(("x.S", n))
                    step(v.tensor_reduce(mx[0:m, 2 * b:2 * b + 2], DD[n % 2].t[0:m, :, 0:NMEM], AX.X, ALU.max))
                    step(v.tensor_scalar(nmx[0:m, 2 * b:2 * b + 2], mx[0:m, 2 * b:2 * b + 2], -SC, None, ALU.mult),
                         E("x.nmax"))

                def x_probs(n, p, t):
                    m = P if t < NCH else TS
                    b = n % 2
                    freed(("x.S", n))
                    step(v.reciprocal(rc[0:m, 2 * b:2 * b + 2], sm[0:m, 2 * b:2 * b + 2]))
                    for e in range(2):
                        i = v.tensor_scalar(prx[0:m, b, e, :], prx[0:m, b, e, :], rc[0:m, 2 * b + e:2 * b + e + 1],
                                            None, ALU.mult)
                        inc(i, dve_step) if e == 0 else step(i, E("x.probs"))

                for n, s_ in enumerate(X_STEPS + [None]):
                    if s_:
                        if n >= 2:
                            full(("x.T", n - 2))
                        x_rows(n, *s_)
                    if n:
                        x_probs(n - 1, *X_STEPS[n - 1])
                h_lo_of([qx[:, 0], qx[:, 1]])
                add_down_norm(2, ("cross", 0))
                ffn(1, FT // 2 + 5)
                add_down_norm(3, ("ffn", 1), early=True)

        @block.gpsimd
        def _(pool):
            with pool.Fori(0, DEPTH) as l:
                def unit(u, i=None):
                    off = 0 if i is None else RING * i
                    j = u % RING
                    pool.wait_ge(landed[j], l * (16 * UNITS // RING) + 16 * (u // RING + 1)
                                 + (0 if i is None else 16 * i))
                    pool.wait_ge(unit_begun, l * UNITS + (u - 1 + RING) + off)
                    hold(pool, "pool")
                    pool.tensor_scalar(w_hi[:, j], w_raw[:, j], 1.0, 0.0, ALU.mult, ALU.add).then_inc(unit_hi, 1)
                    pool.wait_ge(unit_hi, l * UNITS + (u + 1) + off)
                    pool.tensor_tensor(w_lo[:, j], w_raw[:, j], w_hi[:, j].bitcast(F32), ALU.subtract)\
                        .then_inc(unit_split, 1)

                def units(first, end):
                    assert first % RING == 0 and (end - first) % RING == 0
                    with pool.Fori(0, (end - first) // RING) as i:
                        for j in range(RING):
                            unit(first + j, i)

                def squares_sum(j, h):
                    c = slice(h * HT, h * HT + HT)
                    for n in range(1, KT):
                        pool.wait_ge(sq_done.sem, sq_done.value(l, KT * (2 * j + h) + n + 1))
                        if n > 1:
                            pool.wait_ge(s2_added.sem, s2_added.value(l, s2_added.n))
                        a = sil[0] if n == 1 else s2
                        inc(pool.tensor_tensor(s2[:, c], a[:, c], sil[n % 2][:, c], ALU.add),
                            stats_ready if n == KT - 1 else s2_added)

                def norm_sums(j, u):
                    squares_sum(j, 0)
                    unit(u)
                    unit(u + 1)
                    squares_sum(j, 1)
                    unit(u + 2)

                mix, cross = FFN_UNITS, FFN_UNITS + MIX_UNITS
                units(0, mix)
                norm_sums(0, mix)
                full_end = mix + 3 + (cross - mix - 3) // RING * RING
                units(mix + 3, full_end)
                for u in range(full_end, cross):
                    unit(u)
                norm_sums(1, cross)
                for u in range(cross + 3, FFN2_AT):
                    unit(u)
                norm_sums(2, FFN2_AT)
                units(FFN2_AT + 3, UNITS)
                squares_sum(3, 0)
                squares_sum(3, 1)

        @block.sync
        def _(sp):
            for j in range(RING):
                sp.dma_start(w_raw[:, j], io["stream"][j]).then_inc(landed[j], 16)
            sp.dma_start(mem_raw[:], io["mem"]).then_inc(ld["mem"], 16)
            sp.dma_start(cst[:], io["consts"]).then_inc(ld["const"], 16)
            with sp.Fori(0, DEPTH * UNITS // RING - 1) as i:
                for j in range(RING):
                    sp.wait_ge(unit_split, RING * i + j + 1)
                    sp.dma_start(w_raw[:, j], io["stream"][RING * i + (RING + j)]).then_inc(landed[j], 16)
            for h in range(2):
                sp.wait_ge(x_hi_done.sem, x_hi_done.per * DEPTH + KT * (1 + h))
                c = slice(h * HT, h * HT + HT)
                sp.dma_start(io["out_y"][:, :, c], y[:, :, c]).then_inc(stored["y"], 16)
            sp.wait_ge(stored["y"], 32)

        for c in sem_list:
            made[c.name] = c.n
        for pair in (A, B, D0, D1):
            made[pair.full.name] = made[pair.free.name] = pair.n
    return made


def constants():
    f = np.float64
    c = {}
    i = np.arange(P)
    c["ident"] = np.eye(P)
    c["ones"] = np.ones((P, P))
    c["avg"] = np.full((P, P), 1.0 / DM)
    c["blk"] = (i[:, None] // HD == i[None] // HD) / float(HD)
    c["perm"] = (i[:, None] == (i[None] ^ 32)).astype(f)
    c["mask"] = np.where(i[:, None] <= i[None], 0.0, -1e30)
    pos = np.arange(TOK, dtype=f)
    inv = np.exp(-np.log(10000.0) * (i % 32) / 32.0)
    ang = inv[:, None] * pos[None]
    c["cos"] = np.cos(ang)
    c["sin"] = np.sin(ang) * np.where(i % HD < 32, -1.0, 1.0)[:, None]
    lg = np.log1p(-np.exp2(-5.0 - np.arange(NH)))
    diff = (i[None] - i[:, None]).astype(f)
    c["dec"] = np.concatenate([np.where(diff >= 0, np.exp(np.maximum(diff, 0) * lg[h]), 0) * HD ** -0.5
                               for h in range(NH)], 1)
    head = lambda p: 2 * p + i // HD
    c["qdec"] = np.concatenate([np.exp((i[None] + 1.0) * lg[head(p)][:, None]) for p in range(2)], 1)
    kd = np.zeros((P, 5, NH))
    for t in range(5):
        n = P if t < NCH else TS
        kd[:n, t] = np.exp((n - 1.0 - np.arange(n))[:, None] * lg[None]) * HD ** -0.5
    c["kdec"] = kd.reshape(P, -1)
    c["gl"] = np.stack([np.exp(n * lg[head(p)]) for p in range(2) for n in (CH, TS)], 1)
    c["selh"] = np.concatenate([np.repeat((i == h).astype(f)[:, None], P, 1) for h in range(NH)], 1)
    c["selp"] = np.concatenate([(i[:, None] == head(p)[None]).astype(f) for p in range(2)], 1)
    return np.concatenate([c[n] for n, _ in CONST_COLS], 1).astype(np.float32)


def weight_stream(a):
    stream = np.zeros((DEPTH * UNITS, P, 8, P), np.float32)
    first = {g: i * WG for i, g in enumerate(IN_ORDER)}
    n = 0

    def cols(w, c):
        nonlocal n
        stream[n] = w[:, c:c + P].reshape(KT, P, P).transpose(1, 0, 2)
        n += 1

    def rows(w, m):
        nonlocal n
        b = w[2 * m * P:(2 * m + 2) * P].reshape(2, P, KT, P).transpose(1, 2, 0, 3).reshape(P, 2, 8, P)
        stream[n:n + 2] = b.transpose(1, 0, 2, 3)
        n += 2

    def ffn(k, l):
        gate, up, down = (a[f"ffn{k}_{x}"][l] for x in ("gate", "up", "down"))
        for t in range(FT):
            cols(gate, t * P)
            cols(up, t * P)
            if t and t % 2 == 0:
                rows(down, t // 2 - 1)
        rows(down, FT // 2 - 1)

    for l in range(DEPTH):
        ffn(1, l)

        def proj(names):
            for g, j in names:
                cols(a["w_in"][l], first[g] + j * P)

        proj(PROJ_D + PROJ_C)
        rows(a["w_out"][l], 3)
        proj(PROJ_A)
        proj(PROJ_B[0:2])
        rows(a["w_out"][l], 2)
        at = n - 2
        rows_c = stream[at:n].copy()
        n = at
        for step in range(len(A_STEPS)):
            if step in A_ROWS:
                stream[n] = rows_c[A_ROWS.index(step)]
                n += 1
            if step in A_PROJ:
                proj([PROJ_B[2 + A_PROJ.index(step)]])
        rows(a["w_out"][l], 0)
        stream[n:n + 2] = a["x_wv"][l].reshape(2, 4, P, 2, P).transpose(0, 2, 1, 3, 4).reshape(2, P, 8, P)
        n += 2
        cols(a["x_wk"][l], 0)
        rows(a["w_out"][l], 1)
        for w, c in ((a["x_wq"][l], 0), (a["x_wq"][l], P), (a["x_wk"][l], P)):
            cols(w, c)
        rows(a["x_wo"][l], 0)
        ffn(2, l)
    assert n == DEPTH * UNITS
    return stream


def parameters(a):
    prm = np.zeros((DEPTH, P, NPRM), np.float32)
    tiles = lambda v: v.reshape(-1, P).T
    first = {g: i * WG for i, g in enumerate(IN_ORDER)}
    for l in range(DEPTH):
        q = prm[l]
        for j in range(4):
            q[:, 8 * j:8 * j + 8] = tiles(a["ln_g"][l, j])
            q[:, 32 + 8 * j:40 + 8 * j] = tiles(a["ln_b"][l, j])
        for g, j in PROJ_ALL:
            c = first[g] + j * P
            q[:, BIAS_COL[(g, j)]] = a["b_in"][l, c:c + P]
        for j in range(2):
            c = slice(j * P, j * P + P)
            q[:, C_CONVW + 4 * j:C_CONVW + 4 * j + 4] = a["conv_w"][l, :, c].T
            q[:, C_CBUF + 3 * j:C_CBUF + 3 * j + 3] = a["state_conv"][l, 0, :, c].T
            for at, n in ((C_CONVB, "conv_b"), (C_BA, "lru_ba"), (C_BI, "lru_bi"), (C_LAM, "lru_lambda")):
                q[:, at + j] = a[n][l, c]
            q[:, C_H0 + j] = a["state_lru_h"][l, 0, c]
        q[:NH, C_GI] = a["b_in"][l, 13 * WG:13 * WG + NH]
        q[:NH, C_GF] = a["b_in"][l, 13 * WG + NH:]
        q[:NH, C_M0] = a["state_mlstm_m"][l, 0]
        q[:, C_SC:C_SC + 128] = a["state_mlstm_c"][l, 0].reshape(2, P, HD).transpose(1, 0, 2).reshape(P, 128)
        q[:, C_SN:C_SN + 2] = a["state_mlstm_n"][l, 0].reshape(2, P).T
        q[:, C_SR:C_SR + 128] = a["state_ret"][l, 0].reshape(2, P, HD).transpose(1, 0, 2).reshape(P, 128)
    return prm


def device_inputs(a):
    gates = np.zeros((DEPTH, P, KT, 36), np.float32)
    g = a["w_in"][:, :, 13 * WG:].reshape(DEPTH, KT, P, 2 * NH).transpose(0, 2, 1, 3)
    gates[..., 0:NH], gates[..., 32:36] = g[..., 0:NH], g[..., NH:]
    lru = np.zeros((DEPTH, P, 4, P), np.float32)
    for n, w in enumerate((a["lru_wa"], a["lru_wi"])):
        for b in range(4):
            r = slice((b % 2) * HD, (b % 2) * HD + HD)
            lru[:, r, 2 * n + b // 2, r] = w[:, b]
    rel = a["a_rel_bias"][:, :, ::-1]
    keys = lambda k: k[:, 0].transpose(0, 2, 3, 1).reshape(DEPTH, 2, P, -1).transpose(0, 2, 1, 3)
    vals = lambda v: v[:, 0].reshape(DEPTH, -1, P, WG).transpose(0, 2, 1, 3)
    x = np.concatenate([a["x_prompt"][0], a["x_sample"][0]], 0)
    return {
        "x": x.T.reshape(KT, P, TOK).transpose(1, 0, 2),
        "consts": constants(),
        "stream": weight_stream(a),
        "prm": parameters(a),
        "gates": gates,
        "lru": lru,
        "rel": np.pad(rel, ((0, 0), (0, 0), (P, 0)), mode="edge")[:, :, :BAND],
        "far": rel[:, None, :, 0],
        "kc": keys(a["cache_a_k"]),
        "vc": vals(a["cache_a_v"]),
        "kms": keys(a["cache_mem_k"]),
        "vms": vals(a["cache_mem_v"]),
        "mem": a["mem_prompt"][0].T.reshape(KT, P, NMEM).transpose(1, 0, 2),
    }


OUTS = {
    "out_y": (P, KT, TOK),
    "out_ak": (DEPTH, P, 4, TOK),
    "out_ret": (DEPTH, P, 2, 2, HD),
    "out_mls": (DEPTH, P, 2, 2, HD + 1),
    "out_m": (DEPTH, NH, 2),
    "out_lru": (DEPTH, P, 2, 8),
    "out_mk": (DEPTH, P, 2, NMEM),
    "out_mv": (DEPTH, P, 2, NMEM),
}


def results(o):
    y = o["out_y"].transpose(1, 0, 2).reshape(DM, TOK).T
    heads = lambda z: z.transpose(0, 3, 2, 1).reshape(DEPTH, 1, -1, NH, HD)
    per_head = lambda z: z.transpose(0, 2, 1, 3).reshape(DEPTH, 1, NH, HD, HD)
    ak = o["out_ak"]
    found = [np.ascontiguousarray(y[:TP])[None], np.ascontiguousarray(y[TP:])[None]]
    side = []
    for s, tok in ((0, slice(0, TP)), (1, slice(TP, TOK))):
        c = o["out_mls"][:, :, :, s]
        lru = o["out_lru"]
        side.append([
            heads(ak[:, :, 0:2, tok]), heads(ak[:, :, 2:4, tok]),
            per_head(o["out_ret"][:, :, :, s]), per_head(c[..., 0:HD]),
            c[..., HD].transpose(0, 2, 1).reshape(DEPTH, 1, NH, HD),
            o["out_m"][:, :, s].reshape(DEPTH, 1, NH),
            lru[..., s].transpose(0, 2, 1).reshape(DEPTH, 1, WG),
            lru[..., 2 + 3 * s:5 + 3 * s].transpose(0, 3, 2, 1).reshape(DEPTH, 1, 3, WG),
        ])
    mk = heads(o["out_mk"])
    mv = o["out_mv"].transpose(0, 2, 1, 3).reshape(DEPTH, 1, NMEM, NH, HD)
    return tuple(np.ascontiguousarray(z) for z in found + side[0] + [mk, mv] + side[1])


def new_program(nc, arrays, counts):
    io = {n: nc.dram_tensor("in_" + n, v.shape, F32, kind="ExternalInput").ap() for n, v in arrays.items()}
    io |= {n: nc.dram_tensor(n, shape, F32, kind="ExternalOutput").ap() for n, shape in OUTS.items()}
    return build_program(nc, io, counts)


def kernel(**inputs):
    import concourse.bacc as bacc
    from concourse.bass_utils import run_bass_kernel_spmd as run

    nc = bacc.Bacc("TRN2", target_bir_lowering=False, num_devices=1)
    laid = device_inputs({k: np.asarray(v) for k, v in inputs.items()})
    arrays = {n: np.ascontiguousarray(v) for n, v in laid.items()}
    made = new_program(nc, arrays, COUNTS)
    assert made == COUNTS, made
    r = run(nc, [{"in_" + n: v for n, v in arrays.items()}], core_ids=[0])
    return results(r.results[0])
```
